# Optimizing a Trainium2 kernel written in Bass

```python
import math
import jax, jax.numpy as jnp
from jax import lax
import numpy as np

D_MODEL = 1024
BATCH = 1
SEQ = 1024
DEPTH = 1

PLE_DIM = 256
W_CONV = D_MODEL
CONV_GROUPS = 8
CONV_K = 31
HG_HEAD_DIM = 128
W_HGRN = D_MODEL
HG_HEADS = W_HGRN // HG_HEAD_DIM
W_MIX = W_CONV + W_HGRN
CHUNK = 64
EPS = 1e-6
W_IN_COLS = 3 * W_CONV + 4 * W_HGRN


def rms_norm(x, g):
    xf = x.astype(jnp.float32)
    y = xf * lax.rsqrt(jnp.mean(xf * xf, axis=-1, keepdims=True) + EPS)
    return (y * g.astype(jnp.float32)).astype(x.dtype)

def group_layer_norm(x, g, b, n_groups):
    shp = x.shape
    xf = x.astype(jnp.float32).reshape(shp[:-1] + (n_groups, shp[-1] // n_groups))
    mu = jnp.mean(xf, axis=-1, keepdims=True)
    var = jnp.mean(jnp.square(xf - mu), axis=-1, keepdims=True)
    y = ((xf - mu) * lax.rsqrt(var + EPS)).reshape(shp)
    return (y * g.astype(jnp.float32) + b.astype(jnp.float32)).astype(x.dtype)

def conformer_conv_branch(z_val, z_glu, z_gate, conv_w, conv_b, cn_g, cn_b, w_pw2, b_pw2):
    v = z_val * jax.nn.sigmoid(z_glu)
    y = lax.conv_general_dilated(
        v, conv_w[:, None, :].astype(v.dtype),
        window_strides=(1,), padding=[(CONV_K - 1, 0)],
        dimension_numbers=("NWC", "WIO", "NWC"),
        feature_group_count=W_CONV) + conv_b.astype(v.dtype)
    y = jax.nn.silu(group_layer_norm(y, cn_g, cn_b, CONV_GROUPS))
    y = y @ w_pw2.astype(y.dtype) + b_pw2.astype(y.dtype)
    return y * jax.nn.silu(z_gate)

def _gla_chunk_step(S, inp):
    q, k, v, lf = inp
    b = jnp.cumsum(lf, axis=2)
    o_inter = jnp.einsum("bhck,bhkv->bhcv", q * jnp.exp(b), S)
    t_idx = jnp.arange(CHUNK)
    causal = (t_idx[:, None] >= t_idx[None, :])[None, None, :, :, None]
    diff = b[:, :, :, None, :] - b[:, :, None, :, :]
    decay = jnp.exp(jnp.where(causal, diff, -jnp.inf))
    A = jnp.einsum("bhtsk,bhsk->bhts", q[:, :, :, None, :] * decay, k)
    o_intra = jnp.einsum("bhts,bhsv->bhtv", A, v)
    b_last = b[:, :, -1, :]
    k_dec = k * jnp.exp(b_last[:, :, None, :] - b)
    S_new = jnp.exp(b_last)[..., None] * S + jnp.einsum("bhsk,bhsv->bhkv", k_dec, v)
    return S_new, o_inter + o_intra

def hgrn2_branch(zq, zf, zi, zg, lb, onorm_g):
    B, T, _ = zq.shape
    n_chunks = T // CHUNK
    lbf = lb.astype(jnp.float32)
    zf32 = zf.astype(jnp.float32)
    f = lbf + (1.0 - lbf) * jax.nn.sigmoid(zf32)
    log_f = jnp.log(f)
    k = (1.0 - lbf) * jax.nn.sigmoid(-zf32)
    q = jax.nn.silu(zq.astype(jnp.float32))
    v = zi.astype(jnp.float32)

    def to_chunks(t):
        return t.reshape(B, n_chunks, CHUNK, HG_HEADS, HG_HEAD_DIM).transpose(1, 0, 3, 2, 4)

    S0 = jnp.zeros((B, HG_HEADS, HG_HEAD_DIM, HG_HEAD_DIM), jnp.float32)
    _, o = lax.scan(_gla_chunk_step, S0,
                    (to_chunks(q), to_chunks(k), to_chunks(v), to_chunks(log_f)))
    o = o.transpose(1, 0, 3, 2, 4).reshape(B, T, HG_HEADS, HG_HEAD_DIM)
    o = rms_norm(o, onorm_g.reshape(HG_HEADS, HG_HEAD_DIM))
    o = o.reshape(B, T, W_HGRN).astype(zq.dtype)
    return o * jax.nn.silu(zg)

def first_inputs(seed: int = 0) -> dict:
    key = jax.random.key(seed)
    ks = jax.random.split(key, 20)
    f32 = jnp.float32
    nrm = lambda k, s, sc: (jax.random.normal(k, s, f32) * sc).astype(f32)
    return {
        "x": jax.random.normal(ks[0], (BATCH, SEQ, D_MODEL), f32),
        "p": jax.random.normal(ks[1], (DEPTH, BATCH, SEQ, PLE_DIM), f32),
        "ln_g": 1.0 + nrm(ks[2], (DEPTH, D_MODEL), 0.02),
        "w_in": nrm(ks[3], (DEPTH, D_MODEL, W_IN_COLS), D_MODEL ** -0.5),
        "conv_w": nrm(ks[4], (DEPTH, CONV_K, W_CONV), CONV_K ** -0.5),
        "conv_b": nrm(ks[5], (DEPTH, W_CONV), 0.01),
        "cnorm_g": 1.0 + nrm(ks[6], (DEPTH, W_CONV), 0.02),
        "cnorm_b": nrm(ks[7], (DEPTH, W_CONV), 0.01),
        "w_pw2": nrm(ks[8], (DEPTH, W_CONV, W_CONV), W_CONV ** -0.5),
        "b_pw2": nrm(ks[9], (DEPTH, W_CONV), 0.01),
        "lb_logits": nrm(ks[10], (DEPTH + 1, W_HGRN), 0.1),
        "onorm_g": 1.0 + nrm(ks[11], (DEPTH, W_HGRN), 0.02),
        "w_out": nrm(ks[12], (DEPTH, W_MIX, D_MODEL), W_MIX ** -0.5),
        "pe_norm_g": 1.0 + nrm(ks[13], (DEPTH, D_MODEL), 0.02),
        "w_pg": nrm(ks[14], (DEPTH, D_MODEL, D_MODEL), D_MODEL ** -0.5),
        "w_pp": nrm(ks[15], (DEPTH, PLE_DIM, D_MODEL), PLE_DIM ** -0.5),
        "final_g": 1.0 + nrm(ks[16], (D_MODEL,), 0.02),
    }

def first_block(x, p, ln_g, w_in, conv_w, conv_b, cnorm_g, cnorm_b, w_pw2, b_pw2,
              lb_logits, onorm_g, w_out, pe_norm_g, w_pg, w_pp, final_g):
    lbs = jnp.cumsum(jax.nn.softmax(lb_logits.astype(jnp.float32), axis=0), axis=0)
    h = x
    split_pts = [W_CONV, 2 * W_CONV, 3 * W_CONV,
                 3 * W_CONV + W_HGRN, 3 * W_CONV + 2 * W_HGRN, 3 * W_CONV + 3 * W_HGRN]
    for i in range(DEPTH):
        u = rms_norm(h, ln_g[i])
        z = u @ w_in[i].astype(u.dtype)
        c_val, c_glu, c_gate, hq, hf, hi, hg = jnp.split(z, split_pts, axis=-1)
        y_conv = conformer_conv_branch(c_val, c_glu, c_gate, conv_w[i], conv_b[i],
                                       cnorm_g[i], cnorm_b[i], w_pw2[i], b_pw2[i])
        y_hgrn = hgrn2_branch(hq, hf, hi, hg, lbs[i], onorm_g[i])
        y = jnp.concatenate([y_conv, y_hgrn.astype(y_conv.dtype)], axis=-1)
        h = h + y @ w_out[i].astype(y.dtype)
        pe = p[i] @ w_pp[i].astype(p.dtype)
        gate = jax.nn.sigmoid(rms_norm(h, pe_norm_g[i]) @ w_pg[i].astype(h.dtype))
        h = h + gate * pe.astype(h.dtype)
    return rms_norm(h, final_g)


_first_inputs = first_inputs


def first_inputs(seed=0):
    import zlib

    import numpy as np

    out = dict(_first_inputs(seed))
    spreads = {}
    factors = {'ln_g': 4.682,
     'conv_b': 27.575,
     'cnorm_g': 147.001,
     'cnorm_b': 200.0,
     'b_pw2': 200.0,
     'lb_logits': 8.0,
     'onorm_g': 109.316,
     'pe_norm_g': 200.0,
     'final_g': 23.508,
     'w_pg': 22.904,
     'p': 7.119,
     'w_pp': 7.141}
    for name, (base, spread) in spreads.items():
        noise = np.random.default_rng([zlib.crc32(name.encode()), seed]).standard_normal(out[name].shape)
        drawn = base * np.exp(spread * noise) if base else spread * noise
        out[name] = __import__('jax').numpy.asarray(drawn.astype(out[name].dtype))
    for name, factor in factors.items():
        out[name] = (out[name] * factor).astype(out[name].dtype)
    return out


_narrow_inputs = first_inputs


def first_inputs(seed=0):

    out = dict(_narrow_inputs(seed))
    wider = {'cnorm_g': 3.85,
     'cnorm_b': 5.66,
     'b_pw2': 4.14,
     'onorm_g': 3.86,
     'pe_norm_g': 6.46,
     'final_g': 3.22}
    for name, times in wider.items():
        mean = out[name].mean()
        out[name] = (mean + times * (out[name] - mean)).astype(out[name].dtype)
    return out


Q_BLOCK = 128
MAX_STREAM_OFFSET = 4096

D_RNN = D_MODEL
LRU_BLOCK_W = 256
LRU_BLOCKS = D_RNN // LRU_BLOCK_W
CONV_W = 4
LRU_C = 8.0

MLA_HEADS = 16
V_HEAD = D_MODEL // MLA_HEADS
QK_NOPE = 64
QK_ROPE = 32
QK_HEAD = QK_NOPE + QK_ROPE
Q_LORA = 768
KV_LORA = 256
ROPE_THETA = 10000.0

N_BRANCH = 2
IN_SPLITS = (D_RNN, D_RNN, Q_LORA, KV_LORA, QK_ROPE, N_BRANCH * D_MODEL)
D_IN = sum(IN_SPLITS)

N_GROUPS = 4
EXPERTS_PER_GROUP = 8
N_EXPERTS = N_GROUPS * EXPERTS_PER_GROUP
TOP_K = 2
D_EXPERT = 256
MOE_BLOCK = 128


def rms_norm_2(x, g):
    xf = x.astype(jnp.float32)
    y = xf * lax.rsqrt(jnp.mean(xf * xf, axis=-1, keepdims=True) + EPS)
    return (y * g.astype(jnp.float32)).astype(x.dtype)

def causal_conv(x, w, b):
    y = lax.conv_general_dilated(
        x, w[:, None, :].astype(x.dtype), window_strides=(1,),
        padding=[(CONV_W - 1, 0)], dimension_numbers=('NWC', 'WIO', 'NWC'),
        feature_group_count=x.shape[-1])
    return y + b.astype(x.dtype)

def rg_lru(x, wa, ba, wx, bx, lam):
    B, S, _ = x.shape
    xb = x.reshape(B, S, LRU_BLOCKS, LRU_BLOCK_W)
    r = jax.nn.sigmoid((jnp.einsum('bshi,hij->bshj', xb, wa).reshape(B, S, D_RNN) + ba).astype(jnp.float32))
    i = jax.nn.sigmoid((jnp.einsum('bshi,hij->bshj', xb, wx).reshape(B, S, D_RNN) + bx).astype(jnp.float32))
    log_a = -LRU_C * r * jax.nn.softplus(-lam.astype(jnp.float32))
    a = jnp.exp(log_a)
    mult = jnp.sqrt(-jnp.expm1(2.0 * log_a))
    b = mult * (i * x.astype(jnp.float32))

    def combine(left, right):
        a_l, b_l = left
        a_r, b_r = right
        return a_l * a_r, a_r * b_l + b_r

    _, h = lax.associative_scan(combine, (a, b), axis=1)
    return h.astype(x.dtype)

def rope(x, pos):
    half = QK_ROPE // 2
    freq = ROPE_THETA ** (-jnp.arange(half, dtype=jnp.float32) / half)
    ang = pos.astype(jnp.float32)[:, :, None, None] * freq
    cos, sin = jnp.cos(ang), jnp.sin(ang)
    x1 = x[..., :half].astype(jnp.float32)
    x2 = x[..., half:].astype(jnp.float32)
    return jnp.concatenate([x1 * cos - x2 * sin, x1 * sin + x2 * cos], axis=-1).astype(x.dtype)

def chunk_causal_attention(q, k, v):
    B, S, H, _ = q.shape
    scale = QK_HEAD ** -0.5
    outs = []
    for blk in range(S // Q_BLOCK):
        q0 = blk * Q_BLOCK
        k_end = q0 + Q_BLOCK
        qb = q[:, q0:k_end]
        s = jnp.einsum('bqhd,bkhd->bhqk', qb, k[:, :k_end]).astype(jnp.float32) * scale
        q_chunk = (q0 + jnp.arange(Q_BLOCK)) // CHUNK
        k_chunk = jnp.arange(k_end) // CHUNK
        mask = k_chunk[None, :] <= q_chunk[:, None]
        s = jnp.where(mask, s, -jnp.inf)
        p = jax.nn.softmax(s, axis=-1).astype(v.dtype)
        outs.append(jnp.einsum('bhqk,bkhd->bqhd', p, v[:, :k_end]))
    return jnp.concatenate(outs, axis=1).reshape(B, S, H * V_HEAD)

def mla(q_c, kv_c, k_pe, pos, q_a_g, w_uq, kv_a_g, w_ukv, q_norm_g, k_norm_g):
    B, S, _ = q_c.shape
    q = (rms_norm_2(q_c, q_a_g) @ w_uq).reshape(B, S, MLA_HEADS, QK_HEAD)
    kv = (rms_norm_2(kv_c, kv_a_g) @ w_ukv).reshape(B, S, MLA_HEADS, QK_NOPE + V_HEAD)
    k_nope, v = kv[..., :QK_NOPE], kv[..., QK_NOPE:]
    k_pe_h = jnp.broadcast_to(k_pe[:, :, None, :], (B, S, MLA_HEADS, QK_ROPE))
    k = jnp.concatenate([k_nope, k_pe_h], axis=-1)
    q = rms_norm_2(q, q_norm_g)
    k = rms_norm_2(k, k_norm_g)
    q = jnp.concatenate([q[..., :QK_NOPE], rope(q[..., QK_NOPE:], pos)], axis=-1)
    k = jnp.concatenate([k[..., :QK_NOPE], rope(k[..., QK_NOPE:], pos)], axis=-1)
    return chunk_causal_attention(q, k, v)

def hier_moe(x, wg, bg, we, be, w_gate, w_up, w_down):
    B, S, D = x.shape
    T = B * S
    xt = x.reshape(T, D)
    xf = xt.astype(jnp.float32)
    g_logits = xf @ wg.astype(jnp.float32) + bg.astype(jnp.float32)
    g_prob = jax.nn.softmax(g_logits, axis=-1)
    grp = jnp.argmax(g_logits, axis=-1)
    p_grp = jnp.take_along_axis(g_prob, grp[:, None], axis=1)
    e_logits = (xf @ we.astype(jnp.float32) + be.astype(jnp.float32)).reshape(T, N_GROUPS, EXPERTS_PER_GROUP)
    e_in = jnp.take_along_axis(e_logits, grp[:, None, None], axis=1)[:, 0]
    top_v, top_i = lax.top_k(e_in, TOP_K)
    combine = p_grp * jax.nn.softmax(top_v, axis=-1)
    expert = grp[:, None] * EXPERTS_PER_GROUP + top_i

    A = T * TOP_K
    e_flat = expert.reshape(A)
    tok_flat = jnp.arange(A, dtype=jnp.int32) // TOP_K
    c_flat = combine.reshape(A)
    order = jnp.argsort(e_flat)
    e_sorted = e_flat[order]
    counts = jnp.bincount(e_flat, length=N_EXPERTS)
    padded = (counts + MOE_BLOCK - 1) // MOE_BLOCK * MOE_BLOCK
    starts = jnp.cumsum(counts) - counts
    p_ends = jnp.cumsum(padded)
    p_starts = p_ends - padded
    dest = p_starts[e_sorted] + (jnp.arange(A) - starts[e_sorted])
    P = A + N_EXPERTS * MOE_BLOCK
    n_blk = P // MOE_BLOCK
    tok_pad = jnp.full((P,), T, jnp.int32).at[dest].set(tok_flat[order])
    c_pad = jnp.zeros((P,), jnp.float32).at[dest].set(c_flat[order])
    blk_expert = jnp.clip(jnp.searchsorted(p_ends, jnp.arange(n_blk) * MOE_BLOCK, side='right'), 0, N_EXPERTS - 1)
    x_pad = jnp.concatenate([xt, jnp.zeros((1, D), xt.dtype)], axis=0)[tok_pad].reshape(n_blk, MOE_BLOCK, D)

    def expert_block(args):
        xb, e = args
        hb = jax.nn.silu(xb @ w_gate[e]) * (xb @ w_up[e])
        return hb @ w_down[e]

    y = lax.map(expert_block, (x_pad, blk_expert)).reshape(P, D).astype(jnp.float32) * c_pad[:, None]
    out = jax.ops.segment_sum(y, tok_pad, num_segments=T + 1)[:T]
    return out.astype(x.dtype).reshape(B, S, D)

def second_inputs(seed: int = 0) -> dict:
    key = jax.random.key(seed)
    ks = jax.random.split(key, 28)
    L = DEPTH

    def nrm(k, shape, s):
        return jax.random.normal(k, shape, jnp.float32) * s

    def gain(k, n):
        return 1.0 + 0.05 * jax.random.normal(k, (L, n), jnp.float32)

    x = jax.random.normal(ks[0], (BATCH, SEQ, D_MODEL), jnp.float32)
    offset = jax.random.randint(ks[1], (BATCH, 1), 0, MAX_STREAM_OFFSET, dtype=jnp.int32)
    positions = offset + jnp.arange(SEQ, dtype=jnp.int32)[None, :]
    a0 = jax.random.uniform(ks[2], (L, D_RNN), jnp.float32, 0.9, 0.999)
    s0 = a0 ** (1.0 / LRU_C)
    lru_lambda = jnp.log(s0) - jnp.log1p(-s0)
    return {
        "x": x,
        "positions": positions,
        "norm_mix_g": gain(ks[3], D_MODEL),
        "w_in": nrm(ks[4], (L, D_MODEL, D_IN), D_MODEL ** -0.5),
        "conv_w": nrm(ks[5], (L, CONV_W, D_RNN), CONV_W ** -0.5),
        "conv_b": nrm(ks[6], (L, D_RNN), 0.02),
        "lru_wa": nrm(ks[7], (L, LRU_BLOCKS, LRU_BLOCK_W, LRU_BLOCK_W), LRU_BLOCK_W ** -0.5),
        "lru_ba": nrm(ks[8], (L, D_RNN), 0.02),
        "lru_wx": nrm(ks[9], (L, LRU_BLOCKS, LRU_BLOCK_W, LRU_BLOCK_W), LRU_BLOCK_W ** -0.5),
        "lru_bx": nrm(ks[10], (L, D_RNN), 0.02),
        "lru_lambda": lru_lambda,
        "q_a_g": gain(ks[11], Q_LORA),
        "w_uq": nrm(ks[12], (L, Q_LORA, MLA_HEADS * QK_HEAD), Q_LORA ** -0.5),
        "kv_a_g": gain(ks[13], KV_LORA),
        "w_ukv": nrm(ks[14], (L, KV_LORA, MLA_HEADS * (QK_NOPE + V_HEAD)), KV_LORA ** -0.5),
        "q_norm_g": gain(ks[15], QK_HEAD),
        "k_norm_g": gain(ks[16], QK_HEAD),
        "w_out": nrm(ks[17], (L, D_MODEL, D_MODEL), D_MODEL ** -0.5),
        "norm_ffn_g": gain(ks[18], D_MODEL),
        "router_group_w": nrm(ks[19], (L, D_MODEL, N_GROUPS), D_MODEL ** -0.5),
        "router_group_b": nrm(ks[20], (L, N_GROUPS), 0.01),
        "router_expert_w": nrm(ks[21], (L, D_MODEL, N_EXPERTS), D_MODEL ** -0.5),
        "router_expert_b": nrm(ks[22], (L, N_EXPERTS), 0.01),
        "w_gate": nrm(ks[23], (L, N_EXPERTS, D_MODEL, D_EXPERT), D_MODEL ** -0.5),
        "w_up": nrm(ks[24], (L, N_EXPERTS, D_MODEL, D_EXPERT), D_MODEL ** -0.5),
        "w_down": nrm(ks[25], (L, N_EXPERTS, D_EXPERT, D_MODEL), D_EXPERT ** -0.5),
    }

def second_block(x, positions, norm_mix_g, w_in, conv_w, conv_b, lru_wa, lru_ba, lru_wx, lru_bx,
              lru_lambda, q_a_g, w_uq, kv_a_g, w_ukv, q_norm_g, k_norm_g, w_out, norm_ffn_g,
              router_group_w, router_group_b, router_expert_w, router_expert_b,
              w_gate, w_up, w_down):
    B, S, _ = x.shape
    split_points = np.cumsum(IN_SPLITS)[:-1].tolist()
    h = x
    for l in range(DEPTH):
        u = rms_norm_2(h, norm_mix_g[l])
        proj = u @ w_in[l]
        x_rnn, g_rnn, q_c, kv_c, k_pe, gate_logits = jnp.split(proj, split_points, axis=-1)
        xa = causal_conv(x_rnn, conv_w[l], conv_b[l])
        ya = rg_lru(xa, lru_wa[l], lru_ba[l], lru_wx[l], lru_bx[l], lru_lambda[l]) * jax.nn.gelu(g_rnn)
        yb = mla(q_c, kv_c, k_pe, positions, q_a_g[l], w_uq[l], kv_a_g[l], w_ukv[l], q_norm_g[l], k_norm_g[l])
        gates = jax.nn.sigmoid(gate_logits.astype(jnp.float32)).reshape(B, S, N_BRANCH, D_MODEL)
        merged = gates[:, :, 0] * ya.astype(jnp.float32) + gates[:, :, 1] * yb.astype(jnp.float32)
        h = h + merged.astype(h.dtype) @ w_out[l]
        h = h + hier_moe(rms_norm_2(h, norm_ffn_g[l]), router_group_w[l], router_group_b[l],
                         router_expert_w[l], router_expert_b[l], w_gate[l], w_up[l], w_down[l])
    return h


def setup_inputs(seed=0):
    out = dict(first_inputs(seed))
    for name, value in second_inputs(seed + 1).items():
        if name != "x":
            out[name + "_2"] = value
    return out


def reference(
    x, p, ln_g, w_in, conv_w, conv_b, cnorm_g, cnorm_b, w_pw2, b_pw2, lb_logits, onorm_g, w_out,
    pe_norm_g, w_pg, w_pp, final_g, positions_2, norm_mix_g_2, w_in_2, conv_w_2, conv_b_2,
    lru_wa_2, lru_ba_2, lru_wx_2, lru_bx_2, lru_lambda_2, q_a_g_2, w_uq_2, kv_a_g_2, w_ukv_2,
    q_norm_g_2, k_norm_g_2, w_out_2, norm_ffn_g_2, router_group_w_2, router_group_b_2,
    router_expert_w_2, router_expert_b_2, w_gate_2, w_up_2, w_down_2,
):
    x = first_block(
        x, p, ln_g, w_in, conv_w, conv_b, cnorm_g, cnorm_b, w_pw2, b_pw2, lb_logits, onorm_g,
        w_out, pe_norm_g, w_pg, w_pp, final_g,
    )
    return second_block(
        x, positions_2, norm_mix_g_2, w_in_2, conv_w_2, conv_b_2, lru_wa_2, lru_ba_2, lru_wx_2,
        lru_bx_2, lru_lambda_2, q_a_g_2, w_uq_2, kv_a_g_2, w_ukv_2, q_norm_g_2, k_norm_g_2,
        w_out_2, norm_ffn_g_2, router_group_w_2, router_group_b_2, router_expert_w_2,
        router_expert_b_2, w_gate_2, w_up_2, w_down_2,
    )


_drawn_inputs = setup_inputs


def setup_inputs(seed=0):
    import zlib

    import numpy as np

    out = dict(_drawn_inputs(seed))
    spreads = {}
    factors = {'norm_mix_g_2': 8.0,
     'w_in_2': 2.791,
     'conv_w_2': 22.648,
     'conv_b_2': 64.0,
     'lru_wa_2': 64.0,
     'lru_ba_2': 64.0,
     'lru_wx_2': 64.0,
     'lru_bx_2': 64.0,
     'lru_lambda_2': 64.0,
     'q_a_g_2': 8.0,
     'w_uq_2': 8.0,
     'kv_a_g_2': 8.0,
     'w_ukv_2': 8.0,
     'q_norm_g_2': 8.0,
     'k_norm_g_2': 8.0,
     'w_out_2': 2.752,
     'norm_ffn_g_2': 8.0,
     'router_group_w_2': 6.4,
     'router_group_b_2': 64.0,
     'router_expert_w_2': 6.262,
     'router_expert_b_2': 55.729,
     'w_gate_2': 5.892,
     'w_up_2': 5.533,
     'w_down_2': 5.532}
    for name, (base, spread) in spreads.items():
        noise = np.random.default_rng([zlib.crc32(name.encode()), seed]).standard_normal(out[name].shape)
        drawn = base * np.exp(spread * noise) if base else spread * noise
        out[name] = __import__('jax').numpy.asarray(drawn.astype(out[name].dtype))
    for name, factor in factors.items():
        out[name] = (out[name] * factor).astype(out[name].dtype)
    return out
```

```python
from contextlib import ExitStack

import numpy as np

import concourse.bass as bass
from concourse import mybir
from concourse.bass import ds

ALU = mybir.AluOpType
ACT = mybir.ActivationFunctionType
AX = mybir.AxisListType
F32 = mybir.dt.float32
I32 = mybir.dt.int32
U8 = mybir.dt.uint8

P = 128
T = 1024
D = 1024
NT = T // P
ND = D // P
HALF = 512
CONV_K = 31
LEVELS = 7
EPS = 1e-6
ROUND = 1.5 * 2.0 ** 23
TWO_PI = (6.28125, 0.0019350051879882812, float(2 * np.pi - 6.28125 - 0.0019350051879882812))

ROWS = {"conv_w": 0, "ln_g": 31, "conv_b": 32, "cnorm_g": 33, "cnorm_b": 34, "b_pw2": 35,
        "lb0": 36, "lb1": 37, "onorm_g": 38, "pe_norm_g": 39, "norm_mix_g": 40, "conv_w_2": 41,
        "conv_b_2": 45, "lru_ba": 46, "lru_bx": 47, "lru_lambda": 48, "q_a_g": 49, "kv_a_g": 50}
NROWS = 51


def shape_constants():
    ident = np.eye(P, dtype=np.float32)
    mean = np.full((P, P), 1.0 / P, np.float32)
    before = np.triu(np.ones((P, P), np.float32), 1)
    restart = np.ones((P, T), np.float32)
    restart[:, ::P] = 0.0
    masks = np.zeros((P, LEVELS + 1, P), np.float32)
    s, t = np.meshgrid(np.arange(P), np.arange(P), indexing="ij")
    for level in range(LEVELS):
        size = 1 << level
        masks[:, level] = (s // (2 * size) == t // (2 * size)) & (s // size % 2 == 0) & (t // size % 2 == 1)
    masks[:, LEVELS] = s == t
    half = 16
    freq = (np.float32(10000.0) ** (-np.arange(half, dtype=np.float32) / np.float32(half))).astype(np.float32)
    return {
        "c_square": np.stack([ident, mean, before], axis=1),
        "c_restart": restart,
        "c_masks": masks,
        "c_freq": np.broadcast_to(freq, (P, half)).copy(),
        "c_expert": np.broadcast_to(np.arange(32, dtype=np.float32), (P, 32)).copy(),
        "c_block": np.broadcast_to(np.arange(48, dtype=np.float32) * 128, (P, 48)).copy(),
        "c_token": (np.arange(P)[:, None] + P * np.arange(NT)[None, :]).astype(np.int32),
    }


def build(nc, a, out, dump=None, upto=99):
    ctx = ExitStack()
    with ctx:
        ctx.enter_context(nc.allow_non_contiguous_dma(reason="parameter vectors and small tables"))

        def sb(name, shape, dt=F32):
            return ctx.enter_context(nc.sbuf_tensor(name, shape, dt))

        in_use = []

        def sem(name):
            in_use.append(nc.alloc_semaphore(name))
            return in_use[-1]

        def retire(*kept):
            done = [s for s in in_use if not any(s is k for k in kept)]
            in_use[:] = list(kept)
            nc.clear_and_free_semaphores(done)
            nc.all_engine_barrier()

        PS = ctx.enter_context(nc.psum_tensor("PS", [P, 8, HALF], F32))
        RA = sb("RA", [P, ND, T])
        RB = sb("RB", [P, ND, T])
        RC = sb("RC", [P, ND, T])
        square = sb("square", [P, 3, P])
        ident, mean, before = square[:, 0, :], square[:, 1, :], square[:, 2, :]
        cols = sb("cols", [P, ND, NROWS])
        small = sb("small", [P, 320])
        ARENA = 25 * T
        arena = sb("arena", [P, ARENA])

        def part(at, shape, dt=F32):
            n = int(np.prod(shape))
            v = arena[:, at:at + n]
            if len(shape) == 2:
                v = v.rearrange("p (x y) -> p x y", y=shape[1])
            if len(shape) == 3:
                v = v.rearrange("p (x y z) -> p x y z", y=shape[1], z=shape[2])
            return v

        def banks(b, n=2):
            return PS[:, b:b + n, :].rearrange("p b n -> p (b n)")

        def col(name, j, k=0):
            r = ROWS[name] + k
            return cols[:, ds(j, 1), r:r + 1].rearrange("p a b -> p (a b)")

        s_const = sem("s_const")
        s_rows = sem("s_rows")
        s_x = sem("s_x")
        s_zero = sem("s_zero")
        s_sumsq = sem("s_sumsq")
        s_var = sem("s_var")
        s_root = sem("s_root")
        s_scaled = sem("s_scaled")
        s_turned = sem("s_turned")
        s_ut = sem("s_ut")
        s_params = sem("s_params")
        s_turned_rows = sem("s_turned_rows")
        s_lb = sem("s_lb")
        s_lbexp = sem("s_lbexp")

        rows = part(0, (D,))
        scratch = part(1 * T, (2, D))
        xtile = RB[:, :, :]
        sumsq, meansq, root, rstd = (small[:, 8 * k:8 * k + 8] for k in range(4))
        lbound, lslack, t0, t1 = (small[:, 32 + 8 * k:40 + 8 * k] for k in range(4))

        with nc.Block() as block:
            @block.sync
            def _(sp):
                sp.dma_start(square[:], a["c_square"]).then_inc(s_const, 16)
                sp.dma_start(xtile, a["x"].rearrange("o (m p) d -> p (o m) d", p=P)).then_inc(s_x, 16)
                sp.wait_ge(s_zero, 1)
                for name, r in ROWS.items():
                    src = {"lb0": a["lb_logits"][0:1, :], "lb1": a["lb_logits"][1:2, :],
                           "conv_w": a["conv_w"].rearrange("o k d -> (o k) d"),
                           "conv_w_2": a["conv_w_2"].rearrange("o k d -> (o k) d")}.get(name)
                    if src is None:
                        full = name if name in a else name + "_2"
                        src = a[full]
                    n, w = src.shape
                    sp.dma_start(rows[r:r + n, 0:w], src).then_inc(s_rows, 16)

            @block.scalar
            def _(act):
                act.wait_ge(s_x, 16)
                for m in range(NT):
                    act.activation(scratch[:, m % 2, :], xtile[:, m, :], ACT.Square, accum_out=sumsq[:, m:m + 1])
                    act.drain()
                act.nop().then_inc(s_sumsq, 1)
                act.wait_ge(s_var, 1)
                act.activation(root, meansq, ACT.Sqrt).then_inc(s_root, 1)
                act.wait_ge(s_lb, 1)
                act.activation(t0, t0, ACT.Exp)
                act.activation(t1, t1, ACT.Exp)
                act.drain()
                act.nop().then_inc(s_lbexp, 1)

            @block.vector
            def _(dve):
                dve.memset(rows, 0.0).then_inc(s_zero, 1)
                dve.wait_ge(s_sumsq, 1)
                dve.tensor_scalar(meansq, sumsq, 1.0 / D, EPS, ALU.mult, ALU.add).then_inc(s_var, 1)
                dve.wait_ge(s_root, 1)
                dve.reciprocal(rstd, root)
                dve.drain()
                for m in range(NT):
                    dve.tensor_scalar(xtile[:, m, :], xtile[:, m, :], rstd[:, m:m + 1], None,
                                      ALU.mult).then_inc(s_scaled, 1)
                for j in range(ND):
                    dve.wait_ge(s_turned_rows, j + 1)
                    dve.tensor_copy(cols[:, j, :], PS[:, 4 + j % 4, 0:NROWS]).then_inc(s_params, 1)
                dve.drain()
                for m in range(NT):
                    dve.wait_ge(s_turned, m + 1)
                    dve.tensor_tensor(RA[:, :, m * P:(m + 1) * P],
                                      banks(2 * (m % 2)).rearrange("p (c t) -> p c t", c=ND),
                                      cols[:, :, ROWS["ln_g"]:ROWS["ln_g"] + 1].to_broadcast([P, ND, P]),
                                      ALU.mult).then_inc(s_ut, 1)
                l0, l1 = cols[:, :, ROWS["lb0"]], cols[:, :, ROWS["lb1"]]
                dve.tensor_tensor(t0, l0, l1, ALU.max)
                dve.drain()
                dve.tensor_tensor(t1, l1, t0, ALU.subtract)
                dve.tensor_tensor(t0, l0, t0, ALU.subtract)
                dve.drain()
                dve.nop().then_inc(s_lb, 1)
                dve.wait_ge(s_lbexp, 1)
                dve.tensor_tensor(lslack, t0, t1, ALU.add)
                dve.drain()
                dve.reciprocal(lslack, lslack)
                dve.drain()
                dve.tensor_tensor(lbound, t0, lslack, ALU.mult)
                dve.drain()
                dve.tensor_scalar(lslack, lbound, -1.0, 1.0, ALU.mult, ALU.add)

            @block.tensor
            def _(pe):
                pe.wait_ge(s_const, 16)
                pe.wait_ge(s_rows, 16 * len(ROWS))
                for j in range(ND):
                    if j >= 4:
                        pe.wait_ge(s_params, j - 3)
                    pe.transpose(PS[:, 4 + j % 4, 0:NROWS], rows[0:NROWS, j * P:(j + 1) * P],
                                 ident[0:NROWS, 0:NROWS]).then_inc(s_turned_rows, 1)
                for m in range(NT):
                    pe.wait_ge(s_scaled, m + 1)
                    if m >= 2:
                        pe.wait_ge(s_ut, m - 1)
                    for c in range(ND):
                        last = pe.transpose(banks(2 * (m % 2))[:, c * P:(c + 1) * P],
                                            xtile[:, m, c * P:(c + 1) * P], ident)
                    last.then_inc(s_turned, 1)
        if upto < 1:
            return

        VAL, GLU, FORGET, KEY, QUERY, VALUE, GATE = (part(k * T, (T,)) for k in range(7))
        CUM, CUMEXP, QDEC, ACC, SQ = (part(k * T, (T,)) for k in range(7, 12))
        DECAY = [part(k * T, (T,)) for k in (12, 13)]
        QK = [part(k * T, (T,)) for k in (14, 15)]
        WEIGHTS = part(16 * T, (NT, P))
        KDEC = part(17 * T, (NT, P))
        STATE = part(18 * T, (NT, P))
        PAD = part(19 * T, (CONV_K - 1 + T,))
        RESTART = part(20 * T + 64, (T,))
        WSLOT = [part(21 * T + 64 + k * T, (ND, P)) for k in range(3)]
        MASKS = sb("MASKS", [P, LEVELS + 1, P], U8)
        NPROJ = 6
        FIRST_COL = [0, D, 4 * D, 3 * D, 5 * D, 6 * D]

        s_tables = sem("s_tables")
        s_wland = [sem(f"s_wland{k}") for k in range(3)]
        s_proj = sem("s_proj")
        s_evac = sem("s_evac")
        s_used = sem("s_used")
        s_cum = sem("s_cum")
        s_logf = sem("s_logf")
        s_diff = sem("s_diff")
        s_dexp = sem("s_dexp")
        s_qk = sem("s_qk")
        s_aprod = sem("s_aprod")
        s_amask = sem("s_amask")
        s_kd = sem("s_kd")
        s_kdt = sem("s_kdt")
        s_kdec = sem("s_kdec")
        s_dstate = sem("s_dstate")
        s_state = sem("s_state")
        s_o = sem("s_o")
        s_osq = sem("s_osq")
        s_oms = sem("s_oms")
        s_oroot = sem("s_oroot")
        s_ohead = sem("s_ohead")
        s_conv = sem("s_conv")
        s_mu = sem("s_mu")
        s_cent = sem("s_cent")
        s_csq = sem("s_csq")
        s_cvar = sem("s_cvar")
        s_croot = sem("s_croot")
        s_cnorm = sem("s_cnorm")
        s_cout = sem("s_cout")
        s_epsv = sem("s_epsv")
        s_held = sem("s_held")
        eps = small[:, 64:65]

        def split(v, size):
            return v.rearrange("p (b u s) -> p b u s", u=2, s=size)

        def hold(eng):
            eng.sem_inc(s_held, 1)

        def chunks(v):
            return v.rearrange("p (c t) -> p c t", t=P)

        with nc.Block() as block:
            @block.sync
            def _(sp):
                sp.dma_start(RESTART, a["c_restart"]).then_inc(s_tables, 16)
                sp.dma_start(WEIGHTS, a["c_masks"]).then_inc(s_tables, 16)

                def load(j, s):
                    c0 = FIRST_COL[s]
                    w = a["w_in"].rearrange("o (k p) n -> p (o k) n", p=P)[:, :, ds(j * P + c0, P)]
                    sp.dma_start(WSLOT[s % 3], w).then_inc(s_wland[s % 3], 16)

                for s in range(NPROJ):
                    if s >= 3:
                        sp.wait_ge(s_proj, s - 2)
                    load(0, s)
                with sp.Fori(1, ND) as j:
                    for s in range(NPROJ):
                        sp.wait_ge(s_proj, NPROJ * j + s - 2)
                        hold(sp)
                        load(j, s)

            def pe_project(pe, j, s):
                pe.wait_ge(s_wland[s % 3], 32 * j + 16 * (s // 3) + 16)
                if s >= 2 or not isinstance(j, int):
                    pe.wait_ge(s_evac, NPROJ * j + s - 1)
                w = WSLOT[s % 3]
                o = banks(2 * (s % 2))
                if s == 4:
                    for c in range(NT):
                        for k in range(ND):
                            last = pe.matmul(o[:, c * P:(c + 1) * P], RA[:, k, c * P:(c + 1) * P], w[:, k, :],
                                             start=(k == 0), stop=(k == ND - 1))
                else:
                    for h in range(2):
                        for k in range(ND):
                            last = pe.matmul(o[:, h * HALF:(h + 1) * HALF], w[:, k, :],
                                             RA[:, k, h * HALF:(h + 1) * HALF],
                                             start=(k == 0), stop=(k == ND - 1))
                last.then_inc(s_proj, 1)

            def pe_mean(pe, o, v, s):
                for h in range(2):
                    last = pe.matmul(o[:, h * HALF:(h + 1) * HALF], mean, v[:, h * HALF:(h + 1) * HALF],
                                     start=True, stop=True)
                last.then_inc(s, 1)

            def pe_level(pe, j, level):
                if level == LEVELS:
                    keys, queries = KEY, QUERY
                else:
                    pe.wait_ge(s_qk, LEVELS * j + level + 1)
                    keys = queries = QK[level % 2]
                if level >= 2:
                    pe.wait_ge(s_amask, (LEVELS + 1) * j + level - 1)
                o = banks(4 + 2 * (level % 2))
                for c in range(NT):
                    last = pe.matmul(o[:, c * P:(c + 1) * P], keys[:, c * P:(c + 1) * P],
                                     queries[:, c * P:(c + 1) * P], start=True, stop=True)
                last.then_inc(s_aprod, 1)

            def pe_conv_mean(pe, j):
                pe.wait_ge(s_conv, j + 1)
                pe_mean(pe, banks(4), ACC, s_mu)

            def pe_conv_var(pe, j):
                pe.wait_ge(s_csq, j + 1)
                pe_mean(pe, banks(6), SQ, s_cvar)
                pe.wait_ge(s_cnorm, j + 1)

            def pe_out(pe, j):
                pe.wait_ge(s_evac, NPROJ * j + 5)
                pe.wait_ge(s_amask, (LEVELS + 1) * (j + 1))
                pe.wait_ge(s_kd, j + 1)
                for c in range(NT):
                    last = pe.transpose(banks(4)[:, c * P:(c + 1) * P], KEY[:, c * P:(c + 1) * P], ident)
                last.then_inc(s_kdt, 1)
                pe.wait_ge(s_kdec, j + 1)
                for c in range(NT):
                    last = pe.matmul(banks(6)[:, c * P:(c + 1) * P], KDEC[:, c, :],
                                     VALUE[:, c * P:(c + 1) * P], start=True, stop=True)
                last.then_inc(s_dstate, 1)
                pe.wait_ge(s_state, j + 1)
                for c in range(NT):
                    o = banks(4)[:, c * P:(c + 1) * P]
                    last = pe.matmul(o, VALUE[:, c * P:(c + 1) * P], WEIGHTS[:, c, :], start=True, stop=(c == 0))
                    if c:
                        last = pe.matmul(o, STATE[:, c, :], QDEC[:, c * P:(c + 1) * P], start=False, stop=True)
                last.then_inc(s_o, 1)
                pe.wait_ge(s_osq, j + 1)
                pe_mean(pe, banks(6), SQ, s_oms)

            @block.tensor
            def _(pe):
                pe.wait_ge(s_tables, 32)
                for s in range(NPROJ):
                    pe_project(pe, 0, s)

                def small_work(j, fill):
                    fill(0)
                    fill(1)
                    pe_conv_mean(pe, j)
                    fill(2)
                    pe_conv_var(pe, j)
                    fill(3)
                    for level in range(LEVELS + 1):
                        pe_level(pe, j, level)
                    pe_out(pe, j)
                    fill(4)
                    fill(5)

                with pe.Fori(0, ND - 1) as j:
                    small_work(j, lambda s: pe_project(pe, j + 1, s))
                small_work(ND - 1, lambda s: None)

            @block.scalar
            def _(act):
                def evacuate(j, s):
                    pair = banks(2 * (s % 2))
                    act.wait_ge(s_proj, NPROJ * j + s + 1)
                    later = not (isinstance(j, int) and j == 0)
                    if s == 0:
                        if later:
                            act.wait_ge(s_used, j)
                        act.activation(VAL, pair, ACT.Copy).then_inc(s_evac, 1)
                    if s == 1:
                        act.activation(GLU, pair, ACT.Sigmoid).then_inc(s_evac, 1)
                    if s == 2:
                        if later:
                            act.wait_ge(s_ohead, j)
                        act.activation(FORGET, pair, ACT.Sigmoid)
                        act.activation(KEY, pair, ACT.Sigmoid, scale=-1.0).then_inc(s_evac, 1)
                    if s == 3:
                        act.activation(QUERY, pair, ACT.Silu).then_inc(s_evac, 1)
                    if s == 4:
                        act.activation(VALUE, pair, ACT.Copy).then_inc(s_evac, 1)
                    if s == 5:
                        act.activation(GATE, pair, ACT.Silu).then_inc(s_evac, 1)

                def conv_norm(j):
                    act.wait_ge(s_cent, j + 1)
                    act.activation(SQ, ACC, ACT.Square).then_inc(s_csq, 1)
                    act.wait_ge(s_cvar, j + 1)
                    act.activation(SQ, banks(6), ACT.Sqrt, bias=eps).then_inc(s_croot, 1)
                    act.wait_ge(s_cnorm, j + 1)
                    act.activation(RB[:, ds(j, 1), :].rearrange("p a t -> p (a t)"), ACC, ACT.Silu,
                                   scale=col("cnorm_g", j), bias=col("cnorm_b", j)).then_inc(s_cout, 1)

                def decays(j):
                    act.drain()
                    act.activation(FORGET, FORGET, ACT.Ln, scale=lslack[:, ds(j, 1)],
                                   bias=lbound[:, ds(j, 1)]).then_inc(s_logf, 1)
                    act.wait_ge(s_cum, j + 1)
                    act.activation(CUMEXP, CUM, ACT.Exp).then_inc(s_dexp, 1)
                    level_decays(j, 0, 2)

                def level_decays(j, first, end):
                    for n in range(first, end):
                        act.wait_ge(s_diff, (LEVELS + 1) * j + n + 1)
                        act.activation(DECAY[n % 2], DECAY[n % 2], ACT.Exp).then_inc(s_dexp, 1)

                def head_out(j):
                    act.wait_ge(s_kdt, j + 1)
                    act.activation(KDEC.rearrange("p c k -> p (c k)"), banks(4), ACT.Copy).then_inc(s_kdec, 1)
                    act.wait_ge(s_o, j + 1)
                    act.activation(SQ, banks(4), ACT.Square).then_inc(s_osq, 1)
                    act.wait_ge(s_oms, j + 1)
                    act.activation(SQ, banks(6), ACT.Sqrt, bias=eps).then_inc(s_oroot, 1)

                def tile(j, more):
                    for s in range(2, NPROJ):
                        evacuate(j, s)
                    decays(j)
                    if more:
                        evacuate(j + 1, 0)
                        evacuate(j + 1, 1)
                    conv_norm(j)
                    level_decays(j, 2, LEVELS + 1)
                    head_out(j)

                act.wait_ge(s_epsv, 1)
                evacuate(0, 0)
                evacuate(0, 1)
                tile(0, True)
                with act.Fori(1, ND - 1) as j:
                    tile(j, True)
                tile(ND - 1, False)

            @block.gpsimd
            def _(pool):
                pool.memset(eps, EPS).then_inc(s_epsv, 1)
                with pool.Fori(0, ND) as j:
                    pool.wait_ge(s_cum, j + 1)
                    for level in range(LEVELS):
                        size = 1 << level
                        if level >= 2:
                            pool.wait_ge(s_qk, LEVELS * j + level - 1)
                        b, d = split(CUM, size), split(DECAY[level % 2], size)
                        pivot = b[:, :, 0, size - 1:size].to_broadcast([P, T // (2 * size), size])
                        pool.tensor_tensor(d[:, :, 1, :], b[:, :, 1, :], pivot, ALU.subtract)
                        pool.tensor_tensor(d[:, :, 0, :], pivot, b[:, :, 0, :], ALU.subtract).then_inc(s_diff, 1)
                    pool.wait_ge(s_qk, LEVELS * j + LEVELS - 1)
                    b = chunks(CUM)
                    pool.tensor_tensor(chunks(DECAY[LEVELS % 2]), b[:, :, P - 1:P].to_broadcast([P, NT, P]), b,
                                       ALU.subtract).then_inc(s_diff, 1)
                    pool.wait_ge(s_dexp, (LEVELS + 2) * (j + 1))
                    pool.wait_ge(s_aprod, (LEVELS + 1) * (j + 1))
                    pool.tensor_tensor(KEY, KEY, DECAY[LEVELS % 2], ALU.mult).then_inc(s_kd, 1)
                    pool.drain()

            @block.vector
            def _(dve):
                dve.memset(PAD[:, 0:CONV_K - 1], 0.0)
                dve.wait_ge(s_tables, 32)
                dve.tensor_copy(MASKS[:], WEIGHTS)
                dve.drain()
                dve.memset(WEIGHTS, 0.0)
                dve.drain()
                with dve.Fori(0, ND) as j:
                    dve.wait_ge(s_evac, NPROJ * j + 2)
                    dve.tensor_tensor(PAD[:, CONV_K - 1:], VAL, GLU, ALU.mult).then_inc(s_used, 1)
                    dve.wait_ge(s_evac, NPROJ * j + 3)
                    dve.tensor_scalar(KEY, KEY, lslack[:, ds(j, 1)], None, ALU.mult)
                    dve.wait_ge(s_logf, j + 1)
                    dve.tensor_tensor_scan(CUM, RESTART, FORGET, 0.0, ALU.mult, ALU.add).then_inc(s_cum, 1)
                    dve.wait_ge(s_dexp, (LEVELS + 2) * j + 1)
                    dve.tensor_tensor(QDEC, QUERY, CUMEXP, ALU.mult)
                    dve.drain()
                    dve.tensor_scalar(ACC, PAD[:, 0:T], col("conv_w", j, 0), col("conv_b", j), ALU.mult, ALU.add)
                    for k in range(1, CONV_K):
                        dve.drain()
                        last = dve.scalar_tensor_tensor(ACC, PAD[:, k:k + T], col("conv_w", j, k), ACC,
                                                        ALU.mult, ALU.add)
                    last.then_inc(s_conv, 1)
                    dve.wait_ge(s_mu, j + 1)
                    dve.tensor_tensor(ACC, ACC, banks(4), ALU.subtract).then_inc(s_cent, 1)
                    dve.wait_ge(s_croot, j + 1)
                    dve.reciprocal(SQ, SQ)
                    dve.drain()
                    dve.tensor_tensor(ACC, ACC, SQ, ALU.mult).then_inc(s_cnorm, 1)

                    def masked(level):
                        dve.drain()
                        dve.wait_ge(s_aprod, (LEVELS + 1) * j + level + 1)
                        hold(dve)
                        dve.copy_predicated(WEIGHTS, MASKS[:, level:level + 1, :].to_broadcast([P, NT, P]),
                                            banks(4 + 2 * (level % 2)).rearrange("p (c t) -> p c t", t=P)
                                            ).then_inc(s_amask, 1)

                    for level in range(LEVELS):
                        size = 1 << level
                        dve.wait_ge(s_dexp, (LEVELS + 2) * j + level + 2)
                        if level >= 2:
                            dve.wait_ge(s_aprod, (LEVELS + 1) * j + level - 1)
                        qk, e = split(QK[level % 2], size), split(DECAY[level % 2], size)
                        dve.tensor_tensor(qk[:, :, 1, :], split(QUERY, size)[:, :, 1, :], e[:, :, 1, :], ALU.mult)
                        dve.tensor_tensor(qk[:, :, 0, :], split(KEY, size)[:, :, 0, :], e[:, :, 0, :],
                                          ALU.mult).then_inc(s_qk, 1)
                        if level:
                            masked(level - 1)
                    masked(LEVELS - 1)
                    masked(LEVELS)
                    dve.wait_ge(s_dstate, j + 1)
                    dstate = banks(6).rearrange("p (c v) -> p c v", v=P)
                    dve.tensor_copy(STATE[:, 1, :], dstate[:, 0, :])
                    for c in range(1, NT - 1):
                        dve.drain()
                        last = dve.scalar_tensor_tensor(STATE[:, c + 1, :], STATE[:, c, :],
                                                        CUMEXP[:, c * P + P - 1:c * P + P], dstate[:, c, :],
                                                        ALU.mult, ALU.add)
                    last.then_inc(s_state, 1)
                    dve.wait_ge(s_oroot, j + 1)
                    dve.reciprocal(SQ, SQ)
                    dve.drain()
                    dve.tensor_tensor(SQ, banks(4), SQ, ALU.mult)
                    dve.drain()
                    dve.wait_ge(s_evac, NPROJ * (j + 1))
                    hold(dve)
                    dve.scalar_tensor_tensor(RC[:, ds(j, 1), :].rearrange("p a t -> p (a t)"), SQ,
                                             col("onorm_g", j), GATE, ALU.mult, ALU.mult).then_inc(s_ohead, 1)
        if upto < 2:
            return

        CONVOUT = part(0, (ND, T))
        WOUT_A = part(8 * T, (ND, T))
        SILU = [part((16 + k) * T, (T,)) for k in range(2)]
        WPAIR = [part((18 + k) * T, (ND, P)) for k in range(4)]

        s_w2land = [sem(f"s_w2land{k}") for k in range(4)]
        s_proj2 = sem("s_proj2")
        s_silu = sem("s_silu")
        s_cgated = sem("s_cgated")
        s_wouta = sem("s_wouta")
        s_woutb = sem("s_woutb")

        with nc.Block() as block:
            @block.sync
            def _(sp):
                def load(b, n):
                    t = 2 * b + n // 2
                    src = a["w_in"] if n % 2 == 0 else a["w_pw2"]
                    c0 = 2 * D if n % 2 == 0 else 0
                    w = src.rearrange("o (k p) n -> p (o k) n", p=P)[:, :, ds(t * P + c0, P)]
                    sp.dma_start(WPAIR[n], w).then_inc(s_w2land[n], 16)

                for n in range(4):
                    load(0, n)
                sp.dma_start(WOUT_A, a["w_out"].rearrange("o (k p) n -> p (o k) n", p=P)[:, 0:ND, :]
                             ).then_inc(s_wouta, 16)
                with sp.Fori(1, ND // 2) as b:
                    for n in range(4):
                        sp.wait_ge(s_proj2, 4 * b + n - 3)
                        hold(sp)
                        load(b, n)

            @block.tensor
            def _(pe):
                def pair(b):
                    for n in range(4):
                        pe.wait_ge(s_w2land[n], 16 * b + 16)
                        if not isinstance(b, int):
                            pe.wait_ge(s_cgated, 2 * b + n // 2 - 1)
                        src = RA if n % 2 == 0 else RB
                        for h in range(2):
                            for k in range(ND):
                                last = pe.matmul(banks(2 * n)[:, h * HALF:(h + 1) * HALF], WPAIR[n][:, k, :],
                                                 src[:, k, h * HALF:(h + 1) * HALF],
                                                 start=(k == 0), stop=(k == ND - 1))
                        last.then_inc(s_proj2, 1)

                pair(0)
                with pe.Fori(1, ND // 2) as b:
                    pair(b)

            @block.scalar
            def _(act):
                def pair(b):
                    for t in range(2):
                        act.wait_ge(s_proj2, 4 * b + 2 * t + 1)
                        if not isinstance(b, int):
                            act.wait_ge(s_cgated, 2 * b + t - 1)
                        act.activation(SILU[t], banks(4 * t), ACT.Silu).then_inc(s_silu, 1)

                pair(0)
                with act.Fori(1, ND // 2) as b:
                    pair(b)

            @block.vector
            def _(dve):
                with dve.Fori(0, ND // 2) as b:
                    for t in range(2):
                        dve.wait_ge(s_silu, 2 * b + t + 1)
                        dve.wait_ge(s_proj2, 4 * b + 2 * t + 2)
                        hold(dve)
                        dve.scalar_tensor_tensor(CONVOUT[:, ds(2 * b + t, 1), :].rearrange("p a t -> p (a t)"),
                                                 banks(4 * t + 2), col("b_pw2", 2 * b + t), SILU[t],
                                                 ALU.add, ALU.mult).then_inc(s_cgated, 1)

        XROW = [part((16 + k) * T, (T,)) for k in range(2)]
        SQUARES = sb("SQUARES", [P, T])
        PTOK = part(18 * T, (NT, 256))
        PFEAT = part(20 * T, (2, T))
        WPP = part(22 * T, (2, T))
        FINAL_G = part(24 * T, (T,))
        s_xrow = [sem(f"s_xrow{k}") for k in range(2)]
        s_hprod = sem("s_hprod")
        s_h = sem("s_h")
        s_ptok = sem("s_ptok")
        s_pturn = sem("s_pturn")
        s_pfeat = sem("s_pfeat")
        s_wpp = sem("s_wpp")
        s_hss = sem("s_hss")
        s_hvar = sem("s_hvar")
        s_hroot = sem("s_hroot")

        with nc.Block() as block:
            @block.sync
            def _(sp):
                sp.dma_start(RB[:], a["w_out"].rearrange("o (k p) n -> p (o k) n", p=P)[:, ND:2 * ND, :]
                             ).then_inc(s_woutb, 16)
                sp.dma_start(PTOK, a["p"].rearrange("l o (m p) d -> p (l o m) d", p=P)).then_inc(s_ptok, 16)
                for m in range(NT):
                    if m >= 2:
                        sp.wait_ge(s_h, m - 1)
                    sp.dma_start(XROW[m % 2], a["x"][0, m * P:(m + 1) * P, :]).then_inc(s_xrow[m % 2], 16)
                sp.dma_start(WPP, a["w_pp"].rearrange("o (k p) n -> p (o k) n", p=P)).then_inc(s_wpp, 16)
                sp.dma_start(FINAL_G, a["final_g"].rearrange("(o d) -> o d", o=1).to_broadcast([P, D])
                             ).then_inc(s_wpp, 16)

            @block.tensor
            def _(pe):
                pe.wait_ge(s_ptok, 16)
                for k in range(2):
                    for m in range(NT):
                        last = pe.transpose(banks(4 + 2 * k)[:, m * P:(m + 1) * P],
                                            PTOK[:, m, k * P:(k + 1) * P], ident)
                last.then_inc(s_pturn, 1)
                pe.wait_ge(s_wouta, 16)
                pe.wait_ge(s_woutb, 16)
                for m in range(NT):
                    if m == 2:
                        pe.wait_ge(s_pfeat, 1)
                    if m >= 4:
                        pe.wait_ge(s_h, m - 3)
                    for h in range(2):
                        for k in range(2 * ND):
                            lhs = CONVOUT if k < ND else RC
                            w = WOUT_A if k < ND else RB
                            last = pe.matmul(banks(2 * (m % 4))[:, h * HALF:(h + 1) * HALF],
                                             lhs[:, k % ND, m * P:(m + 1) * P],
                                             w[:, k % ND, h * HALF:(h + 1) * HALF],
                                             start=(k == 0), stop=(k == 2 * ND - 1))
                    last.then_inc(s_hprod, 1)

            @block.vector
            def _(dve):
                dve.wait_ge(s_pturn, 1)
                for k in range(2):
                    last = dve.tensor_copy(PFEAT[:, k, :], banks(4 + 2 * k))
                last.then_inc(s_pfeat, 1)
                for m in range(NT):
                    dve.wait_ge(s_hprod, m + 1)
                    dve.wait_ge(s_xrow[m % 2], 16 * (m // 2) + 16)
                    dve.tensor_tensor(RA[:, m, :], banks(2 * (m % 4)), XROW[m % 2], ALU.add).then_inc(s_h, 1)
                dve.wait_ge(s_hss, 1)
                dve.tensor_scalar(meansq, sumsq, 1.0 / D, EPS, ALU.mult, ALU.add).then_inc(s_hvar, 1)
                dve.wait_ge(s_hroot, 1)
                dve.reciprocal(rstd, root)

            @block.scalar
            def _(act):
                for m in range(NT):
                    act.wait_ge(s_h, m + 1)
                    act.activation(SQUARES[:], RA[:, m, :], ACT.Square,
                                   accum_out=sumsq[:, m:m + 1])
                    act.drain()
                act.nop().then_inc(s_hss, 1)
                act.wait_ge(s_hvar, 1)
                act.activation(root, meansq, ACT.Sqrt).then_inc(s_hroot, 1)
        if upto < 3:
            return

        retire(s_wpp, s_held)
        x1_dram = nc.dram_tensor("x1_dram", [NT, P, D], F32).ap()
        NORMED = [part((16 + k) * T, (T,)) for k in range(2)]
        GATES = [part((18 + k) * T, (T,)) for k in range(2)]
        WPG = part(8 * T, (ND, T))
        s_wpg = sem("s_wpg")
        s_normed = sem("s_normed")
        s_nturn = sem("s_nturn")
        s_hnt = sem("s_hnt")
        s_gprod = sem("s_gprod")
        s_gsig = sem("s_gsig")
        s_gmul = sem("s_gmul")
        s_h1 = sem("s_h1")
        s_f1 = sem("s_f1")
        s_x1 = sem("s_x1")
        s_st = [sem(f"s_st{k}") for k in range(3)]
        s_u2n = sem("s_u2n")
        s_u2turn = sem("s_u2turn")
        s_u2t = sem("s_u2t")
        s_x1st = sem("s_x1st")

        def root_mean_square(act, ready, n, src=RA):
            for m in range(NT):
                act.wait_ge(ready, m + 1)
                act.activation(SQUARES[:], src[:, m, :], ACT.Square, accum_out=sumsq[:, m:m + 1])
                act.drain()
            act.nop().then_inc(s_st[0], 1)
            act.wait_ge(s_st[1], n)
            act.activation(root, meansq, ACT.Sqrt).then_inc(s_st[2], 1)

        def reciprocal_roots(dve, n):
            dve.wait_ge(s_st[0], n)
            dve.tensor_scalar(meansq, sumsq, 1.0 / D, EPS, ALU.mult, ALU.add).then_inc(s_st[1], 1)
            dve.wait_ge(s_st[2], n)
            dve.reciprocal(rstd, root)
            dve.drain()

        def pe_turn(pe, dst, src, done):
            for c in range(ND):
                last = pe.transpose(dst[:, c * P:(c + 1) * P], src[:, c * P:(c + 1) * P], ident)
            last.then_inc(done, 1)

        def gain_of(name):
            r = ROWS[name]
            return cols[:, :, r:r + 1].to_broadcast([P, ND, P])

        with nc.Block() as block:
            @block.sync
            def _(sp):
                sp.dma_start(WPG, a["w_pg"].rearrange("o (k p) n -> p (o k) n", p=P)).then_inc(s_wpg, 16)
                for m in range(NT):
                    sp.wait_ge(s_x1, m + 1)
                    sp.dma_start(x1_dram[m], RA[:, m, :]).then_inc(s_x1st, 16)
                sp.wait_ge(s_x1st, 16 * NT)

            @block.tensor
            def _(pe):
                for m in range(NT):
                    pe.wait_ge(s_normed, m + 1)
                    if m >= 2:
                        pe.wait_ge(s_hnt, m - 1)
                    pe_turn(pe, banks(2 * (m % 2)), NORMED[m % 2], s_nturn)
                pe.wait_ge(s_hnt, NT)
                pe.wait_ge(s_wpg, 16)
                pe.wait_ge(s_wpp, 32)
                for m in range(NT):
                    if m >= 2:
                        pe.wait_ge(s_gmul, m - 1)
                    for h in range(2):
                        for k in range(2):
                            pe.matmul(banks(4 + 2 * (m % 2))[:, h * HALF:(h + 1) * HALF],
                                      PFEAT[:, k, m * P:(m + 1) * P], WPP[:, k, h * HALF:(h + 1) * HALF],
                                      start=(k == 0), stop=(k == 1))
                    for h in range(2):
                        for k in range(ND):
                            last = pe.matmul(banks(2 * (m % 2))[:, h * HALF:(h + 1) * HALF],
                                             RB[:, k, m * P:(m + 1) * P], WPG[:, k, h * HALF:(h + 1) * HALF],
                                             start=(k == 0), stop=(k == ND - 1))
                    last.then_inc(s_gprod, 1)
                pe.wait_ge(s_gmul, NT)
                for m in range(NT):
                    pe.wait_ge(s_u2n, m + 1)
                    if m >= 2:
                        pe.wait_ge(s_u2t, m - 1)
                    pe_turn(pe, banks(2 * (m % 2)), NORMED[m % 2], s_u2turn)

            @block.scalar
            def _(act):
                for m in range(NT):
                    act.wait_ge(s_gprod, m + 1)
                    if m >= 2:
                        act.wait_ge(s_h1, m - 1)
                    act.activation(GATES[m % 2], banks(2 * (m % 2)), ACT.Sigmoid).then_inc(s_gsig, 1)
                root_mean_square(act, s_h1, 1)
                root_mean_square(act, s_x1, 2)

            @block.vector
            def _(dve):
                def evacuate(m, turned, dst, name, done):
                    dve.wait_ge(turned, m + 1)
                    dve.tensor_tensor(dst[:, :, m * P:(m + 1) * P],
                                      banks(2 * (m % 2)).rearrange("p (c t) -> p c t", c=ND),
                                      gain_of(name), ALU.mult).then_inc(done, 1)

                for m in range(NT):
                    if m >= 2:
                        dve.wait_ge(s_nturn, m - 1)
                    dve.tensor_scalar(NORMED[m % 2], RA[:, m, :], rstd[:, m:m + 1], None,
                                      ALU.mult).then_inc(s_normed, 1)
                    if m:
                        evacuate(m - 1, s_nturn, RB, "pe_norm_g", s_hnt)
                evacuate(NT - 1, s_nturn, RB, "pe_norm_g", s_hnt)
                for m in range(NT):
                    dve.wait_ge(s_gsig, m + 1)
                    g = GATES[m % 2]
                    dve.tensor_tensor(g, g, banks(4 + 2 * (m % 2)), ALU.mult).then_inc(s_gmul, 1)
                    dve.drain()
                    dve.tensor_tensor(RA[:, m, :], RA[:, m, :], g, ALU.add).then_inc(s_h1, 1)
                reciprocal_roots(dve, 1)
                dve.wait_ge(s_wpp, 32)
                for m in range(NT):
                    dve.scalar_tensor_tensor(RA[:, m, :], RA[:, m, :], rstd[:, m:m + 1], FINAL_G,
                                             ALU.mult, ALU.mult).then_inc(s_x1, 1)
                reciprocal_roots(dve, 2)
                for m in range(NT):
                    if m >= 2:
                        dve.wait_ge(s_u2turn, m - 1)
                    dve.tensor_scalar(NORMED[m % 2], RA[:, m, :], rstd[:, m:m + 1], None,
                                      ALU.mult).then_inc(s_u2n, 1)
                    if m:
                        evacuate(m - 1, s_u2turn, RC, "norm_mix_g", s_u2t)
                evacuate(NT - 1, s_u2turn, RC, "norm_mix_g", s_u2t)
        if upto < 5:
            return

        NB = ND // 2
        GATE0_COL = 2 * D + 768 + 256 + 32
        RPAD = [part(k * (T + 4), (T + 4,))[:, 0:T + 3] for k in range(2)]
        REC, INP, AEXP, THMUL, GELU, SIG, XA = ([part((2 + 2 * n + k) * T + 8, (T,)) for k in range(2)]
                                                for n in range(7))
        WREC = [part((16 + k) * T + 8, (ND, P)) for k in range(3)]
        WAX = part(19 * T + 8, (2, 2, 256))
        WQC = RB[:, 0:6, :].rearrange("p k t -> p (k t)").rearrange("p (k n) -> p k n", n=768)
        WKV = part(21 * T, (ND, 288))
        CREC = [small[:, 72 + 8 * k:80 + 8 * k] for k in range(5)]
        crec = CREC[0]
        XCOLS = [0, P, D, D + P, GATE0_COL, GATE0_COL + P]

        s_rland = [sem(f"s_rland{k}") for k in range(3)]
        s_ax = sem("s_ax")
        s_wqc = sem("s_wqc")
        s_wkv = sem("s_wkv")
        s_rproj = sem("s_rproj")
        s_revac = sem("s_revac")
        s_xa = sem("s_xa")
        s_ri = sem("s_ri")
        s_riev = sem("s_riev")
        s_la = sem("s_la")
        s_at = sem("s_at")
        s_mq = sem("s_mq")
        s_mroot = sem("s_mroot")
        s_mt = sem("s_mt")
        s_soft = sem("s_soft")
        s_softexp = sem("s_softexp")

        with nc.Block() as block:
            @block.sync
            def _(sp):
                def load(b, n):
                    w = a["w_in_2"].rearrange("o (k p) n -> p (o k) n", p=P)[:, :, ds(b * 256 + XCOLS[n], P)]
                    sp.dma_start(WREC[n % 3], w).then_inc(s_rland[n % 3], 16)

                def load_gates(b):
                    for i, name in enumerate(("lru_wa_2", "lru_wx_2")):
                        w = a[name].rearrange("o b (k p) n -> p (o b) k n", p=P)[:, ds(b, 1)]
                        sp.dma_start(WAX[:, i], w.rearrange("p a k n -> p (a k) n")).then_inc(s_ax, 16)

                for n in range(6):
                    if n >= 3:
                        sp.wait_ge(s_rproj, n - 2)
                    load(0, n)
                    if n == 2:
                        load_gates(0)
                w = a["w_in_2"].rearrange("o (k p) n -> p (o k) n", p=P)
                sp.dma_start(WQC, w[:, :, 2 * D:2 * D + 768]).then_inc(s_wqc, 16)
                sp.dma_start(WKV, w[:, :, 2 * D + 768:2 * D + 1056]).then_inc(s_wkv, 16)
                with sp.Fori(1, NB) as b:
                    for n in range(6):
                        sp.wait_ge(s_rproj, 6 * b + n - 2)
                        hold(sp)
                        load(b, n)
                    sp.wait_ge(s_ri, 2 * b)
                    hold(sp)
                    load_gates(b)

            @block.tensor
            def _(pe):
                def project(b, n):
                    pe.wait_ge(s_rland[n % 3], 32 * b + 16 * (n // 3) + 16)
                    if n >= 2 or not isinstance(b, int):
                        pe.wait_ge(s_revac, 6 * b + n - 1)
                    o = banks(2 * (n % 2))
                    for h in range(2):
                        for k in range(ND):
                            last = pe.matmul(o[:, h * HALF:(h + 1) * HALF], WREC[n % 3][:, k, :],
                                             RC[:, k, h * HALF:(h + 1) * HALF], start=(k == 0), stop=(k == ND - 1))
                    last.then_inc(s_rproj, 1)

                def gates(b, t):
                    pe.wait_ge(s_ax, 32 * b + 32)
                    pe.wait_ge(s_xa, 2 * b + 2)
                    if t or not isinstance(b, int):
                        pe.wait_ge(s_riev, 2 * b + t)
                    for i in range(2):
                        for h in range(2):
                            for k in range(2):
                                last = pe.matmul(banks(4 + 2 * i)[:, h * HALF:(h + 1) * HALF],
                                                 WAX[:, i, k, t * P:(t + 1) * P],
                                                 XA[k][:, h * HALF:(h + 1) * HALF], start=(k == 0), stop=(k == 1))
                    last.then_inc(s_ri, 1)

                def block_of(b):
                    for n in range(3):
                        project(b, n)
                    gates(b, 0)
                    project(b, 3)
                    gates(b, 1)
                    project(b, 4)
                    project(b, 5)

                block_of(0)
                with pe.Fori(1, NB) as b:
                    block_of(b)

            @block.scalar
            def _(act):
                def evacuate(b, n):
                    act.wait_ge(s_rproj, 6 * b + n + 1)
                    t, pair, later = n % 2, banks(2 * (n % 2)), not isinstance(b, int)
                    if n < 2:
                        if later:
                            act.wait_ge(s_xa, 2 * b)
                        act.activation(RPAD[t][:, 3:], pair, ACT.Copy).then_inc(s_revac, 1)
                    else:
                        if later:
                            act.wait_ge(s_mt, 2 * b + t - 1)
                        act.activation((GELU if n < 4 else SIG)[t], pair,
                                       ACT.Gelu_apprx_tanh if n < 4 else ACT.Sigmoid).then_inc(s_revac, 1)

                def gates(b, t):
                    act.wait_ge(s_ri, 2 * b + t + 1)
                    if not isinstance(b, int):
                        act.wait_ge(s_mt, 2 * b + t - 1)
                    act.activation(REC[t], banks(4), ACT.Sigmoid, bias=col("lru_ba", 2 * b + t))
                    act.activation(INP[t], banks(6), ACT.Sigmoid, bias=col("lru_bx", 2 * b + t)).then_inc(s_riev, 1)

                def block_of(b):
                    for n in range(3):
                        evacuate(b, n)
                    gates(b, 0)
                    evacuate(b, 3)
                    gates(b, 1)
                    evacuate(b, 4)
                    evacuate(b, 5)
                    for t in range(2):
                        act.wait_ge(s_la, 2 * b + t + 1)
                        act.activation(AEXP[t], REC[t], ACT.Exp)
                        act.activation(THMUL[t], REC[t], ACT.Tanh, scale=-1.0).then_inc(s_at, 1)
                    for t in range(2):
                        act.wait_ge(s_mq, 2 * b + t + 1)
                        act.activation(THMUL[t], THMUL[t], ACT.Sqrt).then_inc(s_mroot, 1)

                act.wait_ge(s_soft, 1)
                act.activation(CREC[1], CREC[1], ACT.Exp, scale=-1.0).then_inc(s_softexp, 1)
                act.wait_ge(s_soft, 2)
                act.activation(CREC[3], CREC[2], ACT.Ln).then_inc(s_softexp, 1)
                block_of(0)
                with act.Fori(1, NB) as b:
                    block_of(b)

            @block.vector
            def _(dve):
                lam = cols[:, :, ROWS["lru_lambda"]]
                dve.tensor_scalar(CREC[0], lam, -1.0, 0.0, ALU.mult, ALU.max)
                dve.drain()
                dve.scalar_tensor_tensor(CREC[1], CREC[0], 2.0, lam, ALU.mult, ALU.add).then_inc(s_soft, 1)
                for t in range(2):
                    dve.memset(RPAD[t][:, 0:3], 0.0)
                dve.wait_ge(s_softexp, 1)
                dve.tensor_scalar(CREC[2], CREC[1], 1.0, None, ALU.add).then_inc(s_soft, 1)
                dve.drain()
                dve.wait_ge(s_softexp, 2)
                dve.tensor_scalar(CREC[2], CREC[2], -1.0, None, ALU.add)
                dve.drain()
                dve.tensor_scalar(CREC[4], CREC[2], 0.0, None, ALU.is_equal)
                dve.tensor_tensor(CREC[3], CREC[3], CREC[1], ALU.mult)
                dve.drain()
                dve.tensor_tensor(CREC[2], CREC[2], CREC[4], ALU.add)
                dve.tensor_tensor(CREC[4], CREC[4], CREC[1], ALU.mult)
                dve.drain()
                dve.reciprocal(CREC[2], CREC[2])
                dve.drain()
                dve.tensor_tensor(CREC[3], CREC[3], CREC[2], ALU.mult)
                dve.drain()
                dve.tensor_tensor(CREC[3], CREC[3], CREC[4], ALU.add)
                dve.drain()
                dve.tensor_tensor(CREC[0], CREC[0], CREC[3], ALU.add)
                dve.drain()
                dve.tensor_scalar(crec, CREC[0], -8.0, None, ALU.mult)
                dve.drain()
                with dve.Fori(0, NB) as b:
                    for t in range(2):
                        j = 2 * b + t
                        dve.wait_ge(s_revac, 6 * b + t + 1)
                        hold(dve)
                        dve.tensor_scalar(XA[t], RPAD[t][:, 0:T], col("conv_w_2", j, 0), col("conv_b_2", j),
                                          ALU.mult, ALU.add)
                        for k in range(1, 4):
                            dve.drain()
                            last = dve.scalar_tensor_tensor(XA[t], RPAD[t][:, k:k + T], col("conv_w_2", j, k),
                                                            XA[t], ALU.mult, ALU.add)
                        last.then_inc(s_xa, 1)
                    for t in range(2):
                        dve.wait_ge(s_riev, 2 * b + t + 1)
                        hold(dve)
                        dve.tensor_scalar(REC[t], REC[t], crec[:, ds(2 * b + t, 1)], None,
                                          ALU.mult).then_inc(s_la, 1)
                        dve.tensor_tensor(INP[t], INP[t], XA[t], ALU.mult)
                    for t in range(2):
                        dve.wait_ge(s_at, 2 * b + t + 1)
                        dve.tensor_scalar(REC[t], THMUL[t], 1.0, None, ALU.add)
                        dve.drain()
                        dve.reciprocal(REC[t], REC[t])
                        dve.drain()
                        dve.scalar_tensor_tensor(THMUL[t], THMUL[t], 2.0, REC[t], ALU.mult,
                                                 ALU.mult).then_inc(s_mq, 1)
                    for t in range(2):
                        dve.wait_ge(s_mroot, 2 * b + t + 1)
                        dve.tensor_tensor(INP[t], INP[t], THMUL[t], ALU.mult)
                        dve.drain()
                        dve.tensor_tensor_scan(REC[t], AEXP[t], INP[t], 0.0, ALU.mult, ALU.add)
                        dve.drain()
                        dve.wait_ge(s_revac, 6 * b + 5 + t)
                        dve.tensor_tensor(REC[t], REC[t], GELU[t], ALU.mult)
                        dve.drain()
                        dve.tensor_tensor(RA[:, ds(2 * b + t, 1), :].rearrange("p a t -> p (a t)"), REC[t],
                                          SIG[t], ALU.mult).then_inc(s_mt, 1)

        if upto < 6:
            return

        NQ, NKV, NROPE = 768, 256, 32
        QC = part(0, (NT, NQ))
        KVC = part(6 * T, (NT, NKV + NROPE))
        ROPE = part(23 * T + 512, (4, NT, 16))
        COS, SIN, ANG, TURNS = (ROPE[:, k] for k in range(4))
        KPE = part(24 * T, (NT, NROPE))
        GAINS = part(24 * T + 256, (2, 96))
        FREQ = part(24 * T + 448, (16,))
        POSF = part(24 * T + 464, (NT,))
        POSI = sb("POSI", [P, NT], I32)
        WUQ = part(17 * T, (6, 384))
        WUKV = part(19 * T + 256, (2, HALF))
        latss = small[:, 112:128].rearrange("p (u m) -> p u m", u=2)
        latms = small[:, 128:144].rearrange("p (u m) -> p u m", u=2)
        s_pos = sem("s_pos")
        s_wup = sem("s_wup")
        s_lproj = sem("s_lproj")
        s_levac = sem("s_levac")
        s_lss = sem("s_lss")
        s_lms = sem("s_lms")
        s_lroot = sem("s_lroot")
        s_lnorm = sem("s_lnorm")
        s_lturn = sem("s_lturn")
        s_lt = sem("s_lt")
        s_ang = sem("s_ang")
        s_trig = sem("s_trig")

        with nc.Block() as block:
            @block.sync
            def _(sp):
                sp.dma_start(POSI[:], a["positions_2"].rearrange("o (m p) -> p (o m)", p=P)).then_inc(s_pos, 16)
                sp.dma_start(FREQ, a["c_freq"]).then_inc(s_pos, 16)
                for i, name in enumerate(("q_norm_g_2", "k_norm_g_2")):
                    sp.dma_start(GAINS[:, i, :], a[name].to_broadcast([P, 96])).then_inc(s_pos, 16)
                sp.dma_start(WUQ, a["w_uq_2"].rearrange("o (k p) n -> p (o k) n", p=P)[:, :, 0:384]
                             ).then_inc(s_wup, 16)
                sp.dma_start(WUKV, a["w_ukv_2"].rearrange("o (k p) n -> p (o k) n", p=P)[:, :, 0:HALF]
                             ).then_inc(s_wup, 16)

            @block.tensor
            def _(pe):
                pe.wait_ge(s_wqc, 16)
                pe.wait_ge(s_wkv, 16)
                for m in range(NT):
                    if m >= 2:
                        pe.wait_ge(s_levac, m - 1)
                    lhs = RC[:, :, m * P:(m + 1) * P]
                    o = banks(2 * (m % 2))
                    for c0, c1 in ((0, HALF), (HALF, NQ)):
                        for k in range(ND):
                            pe.matmul(o[:, c0:c1], lhs[:, k, :], WQC[:, k, c0:c1], start=(k == 0), stop=(k == ND - 1))
                    for k in range(ND):
                        last = pe.matmul(PS[:, 4 + m % 2, 0:288], lhs[:, k, :], WKV[:, k, :],
                                         start=(k == 0), stop=(k == ND - 1))
                    last.then_inc(s_lproj, 1)
                for m in range(NT):
                    pe.wait_ge(s_lnorm, m + 1)
                    if m >= 2:
                        pe.wait_ge(s_lt, m - 1)
                    o = banks(2 * (m % 2))
                    for c in range(ND):
                        src = QC[:, m, c * P:(c + 1) * P] if c < 6 else KVC[:, m, (c - 6) * P:(c - 5) * P]
                        last = pe.transpose(o[:, c * P:(c + 1) * P], src, ident)
                    last.then_inc(s_lturn, 1)

            @block.scalar
            def _(act):
                for m in range(NT):
                    act.wait_ge(s_lproj, m + 1)
                    o = banks(2 * (m % 2))
                    act.activation(SQUARES[:, 0:NQ], o[:, 0:NQ], ACT.Square, accum_out=latss[:, 0, m:m + 1])
                    act.drain()
                    act.activation(SQUARES[:, 0:NKV], PS[:, 4 + m % 2, 0:NKV], ACT.Square,
                                   accum_out=latss[:, 1, m:m + 1])
                    act.activation(QC[:, m, :], o[:, 0:NQ], ACT.Copy)
                    act.activation(KVC[:, m, :], PS[:, 4 + m % 2, 0:288], ACT.Copy)
                    act.drain()
                    act.nop().then_inc(s_levac, 1)
                act.wait_ge(s_lms, 1)
                act.activation(latms, latms, ACT.Sqrt).then_inc(s_lroot, 1)
                act.wait_ge(s_ang, 1)
                act.activation(SIN, SIN, ACT.Sin)
                act.activation(COS, COS, ACT.Sin)
                act.drain()
                act.nop().then_inc(s_trig, 1)

            @block.vector
            def _(dve):
                dve.wait_ge(s_pos, 64)
                dve.tensor_copy(POSF, POSI[:])
                dve.drain()
                pos = POSF.rearrange("p (m o) -> p m o", o=1).to_broadcast([P, NT, 16])
                freq = FREQ.rearrange("p (o i) -> p o i", o=1).to_broadcast([P, NT, 16])
                dve.tensor_tensor(ANG, pos, freq, ALU.mult)
                dve.drain()
                dve.tensor_scalar(TURNS, ANG, float(1 / (2 * np.pi)), ROUND, ALU.mult, ALU.add)
                dve.drain()
                dve.tensor_scalar(TURNS, TURNS, -ROUND, None, ALU.add)
                dve.drain()
                for c in TWO_PI:
                    dve.scalar_tensor_tensor(ANG, TURNS, -c, ANG, ALU.mult, ALU.add)
                    dve.drain()
                dve.tensor_scalar(COS, ANG, float(np.pi / 2), None, ALU.add)
                dve.drain()
                dve.tensor_scalar(TURNS, COS, float(np.pi), -float(2 * np.pi), ALU.is_gt, ALU.mult)
                dve.drain()
                dve.tensor_tensor(COS, COS, TURNS, ALU.add)
                dve.drain()
                dve.tensor_scalar(SIN, ANG, 3.1415925, -3.1415925, ALU.min, ALU.max)
                dve.tensor_scalar(COS, COS, 3.1415925, -3.1415925, ALU.min, ALU.max)
                dve.drain()
                dve.nop().then_inc(s_ang, 1)

                dve.wait_ge(s_levac, NT)
                dve.tensor_scalar(latms[:, 0], latss[:, 0], 1.0 / NQ, EPS, ALU.mult, ALU.add)
                dve.tensor_scalar(latms[:, 1], latss[:, 1], 1.0 / NKV, EPS, ALU.mult, ALU.add)
                dve.tensor_copy(KPE, KVC[:, :, NKV:NKV + NROPE])
                dve.drain()
                dve.nop().then_inc(s_lms, 1)
                dve.wait_ge(s_lroot, 1)
                dve.reciprocal(latms, latms)
                dve.drain()

                def evacuate(m):
                    dve.wait_ge(s_lturn, m + 1)
                    o = banks(2 * (m % 2)).rearrange("p (c t) -> p c t", c=ND)
                    for c0, c1, name in ((0, 6, "q_a_g"), (6, 8, "kv_a_g")):
                        g = cols[:, 0:c1 - c0, ROWS[name]:ROWS[name] + 1].to_broadcast([P, c1 - c0, P])
                        last = dve.tensor_tensor(RB[:, c0:c1, m * P:(m + 1) * P], o[:, c0:c1, :], g, ALU.mult)
                    dve.drain()
                    dve.nop().then_inc(s_lt, 1)

                for m in range(NT):
                    dve.tensor_scalar(QC[:, m, :], QC[:, m, :], latms[:, 0, m:m + 1], None, ALU.mult)
                    dve.tensor_scalar(KVC[:, m, 0:NKV], KVC[:, m, 0:NKV], latms[:, 1, m:m + 1], None, ALU.mult)
                    dve.drain()
                    dve.nop().then_inc(s_lnorm, 1)
                    if m:
                        evacuate(m - 1)
                evacuate(NT - 1)
        if upto < 7:
            with nc.Block() as block:
                @block.sync
                def _(sp):
                    sp.wait_ge(s_wup, 32)
            return

        NG, GH, NTASK = 4, 4, 4 * NT
        GATE1_COL = GATE0_COL + D
        SCALE = 96 ** -0.5
        QKTOK = part(0, (NT * 2 * GH, 96))
        PROB = [part(k * T, (T,)) for k in range(2)]
        PROBT = [part((2 + k) * T, (NT, P)) for k in range(2)]
        YTOK = part(4 * T, (NT, GH * 64))
        QKSQ = part(6 * T, (2 * GH, 96))
        ROT = [part(7 * T + k * T, (T,)) for k in range(4)]
        QFEAT = part(7 * T, (GH, T))
        KFEAT = part(11 * T, (GH, T))
        VTOK = part(15 * T, (NT, GH, 64))
        WGATE = [part(20 * T + 256 + k * T, (ND, P)) for k in range(2)]
        SIG1 = [part(20 * T + 256 + k * T, (T,)) for k in range(2)]
        headss = small[:, 144:208]
        rowmax = small[:, 208:210]
        rowsum = small[:, 210:212]
        rowrec = small[:, 212:214]

        s_w1 = sem("s_w1")
        s_wup7 = sem("s_wup7")
        s_qkv = sem("s_qkv")
        s_qev = sem("s_qev")
        s_kev = sem("s_kev")
        s_g1 = sem("s_g1")
        s_g1sig = sem("s_g1sig")
        s_qms = sem("s_qms")
        s_qroot = sem("s_qroot")
        s_rot = sem("s_rot")
        s_qkturn = sem("s_qkturn")
        s_qfeat = sem("s_qfeat")
        s_kfeat = sem("s_kfeat")
        s_score = sem("s_score")
        s_max = sem("s_max")
        s_prob = sem("s_prob")
        s_pturn7 = sem("s_pturn7")
        s_probt = sem("s_probt")
        s_pv = sem("s_pv")
        s_y = sem("s_y")
        s_yturn = sem("s_yturn")
        s_merged = sem("s_merged")

        with nc.Block() as block:
            @block.sync
            def _(sp):
                def load_gate(g):
                    for t in range(2):
                        w = a["w_in_2"].rearrange("o (k p) n -> p (o k) n", p=P)
                        sp.dma_start(WGATE[t], w[:, :, ds(g * 256 + GATE1_COL + t * P, P)]).then_inc(s_w1, 16)

                load_gate(0)
                with sp.Fori(1, NG) as g:
                    sp.wait_ge(s_qkv, NT * g)
                    hold(sp)
                    sp.dma_start(WUQ, a["w_uq_2"].rearrange("o (k p) n -> p (o k) n", p=P)[:, :, ds(g * 384, 384)]
                                 ).then_inc(s_wup7, 16)
                    sp.dma_start(WUKV, a["w_ukv_2"].rearrange("o (k p) n -> p (o k) n", p=P)[:, :, ds(g * HALF, HALF)]
                                 ).then_inc(s_wup7, 16)
                    sp.wait_ge(s_merged, g)
                    hold(sp)
                    load_gate(g)

            @block.tensor
            def _(pe):
                def scores(g, n):
                    h, i = n // NT, n % NT
                    if n >= 2:
                        pe.wait_ge(s_prob, NTASK * g + n - 1)
                    o = banks(2 * (n % 2))
                    for c0 in range(0, (i + 1) * P, HALF):
                        c1 = min(c0 + HALF, (i + 1) * P)
                        last = pe.matmul(o[:, c0:c1], QFEAT[0:96, h, i * P:(i + 1) * P], KFEAT[0:96, h, c0:c1],
                                         start=True, stop=True)
                    last.then_inc(s_score, 1)

                def turn(g, n):
                    i = n % NT
                    pe.wait_ge(s_prob, NTASK * g + n + 1)
                    if n:
                        pe.wait_ge(s_probt, NTASK * g + n)
                    for c in range(i + 1):
                        last = pe.transpose(banks(4)[:, c * P:(c + 1) * P], PROB[n % 2][:, c * P:(c + 1) * P], ident)
                    last.then_inc(s_pturn7, 1)

                def values(g, n):
                    h, i = n // NT, n % NT
                    pe.wait_ge(s_probt, NTASK * g + n + 1)
                    if n >= 2:
                        pe.wait_ge(s_y, NTASK * g + n - 1)
                    for c in range(i + 1):
                        last = pe.matmul(PS[:, 6 + n % 2, 0:64], PROBT[n % 2][:, c, :], VTOK[:, c, h, :],
                                         start=(c == 0), stop=(c == i))
                    last.then_inc(s_pv, 1)

                def group(g, first):
                    if first:
                        pe.wait_ge(s_wup, 32)
                    else:
                        pe.wait_ge(s_wup7, 32 * g)
                        pe.wait_ge(s_merged, g)
                    for m in range(NT):
                        if m >= 2:
                            pe.wait_ge(s_qev, NT * g + m - 1)
                            pe.wait_ge(s_kev, NT * g + m - 1)
                        for k in range(6):
                            pe.matmul(PS[:, m % 2, 0:384], RB[:, k, m * P:(m + 1) * P], WUQ[:, k, :],
                                      start=(k == 0), stop=(k == 5))
                        for k in range(2):
                            last = pe.matmul(PS[:, 2 + m % 2, :], RB[:, 6 + k, m * P:(m + 1) * P], WUKV[:, k, :],
                                             start=(k == 0), stop=(k == 1))
                        last.then_inc(s_qkv, 1)
                    pe.wait_ge(s_w1, 32 * g + 32)
                    for t in range(2):
                        for h in range(2):
                            for k in range(ND):
                                last = pe.matmul(banks(4 + 2 * t)[:, h * HALF:(h + 1) * HALF], WGATE[t][:, k, :],
                                                 RC[:, k, h * HALF:(h + 1) * HALF],
                                                 start=(k == 0), stop=(k == ND - 1))
                        last.then_inc(s_g1, 1)
                    pe.wait_ge(s_rot, g + 1)
                    for m in range(NT):
                        if m >= 2:
                            pe.wait_ge(s_qfeat, NT * g + m - 1)
                            pe.wait_ge(s_kfeat, NT * g + m - 1)
                        for u in range(2):
                            for h in range(GH):
                                last = pe.transpose(PS[0:96, 2 * (m % 2) + u, h * P:(h + 1) * P],
                                                    QKTOK[:, (2 * m + u) * GH + h, :], ident)
                        last.then_inc(s_qkturn, 1)
                    pe.wait_ge(s_qfeat, NT * g + NT)
                    pe.wait_ge(s_kfeat, NT * g + NT)
                    pe.wait_ge(s_g1sig, 2 * g + 2)
                    scores(g, 0)
                    for n in range(NTASK):
                        if n + 1 < NTASK:
                            scores(g, n + 1)
                        turn(g, n)
                        if n:
                            values(g, n - 1)
                    values(g, NTASK - 1)
                    pe.wait_ge(s_y, NTASK * g + NTASK)
                    for t in range(2):
                        for m in range(NT):
                            last = pe.transpose(banks(2 * t)[:, m * P:(m + 1) * P],
                                                YTOK[:, m, t * P:(t + 1) * P], ident)
                    last.then_inc(s_yturn, 1)

                group(0, True)
                with pe.Fori(1, NG) as g:
                    group(g, False)

            @block.scalar
            def _(act):
                with act.Fori(0, NG) as g:
                    for m in range(NT):
                        act.wait_ge(s_qkv, NT * g + m + 1)
                        act.activation(QKTOK[:, 2 * m * GH:(2 * m + 1) * GH, :].rearrange("p h d -> p (h d)"),
                                       PS[:, m % 2, 0:384], ACT.Copy).then_inc(s_qev, 1)
                    for t in range(2):
                        act.wait_ge(s_g1, 2 * g + t + 1)
                        act.activation(SIG1[t], banks(4 + 2 * t), ACT.Sigmoid).then_inc(s_g1sig, 1)
                    act.wait_ge(s_qms, g + 1)
                    act.activation(headss, headss, ACT.Sqrt).then_inc(s_qroot, 1)
                    for m in range(NT):
                        act.wait_ge(s_qkturn, NT * g + m + 1)
                        act.activation(QFEAT[0:96, :, m * P:(m + 1) * P],
                                       PS[0:96, 2 * (m % 2), :].rearrange("p (h t) -> p h t", h=GH),
                                       ACT.Copy).then_inc(s_qfeat, 1)
                    for n in range(NTASK):
                        w = (n % NT + 1) * P
                        act.wait_ge(s_max, NTASK * g + n + 1)
                        if n >= 2:
                            act.wait_ge(s_pturn7, NTASK * g + n - 1)
                        act.activation(PROB[n % 2][:, 0:w], banks(2 * (n % 2))[:, 0:w], ACT.Exp, scale=SCALE,
                                       bias=rowmax[:, n % 2:n % 2 + 1], accum_out=rowsum[:, n % 2:n % 2 + 1])
                        act.drain()
                        act.nop().then_inc(s_prob, 1)

            @block.vector
            def _(dve):
                with dve.Fori(0, NG) as g:
                    for m in range(NT):
                        dve.wait_ge(s_qkv, NT * g + m + 1)
                        k = QKTOK[:, (2 * m + 1) * GH:(2 * m + 2) * GH, :]
                        dve.tensor_copy(k[:, :, 0:64],
                                        PS[:, 2 + m % 2, :].rearrange("p (h d) -> p h d", h=GH)[:, :, 0:64])
                        dve.tensor_copy(VTOK[:, m], PS[:, 2 + m % 2, :].rearrange("p (h d) -> p h d", h=GH)[:, :, 64:])
                        dve.tensor_copy(k[:, :, 64:96], KPE[:, m:m + 1, :].to_broadcast([P, GH, NROPE]))
                        dve.drain()
                        dve.nop().then_inc(s_kev, 1)
                    for m in range(NT):
                        dve.wait_ge(s_qev, NT * g + m + 1)
                        qk = QKTOK[:, 2 * m * GH:2 * (m + 1) * GH, :]
                        dve.tensor_tensor(QKSQ, qk, qk, ALU.mult)
                        dve.drain()
                        dve.tensor_reduce(headss[:, 2 * m * GH:2 * (m + 1) * GH], QKSQ, AX.X, ALU.add)
                        dve.drain()
                    dve.tensor_scalar(headss, headss, 1.0 / 96, EPS, ALU.mult, ALU.add).then_inc(s_qms, 1)
                    dve.wait_ge(s_qroot, g + 1)
                    dve.reciprocal(headss, headss)
                    dve.drain()
                    dve.tensor_tensor(QKTOK, QKTOK, headss.rearrange("p (h o) -> p h o", o=1)
                                      .to_broadcast([P, NT * 2 * GH, 96]), ALU.mult)
                    dve.drain()
                    for m in range(NT):
                        for u in range(2):
                            qk = QKTOK[:, (2 * m + u) * GH:(2 * m + u + 1) * GH, :]
                            dve.tensor_tensor(qk, qk, GAINS[:, u:u + 1, :].to_broadcast([P, GH, 96]), ALU.mult)
                    dve.drain()
                    qk = QKTOK.rearrange("p (m h) d -> p m h d", m=NT)
                    x1, x2 = qk[:, :, :, 64:80], qk[:, :, :, 80:96]

                    def table(v):
                        return v.rearrange("p m (o i) -> p m o i", o=1).to_broadcast([P, NT, 2 * GH, 16])

                    r = [v.rearrange("p (m h i) -> p m h i", m=NT, h=2 * GH) for v in ROT]
                    for v, x, c in ((r[0], x1, COS), (r[1], x2, SIN), (r[2], x1, SIN), (r[3], x2, COS)):
                        dve.tensor_tensor(v, x, table(c), ALU.mult)
                    dve.drain()
                    dve.tensor_tensor(x1, r[0], r[1], ALU.subtract)
                    dve.tensor_tensor(x2, r[2], r[3], ALU.add)
                    dve.drain()
                    dve.nop().then_inc(s_rot, 1)
                    for m in range(NT):
                        dve.wait_ge(s_qkturn, NT * g + m + 1)
                        dve.tensor_copy(KFEAT[0:96, :, m * P:(m + 1) * P],
                                        PS[0:96, 2 * (m % 2) + 1, :].rearrange("p (h t) -> p h t", h=GH)
                                        ).then_inc(s_kfeat, 1)

                    def largest(n):
                        w = (n % NT + 1) * P
                        s = banks(2 * (n % 2))
                        dve.wait_ge(s_score, NTASK * g + n + 1)
                        dve.memset(s[0:64, w - 64:w], -1e30)
                        dve.drain()
                        dve.tensor_reduce(rowmax[:, n % 2:n % 2 + 1], s[:, 0:w], AX.X, ALU.max)
                        dve.drain()
                        dve.tensor_scalar(rowmax[:, n % 2:n % 2 + 1], rowmax[:, n % 2:n % 2 + 1], -SCALE, None,
                                          ALU.mult).then_inc(s_max, 1)

                    def normalise(n):
                        h, i = n // NT, n % NT
                        dve.wait_ge(s_pv, NTASK * g + n + 1)
                        dve.tensor_scalar(YTOK[:, i, h * 64:(h + 1) * 64], PS[:, 6 + n % 2, 0:64],
                                          rowrec[:, n % 2:n % 2 + 1], None, ALU.mult).then_inc(s_y, 1)

                    largest(0)
                    for n in range(NTASK):
                        w = (n % NT + 1) * P
                        if n + 1 < NTASK:
                            if n >= 1:
                                dve.wait_ge(s_prob, NTASK * g + n)
                            largest(n + 1)
                        dve.wait_ge(s_pturn7, NTASK * g + n + 1)
                        if n >= 2:
                            dve.wait_ge(s_pv, NTASK * g + n - 1)
                        dve.tensor_copy(PROBT[n % 2].rearrange("p c t -> p (c t)")[:, 0:w],
                                        banks(4)[:, 0:w]).then_inc(s_probt, 1)
                        if n:
                            normalise(n - 1)
                        dve.reciprocal(rowrec[:, n % 2:n % 2 + 1], rowsum[:, n % 2:n % 2 + 1])
                        dve.drain()
                    normalise(NTASK - 1)
                    dve.wait_ge(s_yturn, g + 1)
                    for t in range(2):
                        dve.tensor_tensor(SIG1[t], SIG1[t], banks(2 * t), ALU.mult)
                    dve.drain()
                    for t in range(2):
                        r = RA[:, ds(2 * g + t, 1), :].rearrange("p a t -> p (a t)")
                        last = dve.tensor_tensor(r, r, SIG1[t], ALU.add)
                    last.then_inc(s_merged, 1)
        if upto < 8:
            return

        retire(*s_st, s_held)
        NE, NGRP, EPG = 32, 4, 8
        NBLK = 48
        BIG = 1e30
        xn_dram = nc.dram_tensor("xn_dram", [T, D], F32).ap()
        list_dram = nc.dram_tensor("list_dram", [NBLK * P, 1], I32).ap()
        y_dram = nc.dram_tensor("y_dram", [NBLK * P, D], F32).ap()
        X1ROW = [part(k * T, (T,)) for k in range(2)]
        NORM8 = [part((2 + k) * T, (T,)) for k in range(2)]
        XNT = [part((4 + k) * T, (ND, P)) for k in range(2)]
        FFN_G = part(6 * T, (T,))
        WROUTE = part(7 * T, (ND, NGRP + NE))
        BROUTE = part(7 * T + 288, (NGRP + NE,))
        LOGITS = part(7 * T + 328, (NT, NGRP + NE))
        R = [part(8 * T + 256 * k, (NT, NE)) for k in range(6)]
        PICK = [part(8 * T + 256 * (6 + k), (NT, NE)) for k in range(2)]
        EXPERT = part(10 * T, (NE,))
        BLOCKAT = part(10 * T + 32, (NBLK,))
        SHORT = [part(10 * T + 96 + 8 * k, (NT,)) for k in range(12)]
        CHOSEN = [small[:, 216 + 8 * k:224 + 8 * k] for k in range(2)]
        LISTROW = [part(10 * T + 208 + 8 * k, (NT,)) for k in range(2)]
        ENDS = part(10 * T + 224, (NE,))
        STARTS = part(10 * T + 256, (NE,))
        PADDED = part(10 * T + 288, (NE,))
        OFBLOCK = part(11 * T, (NBLK, NE))
        BLKF = part(13 * T, (NBLK,))
        GGRP = part(13 * T + 64, (NT, NGRP))
        GGRP2 = part(13 * T + 96, (NT, NGRP))
        ONES = sb("ONES", [P, P])
        ROWI = sb("ROWI", [P, 2, NT], I32)
        TOKI = sb("TOKI", [P, NT], I32)
        COUNTI = sb("COUNTI", [P, NE], I32)
        BLKI = sb("BLKI", [P, NBLK], I32)
        LISTI = sb("LISTI", [P, NBLK], I32)

        s_w8 = sem("s_w8")
        s_wr = sem("s_wr")
        s_x1row = [sem(f"s_x1row{k}") for k in range(2)]
        s_h2p = sem("s_h2p")
        s_h2 = sem("s_h2")
        s_xn = sem("s_xn")
        s_xnst = [sem(f"s_xnst{k}") for k in range(2)]
        s_xnturn = sem("s_xnturn")
        s_xnt = sem("s_xnt")
        s_log = sem("s_log")
        s_logev = sem("s_logev")
        s_gsub = sem("s_gsub")
        s_gexp = sem("s_gexp")
        s_pick = sem("s_pick")
        s_rank = sem("s_rank")
        s_rows8 = sem("s_rows8")
        s_zlist = sem("s_zlist")
        s_list = sem("s_list")

        with nc.Block() as block:
            @block.sync
            def _(sp):
                sp.dma_start(RB[:], a["w_out_2"].rearrange("o (k p) n -> p (o k) n", p=P)).then_inc(s_w8, 16)
                sp.dma_start(FFN_G, a["norm_ffn_g_2"].to_broadcast([P, D])).then_inc(s_wr, 16)
                sp.dma_start(WROUTE[:, :, 0:NGRP], a["router_group_w_2"].rearrange("o (k p) n -> p (o k) n", p=P)
                             ).then_inc(s_wr, 16)
                sp.dma_start(WROUTE[:, :, NGRP:], a["router_expert_w_2"].rearrange("o (k p) n -> p (o k) n", p=P)
                             ).then_inc(s_wr, 16)
                sp.dma_start(BROUTE[:, 0:NGRP], a["router_group_b_2"].to_broadcast([P, NGRP])).then_inc(s_wr, 16)
                sp.dma_start(BROUTE[:, NGRP:], a["router_expert_b_2"].to_broadcast([P, NE])).then_inc(s_wr, 16)
                sp.dma_start(EXPERT, a["c_expert"]).then_inc(s_wr, 16)
                sp.dma_start(BLOCKAT, a["c_block"]).then_inc(s_wr, 16)
                sp.dma_start(TOKI[:], a["c_token"]).then_inc(s_wr, 16)
                for m in range(NT):
                    if m >= 2:
                        sp.wait_ge(s_h2, m - 1)
                    sp.dma_start(X1ROW[m % 2], x1_dram[m]).then_inc(s_x1row[m % 2], 16)
                for m in range(NT):
                    sp.wait_ge(s_xn, m + 1)
                    sp.dma_start(xn_dram[m * P:(m + 1) * P, :], NORM8[m % 2]).then_inc(s_xnst[m % 2], 16)
                for k in range(2):
                    sp.wait_ge(s_xnst[k], 8 * NT)

            @block.tensor
            def _(pe):
                pe.wait_ge(s_w8, 16)
                for m in range(NT):
                    if m >= 4:
                        pe.wait_ge(s_h2, m - 3)
                    for h in range(2):
                        for k in range(ND):
                            last = pe.matmul(banks(2 * (m % 4))[:, h * HALF:(h + 1) * HALF],
                                             RA[:, k, m * P:(m + 1) * P], RB[:, k, h * HALF:(h + 1) * HALF],
                                             start=(k == 0), stop=(k == ND - 1))
                    last.then_inc(s_h2p, 1)
                pe.wait_ge(s_h2, NT)
                pe.wait_ge(s_wr, 16 * 8)
                for m in range(NT):
                    pe.wait_ge(s_xn, m + 1)
                    if m >= 2:
                        pe.wait_ge(s_xnt, m - 1)
                    pe_turn(pe, banks(2 * (m % 2)), NORM8[m % 2], s_xnturn)
                    pe.wait_ge(s_xnt, m + 1)
                    if m >= 2:
                        pe.wait_ge(s_logev, m - 1)
                    for k in range(ND):
                        last = pe.matmul(PS[:, 4 + m % 2, 0:NGRP + NE], XNT[m % 2][:, k, :], WROUTE[:, k, :],
                                         start=(k == 0), stop=(k == ND - 1))
                    last.then_inc(s_log, 1)
                pe.wait_ge(s_pick, 1)
                pe.wait_ge(s_zlist, 1)
                for m in range(NT):
                    for e in range(m + 1):
                        pe.matmul(PS[:, 6, m * NE:(m + 1) * NE], before if e == m else ONES[:], R[0][:, e, :],
                                  start=(e == 0), stop=(e == m))
                for e in range(NT):
                    last = pe.matmul(PS[:, 7, 0:NE], ONES[:], R[0][:, e, :], start=(e == 0), stop=(e == NT - 1))
                last.then_inc(s_rank, 1)

            @block.scalar
            def _(act):
                root_mean_square(act, s_h2, 3, RC)
                for m in range(NT):
                    act.wait_ge(s_xnturn, m + 1)
                    if m >= 2:
                        act.wait_ge(s_log, m - 1)
                    act.activation(XNT[m % 2].rearrange("p c t -> p (c t)"), banks(2 * (m % 2)),
                                   ACT.Copy).then_inc(s_xnt, 1)
                for n in range(2):
                    act.wait_ge(s_gsub, n + 1)
                    v = (GGRP, SHORT[4])[n]
                    act.activation(v, v, ACT.Exp).then_inc(s_gexp, 1)

            @block.gpsimd
            def _(pool):
                pool.memset(LISTI[:], 0)
                pool.memset(ONES[:], 1.0).then_inc(s_zlist, 1)
                pool.drain()
                pool.dma_start(list_dram.rearrange("(b p) o -> p (b o)", p=P), LISTI[:]).then_inc(s_list, 16)
                pool.wait_ge(s_rows8, 1)
                pool.wait_ge(s_list, 16)
                pool.wait_ge(s_wr, 16 * 8)
                for u in range(2):
                    for m in range(NT):
                        pool.indirect_dma_start(list_dram, bass.IndirectOffsetOnAxis(ap=ROWI[:, u, m:m + 1], axis=0),
                                                TOKI[:, m:m + 1], None).then_inc(s_list, 16)
                pool.wait_ge(s_list, 16 * (1 + 2 * NT))
                pool.dma_start(LISTI[:], list_dram.rearrange("(b p) o -> p (b o)", p=P)).then_inc(s_list, 16)

            @block.vector
            def _(dve):
                for m in range(NT):
                    dve.wait_ge(s_h2p, m + 1)
                    dve.wait_ge(s_x1row[m % 2], 16 * (m // 2) + 16)
                    dve.tensor_tensor(RC[:, m, :], banks(2 * (m % 4)), X1ROW[m % 2], ALU.add).then_inc(s_h2, 1)
                reciprocal_roots(dve, 3)
                dve.wait_ge(s_wr, 16 * 8)

                def logits(m):
                    dve.wait_ge(s_log, m + 1)
                    dve.tensor_tensor(LOGITS[:, m, :], PS[:, 4 + m % 2, 0:NGRP + NE], BROUTE,
                                      ALU.add).then_inc(s_logev, 1)

                for m in range(NT):
                    if m >= 2:
                        dve.wait_ge(s_xnturn, m - 1)
                        dve.wait_ge(s_xnst[m % 2], 16 * (m // 2))
                    dve.scalar_tensor_tensor(NORM8[m % 2], RC[:, m, :], rstd[:, m:m + 1], FFN_G, ALU.mult,
                                             ALU.mult).then_inc(s_xn, 1)
                    if m:
                        logits(m - 1)
                logits(NT - 1)
                dve.drain()

                def wide(v, n):
                    return v.rearrange("p (m o) -> p m o", o=1).to_broadcast([P, NT, n])

                def narrow(v, n):
                    return v[:, 0:n].rearrange("p (o e) -> p o e", o=1).to_broadcast([P, NT, n])

                def then(*_):
                    dve.drain()

                def first_largest(v, n, top, index, pick, scratch):
                    then(dve.tensor_reduce(top, v, AX.X, ALU.max))
                    then(dve.tensor_tensor(scratch, v, wide(top, n), ALU.not_equal))
                    then(dve.tensor_scalar(scratch, scratch, BIG, None, ALU.mult))
                    then(dve.tensor_tensor(scratch, scratch, narrow(EXPERT, n), ALU.add))
                    then(dve.tensor_reduce(index, scratch, AX.X, ALU.min))
                    then(dve.tensor_tensor(pick, narrow(EXPERT, n), wide(index, n), ALU.is_equal))

                grp, exp = LOGITS[:, :, 0:NGRP], LOGITS[:, :, NGRP:]
                gmax, gidx, ptop, v1, v2, w1, w2, idx = SHORT[0], SHORT[1], SHORT[2], SHORT[3], SHORT[4], *SHORT[5:8]
                first_largest(grp, NGRP, gmax, gidx, GGRP2, GGRP)
                dve.tensor_tensor(GGRP, grp, wide(gmax, NGRP), ALU.subtract).then_inc(s_gsub, 1)
                dve.wait_ge(s_gexp, 1)
                then(dve.tensor_reduce(ptop, GGRP, AX.X, ALU.add))
                then(dve.reciprocal(ptop, ptop))
                oh = GGRP2.rearrange("p m (g o) -> p m g o", o=1).to_broadcast([P, NT, NGRP, EPG])
                e4 = exp.rearrange("p m (g e) -> p m g e", g=NGRP)
                r1 = R[1].rearrange("p m (g e) -> p m g e", g=NGRP)
                r2 = R[2].rearrange("p m (g e) -> p m g e", g=NGRP)
                dve.tensor_tensor(r1, e4, oh, ALU.mult)
                then(dve.tensor_scalar(r2, oh, -1.0, BIG, ALU.add, ALU.mult))
                then(dve.tensor_tensor(R[1], R[1], R[2], ALU.add))
                first_largest(R[1], NE, v1, idx, PICK[0], R[2])
                then(dve.tensor_scalar(R[2], PICK[0], -2 * BIG, None, ALU.mult))
                then(dve.tensor_tensor(R[1], R[1], R[2], ALU.add))
                first_largest(R[1], NE, v2, idx, PICK[1], R[2])
                then(dve.tensor_tensor(R[0], PICK[0], PICK[1], ALU.add))
                dve.nop().then_inc(s_pick, 1)
                dve.tensor_tensor(v2, v2, v1, ALU.subtract).then_inc(s_gsub, 1)
                dve.wait_ge(s_gexp, 2)
                then(dve.tensor_scalar(w1, v2, 1.0, None, ALU.add))
                then(dve.reciprocal(w1, w1))
                then(dve.tensor_tensor(CHOSEN[0], ptop, w1, ALU.mult))
                then(dve.tensor_tensor(CHOSEN[1], CHOSEN[0], v2, ALU.mult))
                dve.wait_ge(s_zlist, 1)
                dve.wait_ge(s_rank, 1)
                then(dve.tensor_scalar(PADDED, PS[:, 7, 0:NE], float(P - 1), None, ALU.add))
                then(dve.tensor_copy(COUNTI[:], PADDED))
                then(dve.tensor_scalar(COUNTI[:], COUNTI[:], 7, 7, ALU.arith_shift_right, ALU.arith_shift_left))
                then(dve.tensor_copy(PADDED, COUNTI[:]))
                then(dve.tensor_tensor_scan(ENDS, ONES[:, 0:NE], PADDED, 0.0, ALU.mult, ALU.add))
                then(dve.tensor_tensor(STARTS, ENDS, PADDED, ALU.subtract))
                then(dve.tensor_tensor(R[3], PS[:, 6, 0:NT * NE].rearrange("p (m e) -> p m e", e=NE),
                                       narrow(STARTS, NE), ALU.add))
                for u in range(2):
                    then(dve.tensor_tensor(R[4], R[3], PICK[u], ALU.mult))
                    then(dve.tensor_reduce(LISTROW[u], R[4], AX.X, ALU.add))
                    then(dve.tensor_copy(ROWI[:, u, :], LISTROW[u]))
                dve.nop().then_inc(s_rows8, 1)
                ends = ENDS.rearrange("p (o e) -> p o e", o=1).to_broadcast([P, NBLK, NE])
                at = BLOCKAT.rearrange("p (b o) -> p b o", o=1).to_broadcast([P, NBLK, NE])
                then(dve.tensor_tensor(OFBLOCK, ends, at, ALU.is_le))
                then(dve.tensor_reduce(BLKF, OFBLOCK, AX.X, ALU.add))
                then(dve.tensor_scalar(BLKF, BLKF, float(NE - 1), None, ALU.min))
                then(dve.tensor_copy(BLKI[:], BLKF))

        if upto < 9:
            with nc.Block() as block:
                @block.sync
                def _(sp):
                    sp.wait_ge(s_list, 16 * (2 + 2 * NT))
            return

        TOKS = [sb(f"TOKS{k}", [P, 1], I32) for k in range(2)]
        EG = [part(k * 6 * T, (ND, 256)) for k in range(2)]
        EU = [part(2 * T + k * 6 * T, (ND, 256)) for k in range(2)]
        ED = [part(4 * T + k * 6 * T, (2, T)) for k in range(2)]
        XG = [part((14 + k) * T, (T,)) for k in range(2)]
        XT = [part((16 + k) * T, (ND, P)) for k in range(2)]
        HB = [part(18 * T + 512 * k, (512,)) for k in range(2)]
        HT = [part(19 * T + 256 * k, (2, P)) for k in range(2)]
        YB = [part((20 + k) * T, (T,)) for k in range(2)]

        s_eland = [sem(f"s_eland{k}") for k in range(2)]
        s_xgath = [sem(f"s_xgath{k}") for k in range(2)]
        s_xgt = sem("s_xgt")
        s_xte = sem("s_xte")
        s_gu = sem("s_gu")
        s_gact = sem("s_gact")
        s_hb = sem("s_hb")
        s_hbt = sem("s_hbt")
        s_hte = sem("s_hte")
        s_down = sem("s_down")
        s_yb = sem("s_yb")
        s_yst = [sem(f"s_yst{k}") for k in range(2)]
        NPAIR = (NBLK + 1) // 2
        wg_t = a["w_gate_2"].rearrange("o e (p k) n -> p (o e) (k n)", k=ND)
        wu_t = a["w_up_2"].rearrange("o e (p k) n -> p (o e) (k n)", k=ND)
        wd_t = a["w_down_2"].rearrange("o e (p k) n -> p (o e) (k n)", k=2)

        with nc.Block() as block:
            @block.sync
            def _(sp):
                def load(b, s):
                    e = sp.value_load(BLKI[0:1, ds(b, 1)], min_val=0, max_val=NE - 1)
                    for dst, src in ((EG, wg_t), (EU, wu_t), (ED, wd_t)):
                        sp.dma_start(dst[s].rearrange("p k n -> p (k n)"),
                                     src[:, ds(e, 1), :].rearrange("p a n -> p (a n)")).then_inc(s_eland[s], 16)

                load(0, 0)
                load(1, 1)
                with sp.Fori(1, NPAIR) as i:
                    for s in range(2):
                        sp.wait_ge(s_down, 2 * i + s - 1)
                        hold(sp)
                        load(2 * i + s, s)

            @block.gpsimd
            def _(pool):
                pool.wait_ge(s_list, 16 * (2 + 2 * NT))

                def gather(b, s):
                    pool.tensor_copy(TOKS[s][:], LISTI[:, ds(b, 1)])
                    pool.drain()
                    pool.indirect_dma_start(XG[s], None, xn_dram,
                                            bass.IndirectOffsetOnAxis(ap=TOKS[s][:], axis=0)
                                            ).then_inc(s_xgath[s], 16)

                gather(0, 0)
                gather(1, 1)
                with pool.Fori(1, NPAIR) as i:
                    for s in range(2):
                        pool.wait_ge(s_xgt, 2 * i + s - 1)
                        hold(pool)
                        gather(2 * i + s, s)

            @block.tensor
            def _(pe):
                def turn(i, s):
                    pe.wait_ge(s_xgath[s], 16 * i + 16)
                    if s or not isinstance(i, int):
                        pe.wait_ge(s_xte, 2 * i + s)
                    x = XG[s].rearrange("p (d k) -> p k d", k=ND)
                    for k in range(ND):
                        last = pe.transpose(banks(0)[:, k * P:(k + 1) * P], x[:, k, :], ident)
                    last.then_inc(s_xgt, 1)

                def expert(i, s):
                    pe.wait_ge(s_eland[s], 48 * i + 48)
                    pe.wait_ge(s_xte, 2 * i + s + 1)
                    for u, w in enumerate((EG[s], EU[s])):
                        for k in range(ND):
                            last = pe.matmul(PS[:, 2 + u, 0:256], XT[s][:, k, :], w[:, k, :],
                                             start=(k == 0), stop=(k == ND - 1))
                    last.then_inc(s_gu, 1)

                def down(i, s):
                    pe.wait_ge(s_hb, 2 * i + s + 1)
                    h = HB[s][:, 0:256].rearrange("p (f k) -> p k f", k=2)
                    for k in range(2):
                        last = pe.transpose(PS[:, 4, k * P:(k + 1) * P], h[:, k, :], ident)
                    last.then_inc(s_hbt, 1)
                    pe.wait_ge(s_hte, 2 * i + s + 1)
                    for h in range(2):
                        for k in range(2):
                            last = pe.matmul(banks(6)[:, h * HALF:(h + 1) * HALF], HT[s][:, k, :],
                                             ED[s][:, k, h * HALF:(h + 1) * HALF], start=(k == 0), stop=(k == 1))
                    last.then_inc(s_down, 1)

                def pair(i):
                    for s in range(2):
                        turn(i, s)
                        expert(i, s)
                        if s or not isinstance(i, int):
                            pe.wait_ge(s_yb, 2 * i + s)
                        down(i, s)

                pair(0)
                with pe.Fori(1, NPAIR) as i:
                    pair(i)

            @block.scalar
            def _(act):
                def pair(i):
                    for s in range(2):
                        b = 2 * i + s
                        act.wait_ge(s_xgt, b + 1)
                        if not isinstance(i, int):
                            act.wait_ge(s_gu, b - 1)
                        act.activation(XT[s].rearrange("p c t -> p (c t)"), banks(0), ACT.Copy).then_inc(s_xte, 1)
                        act.wait_ge(s_gu, b + 1)
                        if not isinstance(i, int):
                            act.wait_ge(s_hb, b - 1)
                        act.activation(HB[s][:, 256:512], PS[:, 2, 0:256], ACT.Silu).then_inc(s_gact, 1)
                        act.wait_ge(s_down, b + 1)
                        if not isinstance(i, int):
                            act.wait_ge(s_yst[s], 16 * i)
                        act.activation(YB[s], banks(6), ACT.Copy).then_inc(s_yb, 1)
                        act.wait_ge(s_yb, b + 1)
                        hold(act)
                        act.dma_start(y_dram[ds(b * P, P), :], YB[s]).then_inc(s_yst[s], 16)

                pair(0)
                with act.Fori(1, NPAIR) as i:
                    pair(i)

            @block.vector
            def _(dve):
                def pair(i):
                    for s in range(2):
                        b = 2 * i + s
                        dve.wait_ge(s_gact, b + 1)
                        if not isinstance(i, int):
                            dve.wait_ge(s_hbt, b - 1)
                        dve.tensor_tensor(HB[s][:, 0:256], HB[s][:, 256:512], PS[:, 3, 0:256],
                                          ALU.mult).then_inc(s_hb, 1)
                        dve.wait_ge(s_hbt, b + 1)
                        dve.tensor_copy(HT[s].rearrange("p k t -> p (k t)"), PS[:, 4, 0:256]).then_inc(s_hte, 1)

                pair(0)
                with dve.Fori(1, NPAIR) as i:
                    pair(i)

        YGATH = [part(k * T, (T,)) for k in range(4)]
        s_yg = [sem(f"s_yg{k}") for k in range(4)]
        s_sum = sem("s_sum")
        s_out = sem("s_out")
        out_rows = out.rearrange("o (m p) d -> p (o m) d", p=P)

        with nc.Block() as block:
            @block.gpsimd
            def _(pool):
                for s in range(2):
                    pool.wait_ge(s_yst[s], 16 * NPAIR)
                for m in range(NT):
                    if m >= 2:
                        pool.wait_ge(s_sum, m - 1)
                    for u in range(2):
                        k = 2 * (m % 2) + u
                        pool.indirect_dma_start(YGATH[k], None, y_dram,
                                                bass.IndirectOffsetOnAxis(ap=ROWI[:, u, m:m + 1], axis=0)
                                                ).then_inc(s_yg[k], 16)

            @block.vector
            def _(dve):
                for m in range(NT):
                    for u in range(2):
                        k = 2 * (m % 2) + u
                        dve.wait_ge(s_yg[k], 16 * (m // 2) + 16)
                        if u:
                            dve.drain()
                        last = dve.scalar_tensor_tensor(RC[:, m, :], YGATH[k], CHOSEN[u][:, m:m + 1], RC[:, m, :],
                                                        ALU.mult, ALU.add)
                    last.then_inc(s_sum, 1)

            @block.sync
            def _(sp):
                for m in range(NT):
                    sp.wait_ge(s_sum, m + 1)
                    sp.dma_start(out_rows[:, m, :], RC[:, m, :]).then_inc(s_out, 16)
                sp.wait_ge(s_out, 16 * NT)


_OUT_SHAPE = (1, T, D)


def kernel(**inputs):
    import concourse.bacc as _bacc
    from concourse.bass_utils import run_bass_kernel_spmd as _run

    nc = _bacc.Bacc("TRN2", target_bir_lowering=False, num_devices=1)
    arrays, aps = {}, {}
    for name, value in {**inputs, **shape_constants()}.items():
        v = np.ascontiguousarray(value)
        arrays[f"in_{name}"] = v
        aps[name] = nc.dram_tensor(f"in_{name}", v.shape, mybir.dt.from_np(v.dtype), kind="ExternalInput").ap()
    out = nc.dram_tensor("out_0", _OUT_SHAPE, F32, kind="ExternalOutput").ap()
    build(nc, aps, out)
    r = _run(nc, [arrays], core_ids=[0])
    return r.results[0]["out_0"]
```

```python
from contextlib import ExitStack

import numpy as np

import concourse.bass as bass
from concourse import mybir
from concourse.bass import ds

ALU = mybir.AluOpType
ACT = mybir.ActivationFunctionType
AX = mybir.AxisListType
F32 = mybir.dt.float32
I32 = mybir.dt.int32
U8 = mybir.dt.uint8

P = 128
T = 1024
D = 1024
NT = T // P
ND = D // P
HALF = 512
CONV_K = 31
LEVELS = 7
EPS = 1e-6
ROUND = 1.5 * 2.0 ** 23
TWO_PI = (6.28125, 0.0019350051879882812, float(2 * np.pi - 6.28125 - 0.0019350051879882812))

ROWS = {"conv_w": 0, "ln_g": 31, "conv_b": 32, "cnorm_g": 33, "cnorm_b": 34, "b_pw2": 35,
        "lb0": 36, "lb1": 37, "onorm_g": 38, "pe_norm_g": 39, "norm_mix_g": 40, "conv_w_2": 41,
        "conv_b_2": 45, "lru_ba": 46, "lru_bx": 47, "lru_lambda": 48, "q_a_g": 49, "kv_a_g": 50}
NROWS = 51


def shape_constants():
    ident = np.eye(P, dtype=np.float32)
    mean = np.full((P, P), 1.0 / P, np.float32)
    before = np.triu(np.ones((P, P), np.float32), 1)
    restart = np.ones((P, T), np.float32)
    restart[:, ::P] = 0.0
    masks = np.zeros((P, LEVELS + 1, P), np.float32)
    s, t = np.meshgrid(np.arange(P), np.arange(P), indexing="ij")
    for level in range(LEVELS):
        size = 1 << level
        masks[:, level] = (s // (2 * size) == t // (2 * size)) & (s // size % 2 == 0) & (t // size % 2 == 1)
    masks[:, LEVELS] = s == t
    half = 16
    freq = (np.float32(10000.0) ** (-np.arange(half, dtype=np.float32) / np.float32(half))).astype(np.float32)
    return {
        "c_square": np.stack([ident, mean, before], axis=1),
        "c_restart": restart,
        "c_masks": masks,
        "c_freq": np.broadcast_to(freq, (P, half)).copy(),
        "c_expert": np.broadcast_to(np.arange(32, dtype=np.float32), (P, 32)).copy(),
        "c_block": np.broadcast_to(np.arange(48, dtype=np.float32) * 128, (P, 48)).copy(),
        "c_token": (np.arange(P)[:, None] + P * np.arange(NT)[None, :]).astype(np.int32),
    }


def build(nc, a, out, dump=None, upto=99):
    ctx = ExitStack()
    with ctx:
        ctx.enter_context(nc.allow_non_contiguous_dma(reason="parameter vectors and small tables"))

        def sb(name, shape, dt=F32):
            return ctx.enter_context(nc.sbuf_tensor(name, shape, dt))

        in_use = []

        def sem(name):
            in_use.append(nc.alloc_semaphore(name))
            return in_use[-1]

        def retire(*kept):
            done = [s for s in in_use if not any(s is k for k in kept)]
            in_use[:] = list(kept)
            nc.clear_and_free_semaphores(done)
            nc.all_engine_barrier()

        PS = ctx.enter_context(nc.psum_tensor("PS", [P, 8, HALF], F32))
        RA = sb("RA", [P, ND, T])
        RB = sb("RB", [P, ND, T])
        RC = sb("RC", [P, ND, T])
        square = sb("square", [P, 3, P])
        ident, mean, before = square[:, 0, :], square[:, 1, :], square[:, 2, :]
        cols = sb("cols", [P, ND, NROWS])
        small = sb("small", [P, 320])
        ARENA = 25 * T
        arena = sb("arena", [P, ARENA])

        def part(at, shape, dt=F32):
            n = int(np.prod(shape))
            v = arena[:, at:at + n]
            if len(shape) == 2:
                v = v.rearrange("p (x y) -> p x y", y=shape[1])
            if len(shape) == 3:
                v = v.rearrange("p (x y z) -> p x y z", y=shape[1], z=shape[2])
            return v

        def banks(b, n=2):
            return PS[:, b:b + n, :].rearrange("p b n -> p (b n)")

        def col(name, j, k=0):
            r = ROWS[name] + k
            return cols[:, ds(j, 1), r:r + 1].rearrange("p a b -> p (a b)")

        s_const = sem("s_const")
        s_rows = sem("s_rows")
        s_x = sem("s_x")
        s_zero = sem("s_zero")
        s_sumsq = sem("s_sumsq")
        s_var = sem("s_var")
        s_root = sem("s_root")
        s_scaled = sem("s_scaled")
        s_turned = sem("s_turned")
        s_ut = sem("s_ut")
        s_params = sem("s_params")
        s_turned_rows = sem("s_turned_rows")
        s_lb = sem("s_lb")
        s_lbexp = sem("s_lbexp")

        rows = part(0, (D,))
        scratch = part(1 * T, (2, D))
        xtile = RB[:, :, :]
        sumsq, meansq, root, rstd = (small[:, 8 * k:8 * k + 8] for k in range(4))
        lbound, lslack, t0, t1 = (small[:, 32 + 8 * k:40 + 8 * k] for k in range(4))

        with nc.Block() as block:
            @block.sync
            def _(sp):
                sp.dma_start(square[:], a["c_square"]).then_inc(s_const, 16)
                sp.dma_start(xtile, a["x"].rearrange("o (m p) d -> p (o m) d", p=P)).then_inc(s_x, 16)
                sp.wait_ge(s_zero, 1)
                for name, r in ROWS.items():
                    src = {"lb0": a["lb_logits"][0:1, :], "lb1": a["lb_logits"][1:2, :],
                           "conv_w": a["conv_w"].rearrange("o k d -> (o k) d"),
                           "conv_w_2": a["conv_w_2"].rearrange("o k d -> (o k) d")}.get(name)
                    if src is None:
                        full = name if name in a else name + "_2"
                        src = a[full]
                    n, w = src.shape
                    sp.dma_start(rows[r:r + n, 0:w], src).then_inc(s_rows, 16)

            @block.scalar
            def _(act):
                act.wait_ge(s_x, 16)
                for m in range(NT):
                    act.activation(scratch[:, m % 2, :], xtile[:, m, :], ACT.Square, accum_out=sumsq[:, m:m + 1])
                    act.drain()
                act.nop().then_inc(s_sumsq, 1)
                act.wait_ge(s_var, 1)
                act.activation(root, meansq, ACT.Sqrt).then_inc(s_root, 1)
                act.wait_ge(s_lb, 1)
                act.activation(t0, t0, ACT.Exp)
                act.activation(t1, t1, ACT.Exp)
                act.drain()
                act.nop().then_inc(s_lbexp, 1)

            @block.vector
            def _(dve):
                dve.memset(rows, 0.0).then_inc(s_zero, 1)
                dve.wait_ge(s_sumsq, 1)
                dve.tensor_scalar(meansq, sumsq, 1.0 / D, EPS, ALU.mult, ALU.add).then_inc(s_var, 1)
                dve.wait_ge(s_root, 1)
                dve.reciprocal(rstd, root)
                dve.drain()
                for m in range(NT):
                    dve.tensor_scalar(xtile[:, m, :], xtile[:, m, :], rstd[:, m:m + 1], None,
                                      ALU.mult).then_inc(s_scaled, 1)
                for j in range(ND):
                    dve.wait_ge(s_turned_rows, j + 1)
                    dve.tensor_copy(cols[:, j, :], PS[:, 4 + j % 4, 0:NROWS]).then_inc(s_params, 1)
                dve.drain()
                for m in range(NT):
                    dve.wait_ge(s_turned, m + 1)
                    dve.tensor_tensor(RA[:, :, m * P:(m + 1) * P],
                                      banks(2 * (m % 2)).rearrange("p (c t) -> p c t", c=ND),
                                      cols[:, :, ROWS["ln_g"]:ROWS["ln_g"] + 1].to_broadcast([P, ND, P]),
                                      ALU.mult).then_inc(s_ut, 1)
                l0, l1 = cols[:, :, ROWS["lb0"]], cols[:, :, ROWS["lb1"]]
                dve.tensor_tensor(t0, l0, l1, ALU.max)
                dve.drain()
                dve.tensor_tensor(t1, l1, t0, ALU.subtract)
                dve.tensor_tensor(t0, l0, t0, ALU.subtract)
                dve.drain()
                dve.nop().then_inc(s_lb, 1)
                dve.wait_ge(s_lbexp, 1)
                dve.tensor_tensor(lslack, t0, t1, ALU.add)
                dve.drain()
                dve.reciprocal(lslack, lslack)
                dve.drain()
                dve.tensor_tensor(lbound, t0, lslack, ALU.mult)
                dve.drain()
                dve.tensor_scalar(lslack, lbound, -1.0, 1.0, ALU.mult, ALU.add)

            @block.tensor
            def _(pe):
                pe.wait_ge(s_const, 16)
                pe.wait_ge(s_rows, 16 * len(ROWS))
                for j in range(ND):
                    if j >= 4:
                        pe.wait_ge(s_params, j - 3)
                    pe.transpose(PS[:, 4 + j % 4, 0:NROWS], rows[0:NROWS, j * P:(j + 1) * P],
                                 ident[0:NROWS, 0:NROWS]).then_inc(s_turned_rows, 1)
                for m in range(NT):
                    pe.wait_ge(s_scaled, m + 1)
                    if m >= 2:
                        pe.wait_ge(s_ut, m - 1)
                    for c in range(ND):
                        last = pe.transpose(banks(2 * (m % 2))[:, c * P:(c + 1) * P],
                                            xtile[:, m, c * P:(c + 1) * P], ident)
                    last.then_inc(s_turned, 1)
        if upto < 1:
            return

        VAL, GLU, FORGET = (part(k * T, (T,)) for k in range(3))
        KEYS, QUERIES, VALUES, GATE_S = ([part((3 + 2 * n + k) * T, (T,)) for k in range(2)] for n in range(4))
        CUM, CUMEXP, QDEC, ACC, SQ = (part(k * T, (T,)) for k in range(11, 16))
        DECAY = [part(k * T, (T,)) for k in (16, 17)]
        QK = [part(k * T, (T,)) for k in (18, 19)]
        WEIGHTS = part(20 * T, (NT, P))
        KDEC = part(21 * T, (NT, P))
        STATE = part(22 * T, (NT, P))
        HOUT = [RC[:, k, :] for k in (0, 1)]
        PAD = RC[:, 2:4, :].rearrange("p a t -> p (a t)")[:, 0:CONV_K - 1 + T]
        RESTART = RC[:, 4, :]
        HSQ = RC[:, 5, :]
        WSLOT = [part(23 * T, (ND, P)), part(24 * T, (ND, P)), RC[:, 6, :].rearrange("p (k n) -> p k n", n=P)]
        yh_dram = nc.dram_tensor("yh_dram", [ND, P, T], F32).ap()
        MASKS = sb("MASKS", [P, LEVELS + 1, P], U8)
        NPROJ = 6
        FIRST_COL = [0, D, 4 * D, 3 * D, 5 * D, 6 * D]

        s_tables = sem("s_tables")
        s_wland = [sem(f"s_wland{k}") for k in range(3)]
        s_proj = sem("s_proj")
        s_evac = sem("s_evac")
        s_used = sem("s_used")
        s_cum = sem("s_cum")
        s_logf = sem("s_logf")
        s_diff = sem("s_diff")
        s_dexp = sem("s_dexp")
        s_qk = sem("s_qk")
        s_aprod = sem("s_aprod")
        s_amask = sem("s_amask")
        s_kd = sem("s_kd")
        s_kdt = sem("s_kdt")
        s_kdec = sem("s_kdec")
        s_dstate = sem("s_dstate")
        s_state = sem("s_state")
        s_o = sem("s_o")
        s_osq = sem("s_osq")
        s_oms = sem("s_oms")
        s_oroot = sem("s_oroot")
        s_ohead = sem("s_ohead")
        s_conv = sem("s_conv")
        s_mu = sem("s_mu")
        s_cent = sem("s_cent")
        s_csq = sem("s_csq")
        s_cvar = sem("s_cvar")
        s_croot = sem("s_croot")
        s_cnorm = sem("s_cnorm")
        s_cout = sem("s_cout")
        s_epsv = sem("s_epsv")
        s_yhst = [sem(f"s_yhst{k}") for k in range(2)]
        s_held = sem("s_held")
        eps = small[:, 64:65]

        def split(v, size):
            return v.rearrange("p (b u s) -> p b u s", u=2, s=size)

        def hold(eng):
            eng.sem_inc(s_held, 1)

        def chunks(v):
            return v.rearrange("p (c t) -> p c t", t=P)

        with nc.Block() as block:
            @block.sync
            def _(sp):
                sp.dma_start(RESTART, a["c_restart"]).then_inc(s_tables, 16)
                sp.dma_start(WEIGHTS, a["c_masks"]).then_inc(s_tables, 16)

                def load(j, s):
                    c0 = FIRST_COL[s]
                    w = a["w_in"].rearrange("o (k p) n -> p (o k) n", p=P)[:, :, ds(j * P + c0, P)]
                    sp.dma_start(WSLOT[s % 3], w).then_inc(s_wland[s % 3], 16)

                for s in range(NPROJ):
                    if s >= 3:
                        sp.wait_ge(s_proj, s - 2)
                    load(0, s)
                with sp.Fori(1, ND) as j:
                    for s in range(NPROJ):
                        sp.wait_ge(s_proj, NPROJ * j + s - 2)
                        hold(sp)
                        load(j, s)

            LOW, HIGH = banks(4), banks(6)
            LEVEL_PAIR = [LOW, HIGH, LOW, HIGH, HIGH, LOW, LOW, HIGH]

            def pe_project(pe, j, s):
                pe.wait_ge(s_wland[s % 3], 32 * j + 16 * (s // 3) + 16)
                if s >= 2 or not (isinstance(j, int) and j == 0):
                    pe.wait_ge(s_evac, NPROJ * j + s - 1)
                w = WSLOT[s % 3]
                o = banks(2 * (s % 2))
                if s == 4:
                    for c in range(NT):
                        for k in range(ND):
                            last = pe.matmul(o[:, c * P:(c + 1) * P], RA[:, k, c * P:(c + 1) * P], w[:, k, :],
                                             start=(k == 0), stop=(k == ND - 1))
                else:
                    for h in range(2):
                        for k in range(ND):
                            last = pe.matmul(o[:, h * HALF:(h + 1) * HALF], w[:, k, :],
                                             RA[:, k, h * HALF:(h + 1) * HALF],
                                             start=(k == 0), stop=(k == ND - 1))
                last.then_inc(s_proj, 1)

            def pe_mean(pe, o, v, s):
                for h in range(2):
                    last = pe.matmul(o[:, h * HALF:(h + 1) * HALF], mean, v[:, h * HALF:(h + 1) * HALF],
                                     start=True, stop=True)
                last.then_inc(s, 1)

            def pe_conv_mean(pe, c):
                pe.wait_ge(s_conv, c + 1)
                pe_mean(pe, LOW, ACC, s_mu)

            def pe_conv_var(pe, c):
                pe.wait_ge(s_csq, c + 1)
                pe_mean(pe, HIGH, SQ, s_cvar)

            def pe_level(pe, i, p, level):
                if level == LEVELS:
                    keys, queries = KEYS[p], QUERIES[p]
                else:
                    pe.wait_ge(s_qk, LEVELS * i + level + 1)
                    keys = queries = QK[level % 2]
                if level == 4:
                    pe.wait_ge(s_amask, (LEVELS + 1) * i + 4)
                elif level >= 2:
                    pe.wait_ge(s_amask, (LEVELS + 1) * i + level - 1 + (level >= 6))
                o = LEVEL_PAIR[level]
                for c in range(NT):
                    last = pe.matmul(o[:, c * P:(c + 1) * P], keys[:, c * P:(c + 1) * P],
                                     queries[:, c * P:(c + 1) * P], start=True, stop=True)
                last.then_inc(s_aprod, 1)

            def pe_head(pe, i, p, conv, fill):
                later = not (isinstance(i, int) and i == 0)
                fill(2)
                if later:
                    pe.wait_ge(s_ohead, i)
                pe_level(pe, i, p, 0)
                fill(3)
                pe_level(pe, i, p, 1)
                pe_level(pe, i, p, 2)
                fill(4)
                pe_level(pe, i, p, 3)
                if conv:
                    pe.wait_ge(s_amask, (LEVELS + 1) * i + 3)
                    pe_conv_mean(pe, i + 1)
                pe_level(pe, i, p, 4)
                fill(5)
                if conv:
                    pe.wait_ge(s_cent, i + 2)
                else:
                    pe.wait_ge(s_amask, (LEVELS + 1) * i + 3)
                pe_level(pe, i, p, 5)
                if conv:
                    pe.wait_ge(s_amask, (LEVELS + 1) * i + 5)
                    pe_conv_var(pe, i + 1)
                pe_level(pe, i, p, 6)
                if conv:
                    pe.wait_ge(s_croot, i + 2)
                else:
                    pe.wait_ge(s_amask, (LEVELS + 1) * i + 5)
                pe_level(pe, i, p, 7)
                fill(6)
                pe.wait_ge(s_amask, (LEVELS + 1) * (i + 1))
                pe.wait_ge(s_kd, i + 1)
                for c in range(NT):
                    last = pe.transpose(LOW[:, c * P:(c + 1) * P], KEYS[p][:, c * P:(c + 1) * P], ident)
                last.then_inc(s_kdt, 1)
                pe.wait_ge(s_kdec, i + 1)
                for c in range(NT):
                    last = pe.matmul(HIGH[:, c * P:(c + 1) * P], KDEC[:, c, :],
                                     VALUES[p][:, c * P:(c + 1) * P], start=True, stop=True)
                last.then_inc(s_dstate, 1)
                fill(7)
                pe.wait_ge(s_state, i + 1)
                for c in range(NT):
                    o = LOW[:, c * P:(c + 1) * P]
                    last = pe.matmul(o, VALUES[p][:, c * P:(c + 1) * P], WEIGHTS[:, c, :], start=True, stop=(c == 0))
                    if c:
                        last = pe.matmul(o, STATE[:, c, :], QDEC[:, c * P:(c + 1) * P], start=False, stop=True)
                last.then_inc(s_o, 1)
                pe.wait_ge(s_osq, i + 1)
                pe_mean(pe, HIGH, HSQ, s_oms)

            def head_loop(eng, body):
                body(0, 0, 2)
                body(1, 1, 2)
                with eng.Fori(1, ND // 2 - 1) as pair:
                    body(2 * pair, 0, 2)
                    body(2 * pair + 1, 1, 2)
                body(ND - 2, 0, 1)
                body(ND - 1, 1, 0)


            @block.tensor
            def _(pe):
                pe.wait_ge(s_tables, 32)
                for s in range(NPROJ):
                    pe_project(pe, 0, s)
                pe_project(pe, 1, 0)
                pe_project(pe, 1, 1)
                pe_conv_mean(pe, 0)
                pe_conv_var(pe, 0)
                pe.wait_ge(s_croot, 1)

                def body(i, p, later):
                    def fill(n):
                        if n // NPROJ < later:
                            pe_project(pe, i + 1 + n // NPROJ, n % NPROJ)
                    pe_head(pe, i, p, later > 0, fill)

                head_loop(pe, body)

            @block.scalar
            def _(act):
                def evacuate(j, s, p):
                    pair = banks(2 * (s % 2))
                    act.wait_ge(s_proj, NPROJ * j + s + 1)
                    later = not (isinstance(j, int) and j == 0)
                    if s == 0:
                        if later:
                            act.wait_ge(s_used, j)
                        act.activation(VAL, pair, ACT.Copy).then_inc(s_evac, 1)
                    if s == 1:
                        act.activation(GLU, pair, ACT.Sigmoid).then_inc(s_evac, 1)
                    if s == 2:
                        if later:
                            act.wait_ge(s_cum, j)
                        act.activation(FORGET, pair, ACT.Sigmoid)
                        act.activation(KEYS[p], pair, ACT.Sigmoid, scale=-1.0).then_inc(s_evac, 1)
                        act.drain()
                        act.activation(FORGET, FORGET, ACT.Ln, scale=lslack[:, ds(j, 1)],
                                       bias=lbound[:, ds(j, 1)]).then_inc(s_logf, 1)
                    if s == 3:
                        act.activation(QUERIES[p], pair, ACT.Silu).then_inc(s_evac, 1)
                    if s == 4:
                        act.activation(VALUES[p], pair, ACT.Copy).then_inc(s_evac, 1)
                    if s == 5:
                        act.activation(GATE_S[p], pair, ACT.Silu).then_inc(s_evac, 1)

                def inverse_root(v, src, done):
                    act.activation(v, src, ACT.Ln, bias=eps)
                    act.drain()
                    act.activation(v, v, ACT.Exp, scale=-0.5).then_inc(done, 1)

                def conv_out(c):
                    act.wait_ge(s_cnorm, c + 1)
                    act.activation(RB[:, ds(c, 1), :].rearrange("p a t -> p (a t)"), ACC, ACT.Silu,
                                   scale=col("cnorm_g", c), bias=col("cnorm_b", c)).then_inc(s_cout, 1)

                def body(i, p, later):
                    def fill(n):
                        if n // NPROJ < later:
                            q = (p + 1 + n // NPROJ) % 2
                            evacuate(i + 1 + n // NPROJ, n % NPROJ, q)

                    def decays(*ns):
                        for n in ns:
                            act.wait_ge(s_diff, (LEVELS + 1) * i + n + 1)
                            act.activation(DECAY[n % 2], DECAY[n % 2], ACT.Exp).then_inc(s_dexp, 1)

                    act.wait_ge(s_cum, i + 1)
                    act.activation(CUMEXP, CUM, ACT.Exp).then_inc(s_dexp, 1)
                    decays(0, 1)
                    fill(2)
                    decays(2)
                    fill(3)
                    decays(3)
                    fill(4)
                    decays(4)
                    if later:
                        act.wait_ge(s_cent, i + 2)
                        act.activation(SQ, ACC, ACT.Square).then_inc(s_csq, 1)
                    decays(5)
                    fill(5)
                    decays(6)
                    if later:
                        act.wait_ge(s_cvar, i + 2)
                        inverse_root(SQ, HIGH, s_croot)
                    decays(7)
                    if later:
                        conv_out(i + 1)
                    fill(6)
                    act.wait_ge(s_kdt, i + 1)
                    act.activation(KDEC.rearrange("p c k -> p (c k)"), LOW, ACT.Copy).then_inc(s_kdec, 1)
                    fill(7)
                    act.wait_ge(s_o, i + 1)
                    act.activation(HSQ, LOW, ACT.Square).then_inc(s_osq, 1)
                    act.wait_ge(s_oms, i + 1)
                    inverse_root(HSQ, HIGH, s_oroot)

                act.wait_ge(s_epsv, 1)
                for s in range(NPROJ):
                    evacuate(0, s, 0)
                evacuate(1, 0, 1)
                evacuate(1, 1, 1)
                act.wait_ge(s_cent, 1)
                act.activation(SQ, ACC, ACT.Square).then_inc(s_csq, 1)
                act.wait_ge(s_cvar, 1)
                inverse_root(SQ, HIGH, s_croot)
                conv_out(0)
                head_loop(act, body)

            @block.gpsimd
            def _(pool):
                def body(i, p, later):
                    pool.wait_ge(s_cum, i + 1)
                    for level in range(LEVELS):
                        size = 1 << level
                        if level >= 2:
                            pool.wait_ge(s_qk, LEVELS * i + level - 1)
                        b, d = split(CUM, size), split(DECAY[level % 2], size)
                        pivot = b[:, :, 0, size - 1:size].to_broadcast([P, T // (2 * size), size])
                        pool.tensor_tensor(d[:, :, 1, :], b[:, :, 1, :], pivot, ALU.subtract)
                        pool.tensor_tensor(d[:, :, 0, :], pivot, b[:, :, 0, :], ALU.subtract).then_inc(s_diff, 1)
                    pool.wait_ge(s_qk, LEVELS * i + LEVELS - 1)
                    b = chunks(CUM)
                    pool.tensor_tensor(chunks(DECAY[LEVELS % 2]), b[:, :, P - 1:P].to_broadcast([P, NT, P]), b,
                                       ALU.subtract).then_inc(s_diff, 1)
                    pool.wait_ge(s_dexp, (LEVELS + 2) * (i + 1))
                    pool.wait_ge(s_aprod, (LEVELS + 1) * (i + 1))
                    pool.tensor_tensor(KEYS[p], KEYS[p], DECAY[LEVELS % 2], ALU.mult).then_inc(s_kd, 1)
                    pool.drain()
                    pool.wait_ge(s_ohead, i + 1)
                    hold(pool)
                    pool.dma_start(yh_dram[ds(i, 1)].rearrange("a p t -> p (a t)"), HOUT[p]).then_inc(s_yhst[p], 16)

                pool.memset(eps, EPS).then_inc(s_epsv, 1)
                head_loop(pool, body)
                for p in range(2):
                    pool.wait_ge(s_yhst[p], 16 * ND // 2)

            @block.vector
            def _(dve):
                def pad(c):
                    dve.drain()
                    dve.wait_ge(s_evac, NPROJ * c + 2)
                    hold(dve)
                    dve.tensor_tensor(PAD[:, CONV_K - 1:], VAL, GLU, ALU.mult).then_inc(s_used, 1)

                def taps(c, first, end):
                    for k in range(first, end):
                        dve.drain()
                        if k == 0:
                            last = dve.tensor_scalar(ACC, PAD[:, 0:T], col("conv_w", c, 0), col("conv_b", c),
                                                     ALU.mult, ALU.add)
                        else:
                            last = dve.scalar_tensor_tensor(ACC, PAD[:, k:k + T], col("conv_w", c, k), ACC,
                                                            ALU.mult, ALU.add)
                    if end == CONV_K:
                        last.then_inc(s_conv, 1)

                def centre(c):
                    dve.wait_ge(s_mu, c + 1)
                    dve.tensor_tensor(ACC, ACC, LOW, ALU.subtract).then_inc(s_cent, 1)

                def norm(c):
                    dve.wait_ge(s_croot, c + 1)
                    dve.tensor_tensor(ACC, ACC, SQ, ALU.mult).then_inc(s_cnorm, 1)

                def body(i, p, later):
                    if later:
                        pad(i + 1)
                    dve.wait_ge(s_evac, NPROJ * i + 4)
                    hold(dve)
                    dve.tensor_scalar(KEYS[p], KEYS[p], lslack[:, ds(i, 1)], None, ALU.mult)
                    dve.wait_ge(s_logf, i + 1)
                    dve.tensor_tensor_scan(CUM, RESTART, FORGET, 0.0, ALU.mult, ALU.add).then_inc(s_cum, 1)
                    if later:
                        dve.wait_ge(s_cout, i + 1)
                        hold(dve)
                        taps(i + 1, 0, 3)
                    dve.wait_ge(s_dexp, (LEVELS + 2) * i + 1)
                    dve.tensor_tensor(QDEC, QUERIES[p], CUMEXP, ALU.mult)
                    dve.drain()

                    def masked(level):
                        dve.drain()
                        dve.wait_ge(s_aprod, (LEVELS + 1) * i + level + 1)
                        hold(dve)
                        dve.copy_predicated(WEIGHTS, MASKS[:, level:level + 1, :].to_broadcast([P, NT, P]),
                                            chunks(LEVEL_PAIR[level])).then_inc(s_amask, 1)

                    for level in range(LEVELS):
                        size = 1 << level
                        dve.wait_ge(s_dexp, (LEVELS + 2) * i + level + 2)
                        if level >= 2:
                            dve.wait_ge(s_aprod, (LEVELS + 1) * i + level - 1)
                        qk, e = split(QK[level % 2], size), split(DECAY[level % 2], size)
                        dve.tensor_tensor(qk[:, :, 1, :], split(QUERIES[p], size)[:, :, 1, :], e[:, :, 1, :], ALU.mult)
                        dve.tensor_tensor(qk[:, :, 0, :], split(KEYS[p], size)[:, :, 0, :], e[:, :, 0, :],
                                          ALU.mult).then_inc(s_qk, 1)
                        if later and level < 4:
                            taps(i + 1, 3 + 7 * level, 10 + 7 * level)
                        if level:
                            masked(level - 1)
                        if later and level == 4:
                            centre(i + 1)
                    masked(LEVELS - 1)
                    if later:
                        norm(i + 1)
                    masked(LEVELS)
                    dve.wait_ge(s_dstate, i + 1)
                    dstate = chunks(HIGH)
                    dve.tensor_copy(STATE[:, 1, :], dstate[:, 0, :])
                    for c in range(1, NT - 1):
                        dve.drain()
                        last = dve.scalar_tensor_tensor(STATE[:, c + 1, :], STATE[:, c, :],
                                                        CUMEXP[:, c * P + P - 1:c * P + P], dstate[:, c, :],
                                                        ALU.mult, ALU.add)
                    last.then_inc(s_state, 1)
                    dve.wait_ge(s_oroot, i + 1)
                    if not (isinstance(i, int) and i < 2):
                        dve.wait_ge(s_yhst[p], 8 * (i - p))
                        hold(dve)
                    dve.tensor_tensor(HOUT[p], LOW, HSQ, ALU.mult)
                    dve.drain()
                    dve.scalar_tensor_tensor(HOUT[p], HOUT[p], col("onorm_g", i), GATE_S[p], ALU.mult,
                                             ALU.mult).then_inc(s_ohead, 1)

                dve.memset(PAD[:, 0:CONV_K - 1], 0.0)
                dve.wait_ge(s_tables, 32)
                dve.tensor_copy(MASKS[:], WEIGHTS)
                dve.drain()
                dve.memset(WEIGHTS, 0.0)
                pad(0)
                taps(0, 0, CONV_K)
                centre(0)
                norm(0)
                head_loop(dve, body)
        if upto < 2:
            return

        CONVOUT = part(0, (ND, T))
        WOUT_A = part(8 * T, (ND, T))
        SILU = [part((16 + k) * T, (T,)) for k in range(2)]
        WPAIR = [part((18 + k) * T, (ND, P)) for k in range(4)]

        s_w2land = [sem(f"s_w2land{k}") for k in range(4)]
        s_proj2 = sem("s_proj2")
        s_silu = sem("s_silu")
        s_cgated = sem("s_cgated")
        s_wouta = sem("s_wouta")
        s_woutb = sem("s_woutb")

        with nc.Block() as block:
            @block.sync
            def _(sp):
                def load(b, n):
                    t = 2 * b + n // 2
                    src = a["w_in"] if n % 2 == 0 else a["w_pw2"]
                    c0 = 2 * D if n % 2 == 0 else 0
                    w = src.rearrange("o (k p) n -> p (o k) n", p=P)[:, :, ds(t * P + c0, P)]
                    sp.dma_start(WPAIR[n], w).then_inc(s_w2land[n], 16)

                for n in range(4):
                    load(0, n)
                sp.dma_start(WOUT_A, a["w_out"].rearrange("o (k p) n -> p (o k) n", p=P)[:, 0:ND, :]
                             ).then_inc(s_wouta, 16)
                sp.dma_start(RC[:], yh_dram.rearrange("j p t -> p j t")).then_inc(s_woutb, 16)
                with sp.Fori(1, ND // 2) as b:
                    for n in range(4):
                        sp.wait_ge(s_proj2, 4 * b + n - 3)
                        hold(sp)
                        load(b, n)

            @block.tensor
            def _(pe):
                def pair(b):
                    for n in range(4):
                        pe.wait_ge(s_w2land[n], 16 * b + 16)
                        if not isinstance(b, int):
                            pe.wait_ge(s_cgated, 2 * b + n // 2 - 1)
                        src = RA if n % 2 == 0 else RB
                        for h in range(2):
                            for k in range(ND):
                                last = pe.matmul(banks(2 * n)[:, h * HALF:(h + 1) * HALF], WPAIR[n][:, k, :],
                                                 src[:, k, h * HALF:(h + 1) * HALF],
                                                 start=(k == 0), stop=(k == ND - 1))
                        last.then_inc(s_proj2, 1)

                pair(0)
                with pe.Fori(1, ND // 2) as b:
                    pair(b)

            @block.scalar
            def _(act):
                def pair(b):
                    for t in range(2):
                        act.wait_ge(s_proj2, 4 * b + 2 * t + 1)
                        if not isinstance(b, int):
                            act.wait_ge(s_cgated, 2 * b + t - 1)
                        act.activation(SILU[t], banks(4 * t), ACT.Silu).then_inc(s_silu, 1)

                pair(0)
                with act.Fori(1, ND // 2) as b:
                    pair(b)

            @block.vector
            def _(dve):
                with dve.Fori(0, ND // 2) as b:
                    for t in range(2):
                        dve.wait_ge(s_silu, 2 * b + t + 1)
                        dve.wait_ge(s_proj2, 4 * b + 2 * t + 2)
                        hold(dve)
                        dve.scalar_tensor_tensor(CONVOUT[:, ds(2 * b + t, 1), :].rearrange("p a t -> p (a t)"),
                                                 banks(4 * t + 2), col("b_pw2", 2 * b + t), SILU[t],
                                                 ALU.add, ALU.mult).then_inc(s_cgated, 1)

        XROW = [part((16 + k) * T, (T,)) for k in range(2)]
        SQUARES = sb("SQUARES", [P, T])
        PTOK = part(18 * T, (NT, 256))
        PFEAT = part(20 * T, (2, T))
        WPP = part(22 * T, (2, T))
        FINAL_G = part(24 * T, (T,))
        s_xrow = [sem(f"s_xrow{k}") for k in range(2)]
        s_hprod = sem("s_hprod")
        s_h = sem("s_h")
        s_ptok = sem("s_ptok")
        s_pturn = sem("s_pturn")
        s_pfeat = sem("s_pfeat")
        s_wpp = sem("s_wpp")
        s_hss = sem("s_hss")
        s_hvar = sem("s_hvar")
        s_hroot = sem("s_hroot")

        with nc.Block() as block:
            @block.sync
            def _(sp):
                sp.dma_start(RB[:], a["w_out"].rearrange("o (k p) n -> p (o k) n", p=P)[:, ND:2 * ND, :]
                             ).then_inc(s_woutb, 16)
                sp.dma_start(PTOK, a["p"].rearrange("l o (m p) d -> p (l o m) d", p=P)).then_inc(s_ptok, 16)
                for m in range(NT):
                    if m >= 2:
                        sp.wait_ge(s_h, m - 1)
                    sp.dma_start(XROW[m % 2], a["x"][0, m * P:(m + 1) * P, :]).then_inc(s_xrow[m % 2], 16)
                sp.dma_start(WPP, a["w_pp"].rearrange("o (k p) n -> p (o k) n", p=P)).then_inc(s_wpp, 16)
                sp.dma_start(FINAL_G, a["final_g"].rearrange("(o d) -> o d", o=1).to_broadcast([P, D])
                             ).then_inc(s_wpp, 16)

            @block.tensor
            def _(pe):
                pe.wait_ge(s_ptok, 16)
                for k in range(2):
                    for m in range(NT):
                        last = pe.transpose(banks(4 + 2 * k)[:, m * P:(m + 1) * P],
                                            PTOK[:, m, k * P:(k + 1) * P], ident)
                last.then_inc(s_pturn, 1)
                pe.wait_ge(s_wouta, 16)
                pe.wait_ge(s_woutb, 32)
                for m in range(NT):
                    if m == 2:
                        pe.wait_ge(s_pfeat, 1)
                    if m >= 4:
                        pe.wait_ge(s_h, m - 3)
                    for h in range(2):
                        for k in range(2 * ND):
                            lhs = CONVOUT if k < ND else RC
                            w = WOUT_A if k < ND else RB
                            last = pe.matmul(banks(2 * (m % 4))[:, h * HALF:(h + 1) * HALF],
                                             lhs[:, k % ND, m * P:(m + 1) * P],
                                             w[:, k % ND, h * HALF:(h + 1) * HALF],
                                             start=(k == 0), stop=(k == 2 * ND - 1))
                    last.then_inc(s_hprod, 1)

            @block.vector
            def _(dve):
                dve.wait_ge(s_pturn, 1)
                for k in range(2):
                    last = dve.tensor_copy(PFEAT[:, k, :], banks(4 + 2 * k))
                last.then_inc(s_pfeat, 1)
                for m in range(NT):
                    dve.wait_ge(s_hprod, m + 1)
                    dve.wait_ge(s_xrow[m % 2], 16 * (m // 2) + 16)
                    dve.tensor_tensor(RA[:, m, :], banks(2 * (m % 4)), XROW[m % 2], ALU.add).then_inc(s_h, 1)
                dve.wait_ge(s_hss, 1)
                dve.tensor_scalar(meansq, sumsq, 1.0 / D, EPS, ALU.mult, ALU.add).then_inc(s_hvar, 1)
                dve.wait_ge(s_hroot, 1)
                dve.reciprocal(rstd, root)

            @block.scalar
            def _(act):
                for m in range(NT):
                    act.wait_ge(s_h, m + 1)
                    act.activation(SQUARES[:], RA[:, m, :], ACT.Square,
                                   accum_out=sumsq[:, m:m + 1])
                    act.drain()
                act.nop().then_inc(s_hss, 1)
                act.wait_ge(s_hvar, 1)
                act.activation(root, meansq, ACT.Sqrt).then_inc(s_hroot, 1)
        if upto < 3:
            return

        retire(s_wpp, s_held)
        x1_dram = nc.dram_tensor("x1_dram", [NT, P, D], F32).ap()
        NORMED = [part((16 + k) * T, (T,)) for k in range(2)]
        GATES = [part((18 + k) * T, (T,)) for k in range(2)]
        WPG = part(8 * T, (ND, T))
        s_wpg = sem("s_wpg")
        s_normed = sem("s_normed")
        s_nturn = sem("s_nturn")
        s_hnt = sem("s_hnt")
        s_gprod = sem("s_gprod")
        s_gsig = sem("s_gsig")
        s_gmul = sem("s_gmul")
        s_h1 = sem("s_h1")
        s_f1 = sem("s_f1")
        s_x1 = sem("s_x1")
        s_st = [sem(f"s_st{k}") for k in range(3)]
        s_u2n = sem("s_u2n")
        s_u2turn = sem("s_u2turn")
        s_u2t = sem("s_u2t")
        s_x1st = sem("s_x1st")

        def root_mean_square(act, ready, n, src=RA):
            for m in range(NT):
                act.wait_ge(ready, m + 1)
                act.activation(SQUARES[:], src[:, m, :], ACT.Square, accum_out=sumsq[:, m:m + 1])
                act.drain()
            act.nop().then_inc(s_st[0], 1)
            act.wait_ge(s_st[1], n)
            act.activation(root, meansq, ACT.Sqrt).then_inc(s_st[2], 1)

        def reciprocal_roots(dve, n):
            dve.wait_ge(s_st[0], n)
            dve.tensor_scalar(meansq, sumsq, 1.0 / D, EPS, ALU.mult, ALU.add).then_inc(s_st[1], 1)
            dve.wait_ge(s_st[2], n)
            dve.reciprocal(rstd, root)
            dve.drain()

        def pe_turn(pe, dst, src, done):
            for c in range(ND):
                last = pe.transpose(dst[:, c * P:(c + 1) * P], src[:, c * P:(c + 1) * P], ident)
            last.then_inc(done, 1)

        def gain_of(name):
            r = ROWS[name]
            return cols[:, :, r:r + 1].to_broadcast([P, ND, P])

        with nc.Block() as block:
            @block.sync
            def _(sp):
                sp.dma_start(WPG, a["w_pg"].rearrange("o (k p) n -> p (o k) n", p=P)).then_inc(s_wpg, 16)
                for m in range(NT):
                    sp.wait_ge(s_x1, m + 1)
                    sp.dma_start(x1_dram[m], RA[:, m, :]).then_inc(s_x1st, 16)
                sp.wait_ge(s_x1st, 16 * NT)

            @block.tensor
            def _(pe):
                for m in range(NT):
                    pe.wait_ge(s_normed, m + 1)
                    if m >= 2:
                        pe.wait_ge(s_hnt, m - 1)
                    pe_turn(pe, banks(2 * (m % 2)), NORMED[m % 2], s_nturn)
                pe.wait_ge(s_hnt, NT)
                pe.wait_ge(s_wpg, 16)
                pe.wait_ge(s_wpp, 32)
                for m in range(NT):
                    if m >= 2:
                        pe.wait_ge(s_gmul, m - 1)
                    for h in range(2):
                        for k in range(2):
                            pe.matmul(banks(4 + 2 * (m % 2))[:, h * HALF:(h + 1) * HALF],
                                      PFEAT[:, k, m * P:(m + 1) * P], WPP[:, k, h * HALF:(h + 1) * HALF],
                                      start=(k == 0), stop=(k == 1))
                    for h in range(2):
                        for k in range(ND):
                            last = pe.matmul(banks(2 * (m % 2))[:, h * HALF:(h + 1) * HALF],
                                             RB[:, k, m * P:(m + 1) * P], WPG[:, k, h * HALF:(h + 1) * HALF],
                                             start=(k == 0), stop=(k == ND - 1))
                    last.then_inc(s_gprod, 1)
                pe.wait_ge(s_gmul, NT)
                for m in range(NT):
                    pe.wait_ge(s_u2n, m + 1)
                    if m >= 2:
                        pe.wait_ge(s_u2t, m - 1)
                    pe_turn(pe, banks(2 * (m % 2)), NORMED[m % 2], s_u2turn)

            @block.scalar
            def _(act):
                for m in range(NT):
                    act.wait_ge(s_gprod, m + 1)
                    if m >= 2:
                        act.wait_ge(s_h1, m - 1)
                    act.activation(GATES[m % 2], banks(2 * (m % 2)), ACT.Sigmoid).then_inc(s_gsig, 1)
                root_mean_square(act, s_h1, 1)
                root_mean_square(act, s_x1, 2)

            @block.vector
            def _(dve):
                def evacuate(m, turned, dst, name, done):
                    dve.wait_ge(turned, m + 1)
                    dve.tensor_tensor(dst[:, :, m * P:(m + 1) * P],
                                      banks(2 * (m % 2)).rearrange("p (c t) -> p c t", c=ND),
                                      gain_of(name), ALU.mult).then_inc(done, 1)

                for m in range(NT):
                    if m >= 2:
                        dve.wait_ge(s_nturn, m - 1)
                    dve.tensor_scalar(NORMED[m % 2], RA[:, m, :], rstd[:, m:m + 1], None,
                                      ALU.mult).then_inc(s_normed, 1)
                    if m:
                        evacuate(m - 1, s_nturn, RB, "pe_norm_g", s_hnt)
                evacuate(NT - 1, s_nturn, RB, "pe_norm_g", s_hnt)
                for m in range(NT):
                    dve.wait_ge(s_gsig, m + 1)
                    g = GATES[m % 2]
                    dve.tensor_tensor(g, g, banks(4 + 2 * (m % 2)), ALU.mult).then_inc(s_gmul, 1)
                    dve.drain()
                    dve.tensor_tensor(RA[:, m, :], RA[:, m, :], g, ALU.add).then_inc(s_h1, 1)
                reciprocal_roots(dve, 1)
                dve.wait_ge(s_wpp, 32)
                for m in range(NT):
                    dve.scalar_tensor_tensor(RA[:, m, :], RA[:, m, :], rstd[:, m:m + 1], FINAL_G,
                                             ALU.mult, ALU.mult).then_inc(s_x1, 1)
                reciprocal_roots(dve, 2)
                for m in range(NT):
                    if m >= 2:
                        dve.wait_ge(s_u2turn, m - 1)
                    dve.tensor_scalar(NORMED[m % 2], RA[:, m, :], rstd[:, m:m + 1], None,
                                      ALU.mult).then_inc(s_u2n, 1)
                    if m:
                        evacuate(m - 1, s_u2turn, RC, "norm_mix_g", s_u2t)
                evacuate(NT - 1, s_u2turn, RC, "norm_mix_g", s_u2t)
        if upto < 5:
            return

        NB = ND // 2
        NBLK = 48
        SURE = 2 * T // P
        y_dram = nc.dram_tensor("y_dram", [NBLK * P, D], F32).ap()
        s_filled = sem("s_filled")
        GATE0_COL = 2 * D + 768 + 256 + 32
        RPAD = [part(k * (T + 4), (T + 4,))[:, 0:T + 3] for k in range(2)]
        REC, INP, AEXP, THMUL, GELU, SIG, XA = ([part((2 + 2 * n + k) * T + 8, (T,)) for k in range(2)]
                                                for n in range(7))
        WREC = [part((16 + k) * T + 8, (ND, P)) for k in range(3)]
        WAX = part(19 * T + 8, (2, 2, 256))
        WQC = RB[:, 0:6, :].rearrange("p k t -> p (k t)").rearrange("p (k n) -> p k n", n=768)
        WKV = part(21 * T, (ND, 288))
        CREC = [small[:, 72 + 8 * k:80 + 8 * k] for k in range(5)]
        crec = CREC[0]
        XCOLS = [0, P, D, D + P, GATE0_COL, GATE0_COL + P]

        s_rland = [sem(f"s_rland{k}") for k in range(3)]
        s_ax = sem("s_ax")
        s_wqc = sem("s_wqc")
        s_wkv = sem("s_wkv")
        s_rproj = sem("s_rproj")
        s_revac = sem("s_revac")
        s_xa = sem("s_xa")
        s_ri = sem("s_ri")
        s_riev = sem("s_riev")
        s_la = sem("s_la")
        s_at = sem("s_at")
        s_mq = sem("s_mq")
        s_mroot = sem("s_mroot")
        s_mt = sem("s_mt")
        s_soft = sem("s_soft")
        s_softexp = sem("s_softexp")

        with nc.Block() as block:
            @block.sync
            def _(sp):
                def load(b, n):
                    w = a["w_in_2"].rearrange("o (k p) n -> p (o k) n", p=P)[:, :, ds(b * 256 + XCOLS[n], P)]
                    sp.dma_start(WREC[n % 3], w).then_inc(s_rland[n % 3], 16)

                def load_gates(b):
                    for i, name in enumerate(("lru_wa_2", "lru_wx_2")):
                        w = a[name].rearrange("o b (k p) n -> p (o b) k n", p=P)[:, ds(b, 1)]
                        sp.dma_start(WAX[:, i], w.rearrange("p a k n -> p (a k) n")).then_inc(s_ax, 16)

                for n in range(6):
                    if n >= 3:
                        sp.wait_ge(s_rproj, n - 2)
                    load(0, n)
                    if n == 5:
                        for r in range(SURE * P, NBLK * P, T):
                            sp.dma_start(y_dram[r:r + T, :], x1_dram.rearrange("m p d -> (m p) d")
                                         ).then_inc(s_filled, 16)
                    if n == 2:
                        load_gates(0)
                w = a["w_in_2"].rearrange("o (k p) n -> p (o k) n", p=P)
                sp.dma_start(WQC, w[:, :, 2 * D:2 * D + 768]).then_inc(s_wqc, 16)
                sp.dma_start(WKV, w[:, :, 2 * D + 768:2 * D + 1056]).then_inc(s_wkv, 16)
                with sp.Fori(1, NB) as b:
                    for n in range(6):
                        sp.wait_ge(s_rproj, 6 * b + n - 2)
                        hold(sp)
                        load(b, n)
                    sp.wait_ge(s_ri, 2 * b)
                    hold(sp)
                    load_gates(b)

            @block.tensor
            def _(pe):
                def project(b, n):
                    pe.wait_ge(s_rland[n % 3], 32 * b + 16 * (n // 3) + 16)
                    if n >= 2 or not isinstance(b, int):
                        pe.wait_ge(s_revac, 6 * b + n - 1)
                    o = banks(2 * (n % 2))
                    for h in range(2):
                        for k in range(ND):
                            last = pe.matmul(o[:, h * HALF:(h + 1) * HALF], WREC[n % 3][:, k, :],
                                             RC[:, k, h * HALF:(h + 1) * HALF], start=(k == 0), stop=(k == ND - 1))
                    last.then_inc(s_rproj, 1)

                def gates(b, t):
                    pe.wait_ge(s_ax, 32 * b + 32)
                    pe.wait_ge(s_xa, 2 * b + 2)
                    if t or not isinstance(b, int):
                        pe.wait_ge(s_riev, 2 * b + t)
                    for i in range(2):
                        for h in range(2):
                            for k in range(2):
                                last = pe.matmul(banks(4 + 2 * i)[:, h * HALF:(h + 1) * HALF],
                                                 WAX[:, i, k, t * P:(t + 1) * P],
                                                 XA[k][:, h * HALF:(h + 1) * HALF], start=(k == 0), stop=(k == 1))
                    last.then_inc(s_ri, 1)

                def block_of(b):
                    for n in range(3):
                        project(b, n)
                    gates(b, 0)
                    project(b, 3)
                    gates(b, 1)
                    project(b, 4)
                    project(b, 5)

                block_of(0)
                with pe.Fori(1, NB) as b:
                    block_of(b)

            @block.scalar
            def _(act):
                def evacuate(b, n):
                    act.wait_ge(s_rproj, 6 * b + n + 1)
                    t, pair, later = n % 2, banks(2 * (n % 2)), not isinstance(b, int)
                    if n < 2:
                        if later:
                            act.wait_ge(s_xa, 2 * b)
                        act.activation(RPAD[t][:, 3:], pair, ACT.Copy).then_inc(s_revac, 1)
                    else:
                        if later:
                            act.wait_ge(s_mt, 2 * b + t - 1)
                        act.activation((GELU if n < 4 else SIG)[t], pair,
                                       ACT.Gelu_apprx_tanh if n < 4 else ACT.Sigmoid).then_inc(s_revac, 1)

                def gates(b, t):
                    act.wait_ge(s_ri, 2 * b + t + 1)
                    if not isinstance(b, int):
                        act.wait_ge(s_mt, 2 * b + t - 1)
                    act.activation(REC[t], banks(4), ACT.Sigmoid, bias=col("lru_ba", 2 * b + t))
                    act.activation(INP[t], banks(6), ACT.Sigmoid, bias=col("lru_bx", 2 * b + t)).then_inc(s_riev, 1)

                def block_of(b):
                    for n in range(3):
                        evacuate(b, n)
                    gates(b, 0)
                    evacuate(b, 3)
                    gates(b, 1)
                    evacuate(b, 4)
                    evacuate(b, 5)
                    for t in range(2):
                        act.wait_ge(s_la, 2 * b + t + 1)
                        act.activation(AEXP[t], REC[t], ACT.Exp)
                        act.activation(THMUL[t], REC[t], ACT.Tanh, scale=-1.0).then_inc(s_at, 1)
                    for t in range(2):
                        act.wait_ge(s_mq, 2 * b + t + 1)
                        act.activation(THMUL[t], THMUL[t], ACT.Sqrt).then_inc(s_mroot, 1)

                act.wait_ge(s_soft, 1)
                act.activation(CREC[1], CREC[1], ACT.Exp, scale=-1.0).then_inc(s_softexp, 1)
                act.wait_ge(s_soft, 2)
                act.activation(CREC[3], CREC[2], ACT.Ln).then_inc(s_softexp, 1)
                block_of(0)
                with act.Fori(1, NB) as b:
                    block_of(b)

            @block.vector
            def _(dve):
                lam = cols[:, :, ROWS["lru_lambda"]]
                dve.tensor_scalar(CREC[0], lam, -1.0, 0.0, ALU.mult, ALU.max)
                dve.drain()
                dve.scalar_tensor_tensor(CREC[1], CREC[0], 2.0, lam, ALU.mult, ALU.add).then_inc(s_soft, 1)
                for t in range(2):
                    dve.memset(RPAD[t][:, 0:3], 0.0)
                dve.wait_ge(s_softexp, 1)
                dve.tensor_scalar(CREC[2], CREC[1], 1.0, None, ALU.add).then_inc(s_soft, 1)
                dve.drain()
                dve.wait_ge(s_softexp, 2)
                dve.tensor_scalar(CREC[2], CREC[2], -1.0, None, ALU.add)
                dve.drain()
                dve.tensor_scalar(CREC[4], CREC[2], 0.0, None, ALU.is_equal)
                dve.tensor_tensor(CREC[3], CREC[3], CREC[1], ALU.mult)
                dve.drain()
                dve.tensor_tensor(CREC[2], CREC[2], CREC[4], ALU.add)
                dve.tensor_tensor(CREC[4], CREC[4], CREC[1], ALU.mult)
                dve.drain()
                dve.reciprocal(CREC[2], CREC[2])
                dve.drain()
                dve.tensor_tensor(CREC[3], CREC[3], CREC[2], ALU.mult)
                dve.drain()
                dve.tensor_tensor(CREC[3], CREC[3], CREC[4], ALU.add)
                dve.drain()
                dve.tensor_tensor(CREC[0], CREC[0], CREC[3], ALU.add)
                dve.drain()
                dve.tensor_scalar(crec, CREC[0], -8.0, None, ALU.mult)
                dve.drain()
                with dve.Fori(0, NB) as b:
                    for t in range(2):
                        j = 2 * b + t
                        dve.wait_ge(s_revac, 6 * b + t + 1)
                        hold(dve)
                        dve.tensor_scalar(XA[t], RPAD[t][:, 0:T], col("conv_w_2", j, 0), col("conv_b_2", j),
                                          ALU.mult, ALU.add)
                        for k in range(1, 4):
                            dve.drain()
                            last = dve.scalar_tensor_tensor(XA[t], RPAD[t][:, k:k + T], col("conv_w_2", j, k),
                                                            XA[t], ALU.mult, ALU.add)
                        last.then_inc(s_xa, 1)
                    for t in range(2):
                        dve.wait_ge(s_riev, 2 * b + t + 1)
                        hold(dve)
                        dve.tensor_scalar(REC[t], REC[t], crec[:, ds(2 * b + t, 1)], None,
                                          ALU.mult).then_inc(s_la, 1)
                        dve.tensor_tensor(INP[t], INP[t], XA[t], ALU.mult)
                    for t in range(2):
                        dve.wait_ge(s_at, 2 * b + t + 1)
                        dve.tensor_scalar(REC[t], THMUL[t], 1.0, None, ALU.add)
                        dve.drain()
                        dve.reciprocal(REC[t], REC[t])
                        dve.drain()
                        dve.scalar_tensor_tensor(THMUL[t], THMUL[t], 2.0, REC[t], ALU.mult,
                                                 ALU.mult).then_inc(s_mq, 1)
                    for t in range(2):
                        dve.wait_ge(s_mroot, 2 * b + t + 1)
                        dve.tensor_tensor(INP[t], INP[t], THMUL[t], ALU.mult)
                        dve.drain()
                        dve.tensor_tensor_scan(REC[t], AEXP[t], INP[t], 0.0, ALU.mult, ALU.add)
                        dve.drain()
                        dve.wait_ge(s_revac, 6 * b + 5 + t)
                        dve.tensor_tensor(REC[t], REC[t], GELU[t], ALU.mult)
                        dve.drain()
                        dve.tensor_tensor(RA[:, ds(2 * b + t, 1), :].rearrange("p a t -> p (a t)"), REC[t],
                                          SIG[t], ALU.mult).then_inc(s_mt, 1)

        if upto < 6:
            return

        NQ, NKV, NROPE = 768, 256, 32
        QC = part(0, (NT, NQ))
        KVC = part(6 * T, (NT, NKV + NROPE))
        ROPE = part(23 * T + 512, (4, NT, 16))
        COS, SIN, ANG, TURNS = (ROPE[:, k] for k in range(4))
        KPE = part(24 * T, (NT, NROPE))
        GAINS = part(24 * T + 256, (2, 96))
        FREQ = part(24 * T + 448, (16,))
        POSF = part(24 * T + 464, (NT,))
        POSI = sb("POSI", [P, NT], I32)
        WUQ = part(17 * T, (6, 384))
        WUKV = part(19 * T + 256, (2, HALF))
        latss = small[:, 112:128].rearrange("p (u m) -> p u m", u=2)
        latms = small[:, 128:144].rearrange("p (u m) -> p u m", u=2)
        s_pos = sem("s_pos")
        s_wup = sem("s_wup")
        s_lproj = sem("s_lproj")
        s_levac = sem("s_levac")
        s_lss = sem("s_lss")
        s_lms = sem("s_lms")
        s_lroot = sem("s_lroot")
        s_lnorm = sem("s_lnorm")
        s_lturn = sem("s_lturn")
        s_lt = sem("s_lt")
        s_ang = sem("s_ang")
        s_trig = sem("s_trig")

        with nc.Block() as block:
            @block.sync
            def _(sp):
                sp.dma_start(POSI[:], a["positions_2"].rearrange("o (m p) -> p (o m)", p=P)).then_inc(s_pos, 16)
                sp.dma_start(FREQ, a["c_freq"]).then_inc(s_pos, 16)
                for i, name in enumerate(("q_norm_g_2", "k_norm_g_2")):
                    sp.dma_start(GAINS[:, i, :], a[name].to_broadcast([P, 96])).then_inc(s_pos, 16)
                sp.dma_start(WUQ, a["w_uq_2"].rearrange("o (k p) n -> p (o k) n", p=P)[:, :, 0:384]
                             ).then_inc(s_wup, 16)
                sp.dma_start(WUKV, a["w_ukv_2"].rearrange("o (k p) n -> p (o k) n", p=P)[:, :, 0:HALF]
                             ).then_inc(s_wup, 16)

            @block.tensor
            def _(pe):
                pe.wait_ge(s_wqc, 16)
                pe.wait_ge(s_wkv, 16)
                for m in range(NT):
                    if m >= 2:
                        pe.wait_ge(s_levac, m - 1)
                    lhs = RC[:, :, m * P:(m + 1) * P]
                    o = banks(2 * (m % 2))
                    for c0, c1 in ((0, HALF), (HALF, NQ)):
                        for k in range(ND):
                            pe.matmul(o[:, c0:c1], lhs[:, k, :], WQC[:, k, c0:c1], start=(k == 0), stop=(k == ND - 1))
                    for k in range(ND):
                        last = pe.matmul(PS[:, 4 + m % 2, 0:288], lhs[:, k, :], WKV[:, k, :],
                                         start=(k == 0), stop=(k == ND - 1))
                    last.then_inc(s_lproj, 1)
                for m in range(NT):
                    pe.wait_ge(s_lnorm, m + 1)
                    if m >= 2:
                        pe.wait_ge(s_lt, m - 1)
                    o = banks(2 * (m % 2))
                    for c in range(ND):
                        src = QC[:, m, c * P:(c + 1) * P] if c < 6 else KVC[:, m, (c - 6) * P:(c - 5) * P]
                        last = pe.transpose(o[:, c * P:(c + 1) * P], src, ident)
                    last.then_inc(s_lturn, 1)

            @block.scalar
            def _(act):
                for m in range(NT):
                    act.wait_ge(s_lproj, m + 1)
                    o = banks(2 * (m % 2))
                    act.activation(SQUARES[:, 0:NQ], o[:, 0:NQ], ACT.Square, accum_out=latss[:, 0, m:m + 1])
                    act.drain()
                    act.activation(SQUARES[:, 0:NKV], PS[:, 4 + m % 2, 0:NKV], ACT.Square,
                                   accum_out=latss[:, 1, m:m + 1])
                    act.activation(QC[:, m, :], o[:, 0:NQ], ACT.Copy)
                    act.activation(KVC[:, m, :], PS[:, 4 + m % 2, 0:288], ACT.Copy)
                    act.drain()
                    act.nop().then_inc(s_levac, 1)
                act.wait_ge(s_lms, 1)
                act.activation(latms, latms, ACT.Sqrt).then_inc(s_lroot, 1)
                act.wait_ge(s_ang, 1)
                act.activation(SIN, SIN, ACT.Sin)
                act.activation(COS, COS, ACT.Sin)
                act.drain()
                act.nop().then_inc(s_trig, 1)

            @block.vector
            def _(dve):
                dve.wait_ge(s_pos, 64)
                dve.tensor_copy(POSF, POSI[:])
                dve.drain()
                pos = POSF.rearrange("p (m o) -> p m o", o=1).to_broadcast([P, NT, 16])
                freq = FREQ.rearrange("p (o i) -> p o i", o=1).to_broadcast([P, NT, 16])
                dve.tensor_tensor(ANG, pos, freq, ALU.mult)
                dve.drain()
                dve.tensor_scalar(TURNS, ANG, float(1 / (2 * np.pi)), ROUND, ALU.mult, ALU.add)
                dve.drain()
                dve.tensor_scalar(TURNS, TURNS, -ROUND, None, ALU.add)
                dve.drain()
                for c in TWO_PI:
                    dve.scalar_tensor_tensor(ANG, TURNS, -c, ANG, ALU.mult, ALU.add)
                    dve.drain()
                dve.tensor_scalar(COS, ANG, float(np.pi / 2), None, ALU.add)
                dve.drain()
                dve.tensor_scalar(TURNS, COS, float(np.pi), -float(2 * np.pi), ALU.is_gt, ALU.mult)
                dve.drain()
                dve.tensor_tensor(COS, COS, TURNS, ALU.add)
                dve.drain()
                dve.tensor_scalar(SIN, ANG, 3.1415925, -3.1415925, ALU.min, ALU.max)
                dve.tensor_scalar(COS, COS, 3.1415925, -3.1415925, ALU.min, ALU.max)
                dve.drain()
                dve.nop().then_inc(s_ang, 1)

                dve.wait_ge(s_levac, NT)
                dve.tensor_scalar(latms[:, 0], latss[:, 0], 1.0 / NQ, EPS, ALU.mult, ALU.add)
                dve.tensor_scalar(latms[:, 1], latss[:, 1], 1.0 / NKV, EPS, ALU.mult, ALU.add)
                dve.tensor_copy(KPE, KVC[:, :, NKV:NKV + NROPE])
                dve.drain()
                dve.nop().then_inc(s_lms, 1)
                dve.wait_ge(s_lroot, 1)
                dve.reciprocal(latms, latms)
                dve.drain()

                def evacuate(m):
                    dve.wait_ge(s_lturn, m + 1)
                    o = banks(2 * (m % 2)).rearrange("p (c t) -> p c t", c=ND)
                    for c0, c1, name in ((0, 6, "q_a_g"), (6, 8, "kv_a_g")):
                        g = cols[:, 0:c1 - c0, ROWS[name]:ROWS[name] + 1].to_broadcast([P, c1 - c0, P])
                        last = dve.tensor_tensor(RB[:, c0:c1, m * P:(m + 1) * P], o[:, c0:c1, :], g, ALU.mult)
                    dve.drain()
                    dve.nop().then_inc(s_lt, 1)

                for m in range(NT):
                    dve.tensor_scalar(QC[:, m, :], QC[:, m, :], latms[:, 0, m:m + 1], None, ALU.mult)
                    dve.tensor_scalar(KVC[:, m, 0:NKV], KVC[:, m, 0:NKV], latms[:, 1, m:m + 1], None, ALU.mult)
                    dve.drain()
                    dve.nop().then_inc(s_lnorm, 1)
                    if m:
                        evacuate(m - 1)
                evacuate(NT - 1)
        if upto < 7:
            with nc.Block() as block:
                @block.sync
                def _(sp):
                    sp.wait_ge(s_wup, 32)
            return

        NG, GH, NTASK = 4, 4, 4 * NT
        GATE1_COL = GATE0_COL + D
        SCALE = 96 ** -0.5
        QKTOK = part(0, (NT * 2 * GH, 96))
        PROB = [part(k * T, (T,)) for k in range(2)]
        PROBT = [part((2 + k) * T, (NT, P)) for k in range(2)]
        YTOK = part(4 * T, (NT, GH * 64))
        QKSQ = part(6 * T, (2 * GH, 96))
        ROT = [part(7 * T + k * T, (T,)) for k in range(4)]
        QFEAT = part(7 * T, (GH, T))
        KFEAT = part(11 * T, (GH, T))
        VTOK = part(15 * T, (NT, GH, 64))
        WGATE = [part(20 * T + 256 + k * T, (ND, P)) for k in range(2)]
        SIG1 = [part(20 * T + 256 + k * T, (T,)) for k in range(2)]
        headss = small[:, 144:208]
        rowmax = small[:, 208:210]
        rowsum = small[:, 210:212]
        rowrec = small[:, 212:214]

        s_w1 = sem("s_w1")
        s_wup7 = sem("s_wup7")
        s_qkv = sem("s_qkv")
        s_qev = sem("s_qev")
        s_kev = sem("s_kev")
        s_g1 = sem("s_g1")
        s_g1sig = sem("s_g1sig")
        s_qms = sem("s_qms")
        s_qroot = sem("s_qroot")
        s_rot = sem("s_rot")
        s_qkturn = sem("s_qkturn")
        s_qfeat = sem("s_qfeat")
        s_kfeat = sem("s_kfeat")
        s_score = sem("s_score")
        s_max = sem("s_max")
        s_prob = sem("s_prob")
        s_pturn7 = sem("s_pturn7")
        s_probt = sem("s_probt")
        s_pv = sem("s_pv")
        s_y = sem("s_y")
        s_yturn = sem("s_yturn")
        s_merged = sem("s_merged")

        with nc.Block() as block:
            @block.sync
            def _(sp):
                def load_gate(g):
                    for t in range(2):
                        w = a["w_in_2"].rearrange("o (k p) n -> p (o k) n", p=P)
                        sp.dma_start(WGATE[t], w[:, :, ds(g * 256 + GATE1_COL + t * P, P)]).then_inc(s_w1, 16)

                load_gate(0)
                with sp.Fori(1, NG) as g:
                    sp.wait_ge(s_qkv, NT * g)
                    hold(sp)
                    sp.dma_start(WUQ, a["w_uq_2"].rearrange("o (k p) n -> p (o k) n", p=P)[:, :, ds(g * 384, 384)]
                                 ).then_inc(s_wup7, 16)
                    sp.dma_start(WUKV, a["w_ukv_2"].rearrange("o (k p) n -> p (o k) n", p=P)[:, :, ds(g * HALF, HALF)]
                                 ).then_inc(s_wup7, 16)
                    sp.wait_ge(s_merged, g)
                    hold(sp)
                    load_gate(g)
                sp.wait_ge(s_filled, 16 * (NBLK - SURE) * P // T)

            @block.tensor
            def _(pe):
                def scores(g, n):
                    h, i = n // NT, n % NT
                    if n >= 2:
                        pe.wait_ge(s_prob, NTASK * g + n - 1)
                    o = banks(2 * (n % 2))
                    for c0 in range(0, (i + 1) * P, HALF):
                        c1 = min(c0 + HALF, (i + 1) * P)
                        last = pe.matmul(o[:, c0:c1], QFEAT[0:96, h, i * P:(i + 1) * P], KFEAT[0:96, h, c0:c1],
                                         start=True, stop=True)
                    last.then_inc(s_score, 1)

                def turn(g, n):
                    i = n % NT
                    pe.wait_ge(s_prob, NTASK * g + n + 1)
                    if n:
                        pe.wait_ge(s_probt, NTASK * g + n)
                    for c in range(i + 1):
                        last = pe.transpose(banks(4)[:, c * P:(c + 1) * P], PROB[n % 2][:, c * P:(c + 1) * P], ident)
                    last.then_inc(s_pturn7, 1)

                def values(g, n):
                    h, i = n // NT, n % NT
                    pe.wait_ge(s_probt, NTASK * g + n + 1)
                    if n >= 2:
                        pe.wait_ge(s_y, NTASK * g + n - 1)
                    for c in range(i + 1):
                        last = pe.matmul(PS[:, 6 + n % 2, 0:64], PROBT[n % 2][:, c, :], VTOK[:, c, h, :],
                                         start=(c == 0), stop=(c == i))
                    last.then_inc(s_pv, 1)

                def group(g, first):
                    if first:
                        pe.wait_ge(s_wup, 32)
                    else:
                        pe.wait_ge(s_wup7, 32 * g)
                        pe.wait_ge(s_merged, g)
                    for m in range(NT):
                        if m >= 2:
                            pe.wait_ge(s_qev, NT * g + m - 1)
                            pe.wait_ge(s_kev, NT * g + m - 1)
                        for k in range(6):
                            pe.matmul(PS[:, m % 2, 0:384], RB[:, k, m * P:(m + 1) * P], WUQ[:, k, :],
                                      start=(k == 0), stop=(k == 5))
                        for k in range(2):
                            last = pe.matmul(PS[:, 2 + m % 2, :], RB[:, 6 + k, m * P:(m + 1) * P], WUKV[:, k, :],
                                             start=(k == 0), stop=(k == 1))
                        last.then_inc(s_qkv, 1)
                    pe.wait_ge(s_w1, 32 * g + 32)
                    for t in range(2):
                        for h in range(2):
                            for k in range(ND):
                                last = pe.matmul(banks(4 + 2 * t)[:, h * HALF:(h + 1) * HALF], WGATE[t][:, k, :],
                                                 RC[:, k, h * HALF:(h + 1) * HALF],
                                                 start=(k == 0), stop=(k == ND - 1))
                        last.then_inc(s_g1, 1)
                    pe.wait_ge(s_rot, g + 1)
                    for m in range(NT):
                        if m >= 2:
                            pe.wait_ge(s_qfeat, NT * g + m - 1)
                            pe.wait_ge(s_kfeat, NT * g + m - 1)
                        for u in range(2):
                            for h in range(GH):
                                last = pe.transpose(PS[0:96, 2 * (m % 2) + u, h * P:(h + 1) * P],
                                                    QKTOK[:, (2 * m + u) * GH + h, :], ident)
                        last.then_inc(s_qkturn, 1)
                    pe.wait_ge(s_qfeat, NT * g + NT)
                    pe.wait_ge(s_kfeat, NT * g + NT)
                    pe.wait_ge(s_g1sig, 2 * g + 2)
                    scores(g, 0)
                    for n in range(NTASK):
                        if n + 1 < NTASK:
                            scores(g, n + 1)
                        turn(g, n)
                        if n:
                            values(g, n - 1)
                    values(g, NTASK - 1)
                    pe.wait_ge(s_y, NTASK * g + NTASK)
                    for t in range(2):
                        for m in range(NT):
                            last = pe.transpose(banks(2 * t)[:, m * P:(m + 1) * P],
                                                YTOK[:, m, t * P:(t + 1) * P], ident)
                    last.then_inc(s_yturn, 1)

                group(0, True)
                with pe.Fori(1, NG) as g:
                    group(g, False)

            @block.scalar
            def _(act):
                with act.Fori(0, NG) as g:
                    for m in range(NT):
                        act.wait_ge(s_qkv, NT * g + m + 1)
                        act.activation(QKTOK[:, 2 * m * GH:(2 * m + 1) * GH, :].rearrange("p h d -> p (h d)"),
                                       PS[:, m % 2, 0:384], ACT.Copy).then_inc(s_qev, 1)
                    for t in range(2):
                        act.wait_ge(s_g1, 2 * g + t + 1)
                        act.activation(SIG1[t], banks(4 + 2 * t), ACT.Sigmoid).then_inc(s_g1sig, 1)
                    act.wait_ge(s_qms, g + 1)
                    act.activation(headss, headss, ACT.Sqrt).then_inc(s_qroot, 1)
                    for m in range(NT):
                        act.wait_ge(s_qkturn, NT * g + m + 1)
                        act.activation(QFEAT[0:96, :, m * P:(m + 1) * P],
                                       PS[0:96, 2 * (m % 2), :].rearrange("p (h t) -> p h t", h=GH),
                                       ACT.Copy).then_inc(s_qfeat, 1)
                    for n in range(NTASK):
                        w = (n % NT + 1) * P
                        act.wait_ge(s_max, NTASK * g + n + 1)
                        if n >= 2:
                            act.wait_ge(s_pturn7, NTASK * g + n - 1)
                        act.activation(PROB[n % 2][:, 0:w], banks(2 * (n % 2))[:, 0:w], ACT.Exp, scale=SCALE,
                                       bias=rowmax[:, n % 2:n % 2 + 1], accum_out=rowsum[:, n % 2:n % 2 + 1])
                        act.drain()
                        act.nop().then_inc(s_prob, 1)

            @block.vector
            def _(dve):
                with dve.Fori(0, NG) as g:
                    for m in range(NT):
                        dve.wait_ge(s_qkv, NT * g + m + 1)
                        k = QKTOK[:, (2 * m + 1) * GH:(2 * m + 2) * GH, :]
                        dve.tensor_copy(k[:, :, 0:64],
                                        PS[:, 2 + m % 2, :].rearrange("p (h d) -> p h d", h=GH)[:, :, 0:64])
                        dve.tensor_copy(VTOK[:, m], PS[:, 2 + m % 2, :].rearrange("p (h d) -> p h d", h=GH)[:, :, 64:])
                        dve.tensor_copy(k[:, :, 64:96], KPE[:, m:m + 1, :].to_broadcast([P, GH, NROPE]))
                        dve.drain()
                        dve.nop().then_inc(s_kev, 1)
                    for m in range(NT):
                        dve.wait_ge(s_qev, NT * g + m + 1)
                        qk = QKTOK[:, 2 * m * GH:2 * (m + 1) * GH, :]
                        dve.tensor_tensor(QKSQ, qk, qk, ALU.mult)
                        dve.drain()
                        dve.tensor_reduce(headss[:, 2 * m * GH:2 * (m + 1) * GH], QKSQ, AX.X, ALU.add)
                        dve.drain()
                    dve.tensor_scalar(headss, headss, 1.0 / 96, EPS, ALU.mult, ALU.add).then_inc(s_qms, 1)
                    dve.wait_ge(s_qroot, g + 1)
                    dve.reciprocal(headss, headss)
                    dve.drain()
                    dve.tensor_tensor(QKTOK, QKTOK, headss.rearrange("p (h o) -> p h o", o=1)
                                      .to_broadcast([P, NT * 2 * GH, 96]), ALU.mult)
                    dve.drain()
                    for m in range(NT):
                        for u in range(2):
                            qk = QKTOK[:, (2 * m + u) * GH:(2 * m + u + 1) * GH, :]
                            dve.tensor_tensor(qk, qk, GAINS[:, u:u + 1, :].to_broadcast([P, GH, 96]), ALU.mult)
                    dve.drain()
                    qk = QKTOK.rearrange("p (m h) d -> p m h d", m=NT)
                    x1, x2 = qk[:, :, :, 64:80], qk[:, :, :, 80:96]

                    def table(v):
                        return v.rearrange("p m (o i) -> p m o i", o=1).to_broadcast([P, NT, 2 * GH, 16])

                    r = [v.rearrange("p (m h i) -> p m h i", m=NT, h=2 * GH) for v in ROT]
                    for v, x, c in ((r[0], x1, COS), (r[1], x2, SIN), (r[2], x1, SIN), (r[3], x2, COS)):
                        dve.tensor_tensor(v, x, table(c), ALU.mult)
                    dve.drain()
                    dve.tensor_tensor(x1, r[0], r[1], ALU.subtract)
                    dve.tensor_tensor(x2, r[2], r[3], ALU.add)
                    dve.drain()
                    dve.nop().then_inc(s_rot, 1)
                    for m in range(NT):
                        dve.wait_ge(s_qkturn, NT * g + m + 1)
                        dve.tensor_copy(KFEAT[0:96, :, m * P:(m + 1) * P],
                                        PS[0:96, 2 * (m % 2) + 1, :].rearrange("p (h t) -> p h t", h=GH)
                                        ).then_inc(s_kfeat, 1)

                    def largest(n):
                        w = (n % NT + 1) * P
                        s = banks(2 * (n % 2))
                        dve.wait_ge(s_score, NTASK * g + n + 1)
                        dve.memset(s[0:64, w - 64:w], -1e30)
                        dve.drain()
                        dve.tensor_reduce(rowmax[:, n % 2:n % 2 + 1], s[:, 0:w], AX.X, ALU.max)
                        dve.drain()
                        dve.tensor_scalar(rowmax[:, n % 2:n % 2 + 1], rowmax[:, n % 2:n % 2 + 1], -SCALE, None,
                                          ALU.mult).then_inc(s_max, 1)

                    def normalise(n):
                        h, i = n // NT, n % NT
                        dve.wait_ge(s_pv, NTASK * g + n + 1)
                        dve.tensor_scalar(YTOK[:, i, h * 64:(h + 1) * 64], PS[:, 6 + n % 2, 0:64],
                                          rowrec[:, n % 2:n % 2 + 1], None, ALU.mult).then_inc(s_y, 1)

                    largest(0)
                    for n in range(NTASK):
                        w = (n % NT + 1) * P
                        if n + 1 < NTASK:
                            if n >= 1:
                                dve.wait_ge(s_prob, NTASK * g + n)
                            largest(n + 1)
                        dve.wait_ge(s_pturn7, NTASK * g + n + 1)
                        if n >= 2:
                            dve.wait_ge(s_pv, NTASK * g + n - 1)
                        dve.tensor_copy(PROBT[n % 2].rearrange("p c t -> p (c t)")[:, 0:w],
                                        banks(4)[:, 0:w]).then_inc(s_probt, 1)
                        if n:
                            normalise(n - 1)
                        dve.reciprocal(rowrec[:, n % 2:n % 2 + 1], rowsum[:, n % 2:n % 2 + 1])
                        dve.drain()
                    normalise(NTASK - 1)
                    dve.wait_ge(s_yturn, g + 1)
                    for t in range(2):
                        dve.tensor_tensor(SIG1[t], SIG1[t], banks(2 * t), ALU.mult)
                    dve.drain()
                    for t in range(2):
                        r = RA[:, ds(2 * g + t, 1), :].rearrange("p a t -> p (a t)")
                        last = dve.tensor_tensor(r, r, SIG1[t], ALU.add)
                    last.then_inc(s_merged, 1)
        if upto < 8:
            return

        retire(*s_st, s_held)
        NE, NGRP, EPG = 32, 4, 8
        BIG = 1e30
        xn_dram = nc.dram_tensor("xn_dram", [T, D], F32).ap()
        list_dram = nc.dram_tensor("list_dram", [(NBLK + 1) * P, 1], I32).ap()
        X1ROW = [part(k * T, (T,)) for k in range(2)]
        NORM8 = [part((2 + k) * T, (T,)) for k in range(2)]
        XNT = [part((4 + k) * T, (ND, P)) for k in range(2)]
        FFN_G = part(6 * T, (T,))
        WROUTE = part(7 * T, (ND, NGRP + NE))
        BROUTE = part(7 * T + 288, (NGRP + NE,))
        LOGITS = part(7 * T + 328, (NT, NGRP + NE))
        R = [part(8 * T + 256 * k, (NT, NE)) for k in range(6)]
        PICK = [part(8 * T + 256 * (6 + k), (NT, NE)) for k in range(2)]
        EXPERT = part(10 * T, (NE,))
        BLOCKAT = part(10 * T + 32, (NBLK,))
        SHORT = [part(10 * T + 96 + 8 * k, (NT,)) for k in range(12)]
        CHOSEN = [small[:, 216 + 8 * k:224 + 8 * k] for k in range(2)]
        LISTROW = [part(10 * T + 208 + 8 * k, (NT,)) for k in range(2)]
        ENDS = part(10 * T + 224, (NE,))
        STARTS = part(10 * T + 256, (NE,))
        PADDED = part(10 * T + 288, (NE,))
        OFBLOCK = part(11 * T, (NBLK, NE))
        BLKF = part(13 * T, (NBLK,))
        PAIRSF = part(13 * T + 128, (1,))
        PAIRSI = sb("PAIRSI", [P, 1], I32)
        GGRP = part(13 * T + 64, (NT, NGRP))
        GGRP2 = part(13 * T + 96, (NT, NGRP))
        ONES = sb("ONES", [P, P])
        ROWI = sb("ROWI", [P, 2, NT], I32)
        TOKI = sb("TOKI", [P, NT], I32)
        COUNTI = sb("COUNTI", [P, NE], I32)
        BLKI = sb("BLKI", [P, NBLK], I32)
        LISTI = sb("LISTI", [P, NBLK + 1], I32)

        s_w8 = sem("s_w8")
        s_wr = sem("s_wr")
        s_x1row = [sem(f"s_x1row{k}") for k in range(2)]
        s_h2p = sem("s_h2p")
        s_h2 = sem("s_h2")
        s_xn = sem("s_xn")
        s_xnst = [sem(f"s_xnst{k}") for k in range(2)]
        s_xnturn = sem("s_xnturn")
        s_xnt = sem("s_xnt")
        s_log = sem("s_log")
        s_logev = sem("s_logev")
        s_gsub = sem("s_gsub")
        s_gexp = sem("s_gexp")
        s_pick = sem("s_pick")
        s_rank = sem("s_rank")
        s_rows8 = sem("s_rows8")
        s_zlist = sem("s_zlist")
        s_list = sem("s_list")

        with nc.Block() as block:
            @block.sync
            def _(sp):
                sp.dma_start(RB[:], a["w_out_2"].rearrange("o (k p) n -> p (o k) n", p=P)).then_inc(s_w8, 16)
                sp.dma_start(FFN_G, a["norm_ffn_g_2"].to_broadcast([P, D])).then_inc(s_wr, 16)
                sp.dma_start(WROUTE[:, :, 0:NGRP], a["router_group_w_2"].rearrange("o (k p) n -> p (o k) n", p=P)
                             ).then_inc(s_wr, 16)
                sp.dma_start(WROUTE[:, :, NGRP:], a["router_expert_w_2"].rearrange("o (k p) n -> p (o k) n", p=P)
                             ).then_inc(s_wr, 16)
                sp.dma_start(BROUTE[:, 0:NGRP], a["router_group_b_2"].to_broadcast([P, NGRP])).then_inc(s_wr, 16)
                sp.dma_start(BROUTE[:, NGRP:], a["router_expert_b_2"].to_broadcast([P, NE])).then_inc(s_wr, 16)
                sp.dma_start(EXPERT, a["c_expert"]).then_inc(s_wr, 16)
                sp.dma_start(BLOCKAT, a["c_block"]).then_inc(s_wr, 16)
                sp.dma_start(TOKI[:], a["c_token"]).then_inc(s_wr, 16)
                for m in range(NT):
                    if m >= 2:
                        sp.wait_ge(s_h2, m - 1)
                    sp.dma_start(X1ROW[m % 2], x1_dram[m]).then_inc(s_x1row[m % 2], 16)
                for m in range(NT):
                    sp.wait_ge(s_xn, m + 1)
                    sp.dma_start(xn_dram[m * P:(m + 1) * P, :], NORM8[m % 2]).then_inc(s_xnst[m % 2], 16)
                for k in range(2):
                    sp.wait_ge(s_xnst[k], 8 * NT)

            @block.tensor
            def _(pe):
                pe.wait_ge(s_w8, 16)
                for m in range(NT):
                    if m >= 4:
                        pe.wait_ge(s_h2, m - 3)
                    for h in range(2):
                        for k in range(ND):
                            last = pe.matmul(banks(2 * (m % 4))[:, h * HALF:(h + 1) * HALF],
                                             RA[:, k, m * P:(m + 1) * P], RB[:, k, h * HALF:(h + 1) * HALF],
                                             start=(k == 0), stop=(k == ND - 1))
                    last.then_inc(s_h2p, 1)
                pe.wait_ge(s_h2, NT)
                pe.wait_ge(s_wr, 16 * 8)
                for m in range(NT):
                    pe.wait_ge(s_xn, m + 1)
                    if m >= 2:
                        pe.wait_ge(s_xnt, m - 1)
                    pe_turn(pe, banks(2 * (m % 2)), NORM8[m % 2], s_xnturn)
                    pe.wait_ge(s_xnt, m + 1)
                    if m >= 2:
                        pe.wait_ge(s_logev, m - 1)
                    for k in range(ND):
                        last = pe.matmul(PS[:, 4 + m % 2, 0:NGRP + NE], XNT[m % 2][:, k, :], WROUTE[:, k, :],
                                         start=(k == 0), stop=(k == ND - 1))
                    last.then_inc(s_log, 1)
                pe.wait_ge(s_pick, 1)
                pe.wait_ge(s_zlist, 1)
                for m in range(NT):
                    for e in range(m + 1):
                        pe.matmul(PS[:, 6, m * NE:(m + 1) * NE], before if e == m else ONES[:], R[0][:, e, :],
                                  start=(e == 0), stop=(e == m))
                for e in range(NT):
                    last = pe.matmul(PS[:, 7, 0:NE], ONES[:], R[0][:, e, :], start=(e == 0), stop=(e == NT - 1))
                last.then_inc(s_rank, 1)

            @block.scalar
            def _(act):
                root_mean_square(act, s_h2, 3, RC)
                for m in range(NT):
                    act.wait_ge(s_xnturn, m + 1)
                    if m >= 2:
                        act.wait_ge(s_log, m - 1)
                    act.activation(XNT[m % 2].rearrange("p c t -> p (c t)"), banks(2 * (m % 2)),
                                   ACT.Copy).then_inc(s_xnt, 1)
                for n in range(2):
                    act.wait_ge(s_gsub, n + 1)
                    v = (GGRP, SHORT[4])[n]
                    act.activation(v, v, ACT.Exp).then_inc(s_gexp, 1)

            @block.gpsimd
            def _(pool):
                pool.memset(LISTI[:], 0)
                pool.memset(ONES[:], 1.0).then_inc(s_zlist, 1)
                pool.drain()
                pool.dma_start(list_dram.rearrange("(b p) o -> p (b o)", p=P), LISTI[:]).then_inc(s_list, 16)
                pool.wait_ge(s_rows8, 1)
                pool.wait_ge(s_list, 16)
                pool.wait_ge(s_wr, 16 * 8)
                for u in range(2):
                    for m in range(NT):
                        pool.indirect_dma_start(list_dram, bass.IndirectOffsetOnAxis(ap=ROWI[:, u, m:m + 1], axis=0),
                                                TOKI[:, m:m + 1], None).then_inc(s_list, 16)
                pool.wait_ge(s_list, 16 * (1 + 2 * NT))
                pool.dma_start(LISTI[:], list_dram.rearrange("(b p) o -> p (b o)", p=P)).then_inc(s_list, 16)

            @block.vector
            def _(dve):
                for m in range(NT):
                    dve.wait_ge(s_h2p, m + 1)
                    dve.wait_ge(s_x1row[m % 2], 16 * (m // 2) + 16)
                    dve.tensor_tensor(RC[:, m, :], banks(2 * (m % 4)), X1ROW[m % 2], ALU.add).then_inc(s_h2, 1)
                reciprocal_roots(dve, 3)
                dve.wait_ge(s_wr, 16 * 8)

                def logits(m):
                    dve.wait_ge(s_log, m + 1)
                    dve.tensor_tensor(LOGITS[:, m, :], PS[:, 4 + m % 2, 0:NGRP + NE], BROUTE,
                                      ALU.add).then_inc(s_logev, 1)

                for m in range(NT):
                    if m >= 2:
                        dve.wait_ge(s_xnturn, m - 1)
                        dve.wait_ge(s_xnst[m % 2], 16 * (m // 2))
                    dve.scalar_tensor_tensor(NORM8[m % 2], RC[:, m, :], rstd[:, m:m + 1], FFN_G, ALU.mult,
                                             ALU.mult).then_inc(s_xn, 1)
                    if m:
                        logits(m - 1)
                logits(NT - 1)
                dve.drain()

                def wide(v, n):
                    return v.rearrange("p (m o) -> p m o", o=1).to_broadcast([P, NT, n])

                def narrow(v, n):
                    return v[:, 0:n].rearrange("p (o e) -> p o e", o=1).to_broadcast([P, NT, n])

                def then(*_):
                    dve.drain()

                def first_largest(v, n, top, index, pick, scratch):
                    then(dve.tensor_reduce(top, v, AX.X, ALU.max))
                    then(dve.tensor_tensor(scratch, v, wide(top, n), ALU.not_equal))
                    then(dve.tensor_scalar(scratch, scratch, BIG, None, ALU.mult))
                    then(dve.tensor_tensor(scratch, scratch, narrow(EXPERT, n), ALU.add))
                    then(dve.tensor_reduce(index, scratch, AX.X, ALU.min))
                    then(dve.tensor_tensor(pick, narrow(EXPERT, n), wide(index, n), ALU.is_equal))

                grp, exp = LOGITS[:, :, 0:NGRP], LOGITS[:, :, NGRP:]
                gmax, gidx, ptop, v1, v2, w1, w2, idx = SHORT[0], SHORT[1], SHORT[2], SHORT[3], SHORT[4], *SHORT[5:8]
                first_largest(grp, NGRP, gmax, gidx, GGRP2, GGRP)
                dve.tensor_tensor(GGRP, grp, wide(gmax, NGRP), ALU.subtract).then_inc(s_gsub, 1)
                dve.wait_ge(s_gexp, 1)
                then(dve.tensor_reduce(ptop, GGRP, AX.X, ALU.add))
                then(dve.reciprocal(ptop, ptop))
                oh = GGRP2.rearrange("p m (g o) -> p m g o", o=1).to_broadcast([P, NT, NGRP, EPG])
                e4 = exp.rearrange("p m (g e) -> p m g e", g=NGRP)
                r1 = R[1].rearrange("p m (g e) -> p m g e", g=NGRP)
                r2 = R[2].rearrange("p m (g e) -> p m g e", g=NGRP)
                dve.tensor_tensor(r1, e4, oh, ALU.mult)
                then(dve.tensor_scalar(r2, oh, -1.0, BIG, ALU.add, ALU.mult))
                then(dve.tensor_tensor(R[1], R[1], R[2], ALU.add))
                first_largest(R[1], NE, v1, idx, PICK[0], R[2])
                then(dve.tensor_scalar(R[2], PICK[0], -2 * BIG, None, ALU.mult))
                then(dve.tensor_tensor(R[1], R[1], R[2], ALU.add))
                first_largest(R[1], NE, v2, idx, PICK[1], R[2])
                then(dve.tensor_tensor(R[0], PICK[0], PICK[1], ALU.add))
                dve.nop().then_inc(s_pick, 1)
                dve.tensor_tensor(v2, v2, v1, ALU.subtract).then_inc(s_gsub, 1)
                dve.wait_ge(s_gexp, 2)
                then(dve.tensor_scalar(w1, v2, 1.0, None, ALU.add))
                then(dve.reciprocal(w1, w1))
                then(dve.tensor_tensor(CHOSEN[0], ptop, w1, ALU.mult))
                then(dve.tensor_tensor(CHOSEN[1], CHOSEN[0], v2, ALU.mult))
                dve.wait_ge(s_zlist, 1)
                dve.wait_ge(s_rank, 1)
                then(dve.tensor_scalar(PADDED, PS[:, 7, 0:NE], float(P - 1), None, ALU.add))
                then(dve.tensor_copy(COUNTI[:], PADDED))
                then(dve.tensor_scalar(COUNTI[:], COUNTI[:], 7, 7, ALU.arith_shift_right, ALU.arith_shift_left))
                then(dve.tensor_copy(PADDED, COUNTI[:]))
                then(dve.tensor_tensor_scan(ENDS, ONES[:, 0:NE], PADDED, 0.0, ALU.mult, ALU.add))
                then(dve.tensor_tensor(STARTS, ENDS, PADDED, ALU.subtract))
                then(dve.tensor_tensor(R[3], PS[:, 6, 0:NT * NE].rearrange("p (m e) -> p m e", e=NE),
                                       narrow(STARTS, NE), ALU.add))
                for u in range(2):
                    then(dve.tensor_tensor(R[4], R[3], PICK[u], ALU.mult))
                    then(dve.tensor_reduce(LISTROW[u], R[4], AX.X, ALU.add))
                    then(dve.tensor_copy(ROWI[:, u, :], LISTROW[u]))
                dve.nop().then_inc(s_rows8, 1)
                ends = ENDS.rearrange("p (o e) -> p o e", o=1).to_broadcast([P, NBLK, NE])
                at = BLOCKAT.rearrange("p (b o) -> p b o", o=1).to_broadcast([P, NBLK, NE])
                then(dve.tensor_tensor(OFBLOCK, ends, at, ALU.is_le))
                then(dve.tensor_reduce(BLKF, OFBLOCK, AX.X, ALU.add))
                then(dve.tensor_scalar(BLKF, BLKF, float(NE - 1), None, ALU.min))
                then(dve.tensor_copy(BLKI[:], BLKF))
                then(dve.tensor_scalar(PAIRSF, ENDS[:, NE - 1:NE], float(P), None, ALU.add))
                then(dve.tensor_copy(PAIRSI[:], PAIRSF))
                dve.tensor_scalar(PAIRSI[:], PAIRSI[:], 8, None, ALU.arith_shift_right)

        if upto < 9:
            with nc.Block() as block:
                @block.sync
                def _(sp):
                    sp.wait_ge(s_list, 16 * (2 + 2 * NT))
            return

        TOKS = [sb(f"TOKS{k}", [P, 1], I32) for k in range(2)]
        EG = [part(k * 6 * T, (ND, 256)) for k in range(2)]
        EU = [part(2 * T + k * 6 * T, (ND, 256)) for k in range(2)]
        ED = [part(4 * T + k * 6 * T, (2, T)) for k in range(2)]
        XG = [part((14 + k) * T, (T,)) for k in range(2)]
        XT = [part((16 + k) * T, (ND, P)) for k in range(2)]
        HB = [part(18 * T + 512 * k, (512,)) for k in range(2)]
        HT = [part(19 * T + 256 * k, (2, P)) for k in range(2)]
        YB = [part((20 + k) * T, (T,)) for k in range(2)]

        s_gland = [sem(f"s_gland{k}") for k in range(2)]
        s_dland = [sem(f"s_dland{k}") for k in range(2)]
        s_xgath = [sem(f"s_xgath{k}") for k in range(2)]
        s_xgt = sem("s_xgt")
        s_xte = sem("s_xte")
        s_gu = sem("s_gu")
        s_gact = sem("s_gact")
        s_hb = sem("s_hb")
        s_hbt = sem("s_hbt")
        s_hte = sem("s_hte")
        s_down = sem("s_down")
        s_yb = sem("s_yb")
        s_yst = [sem(f"s_yst{k}") for k in range(2)]
        NPAIR = NBLK // 2
        wg_t = a["w_gate_2"].rearrange("o e (p k) n -> p (o e) (k n)", k=ND)
        wu_t = a["w_up_2"].rearrange("o e (p k) n -> p (o e) (k n)", k=ND)
        wd_t = a["w_down_2"].rearrange("o e (p k) n -> p (o e) (k n)", k=2)

        def active_pairs(eng, body):
            used = eng.value_load(PAIRSI[0:1, 0:1], min_val=NBLK // 6, max_val=NPAIR)
            body(0)
            with eng.Fori(1, NPAIR) as i:
                with eng.If(i < used):
                    body(i)

        with nc.Block() as block:
            @block.sync
            def _(sp):
                def body(i):
                    for s in range(2):
                        b = 2 * i + s
                        e = sp.value_load(BLKI[0:1, ds(b, 1)], min_val=0, max_val=NE - 1)
                        if not isinstance(i, int):
                            sp.wait_ge(s_gu, b - 1)
                            hold(sp)
                        for dst, src in ((EG, wg_t), (EU, wu_t)):
                            sp.dma_start(dst[s].rearrange("p k n -> p (k n)"),
                                         src[:, ds(e, 1), :].rearrange("p a n -> p (a n)")).then_inc(s_gland[s], 16)
                        if not isinstance(i, int):
                            sp.wait_ge(s_down, b - 1)
                            hold(sp)
                        sp.dma_start(ED[s].rearrange("p k n -> p (k n)"),
                                     wd_t[:, ds(e, 1), :].rearrange("p a n -> p (a n)")).then_inc(s_dland[s], 16)

                active_pairs(sp, body)

            @block.gpsimd
            def _(pool):
                pool.wait_ge(s_list, 16 * (2 + 2 * NT))

                def gather(b, s):
                    pool.tensor_copy(TOKS[s][:], LISTI[:, ds(b, 1)])
                    pool.drain()
                    pool.indirect_dma_start(XG[s], None, xn_dram,
                                            bass.IndirectOffsetOnAxis(ap=TOKS[s][:], axis=0)
                                            ).then_inc(s_xgath[s], 16)

                def body(i):
                    if not isinstance(i, int):
                        pool.wait_ge(s_xgt, 2 * i)
                        hold(pool)
                    gather(2 * i + 1, 1)
                    pool.wait_ge(s_xgt, 2 * i + 1)
                    hold(pool)
                    gather(2 * i + 2, 0)

                gather(0, 0)
                active_pairs(pool, body)

            @block.tensor
            def _(pe):
                def turn(i, s):
                    pe.wait_ge(s_xgath[s], 16 * i + 16)
                    if s or not (isinstance(i, int) and i == 0):
                        pe.wait_ge(s_xte, 2 * i + s)
                    x = XG[s].rearrange("p (d k) -> p k d", k=ND)
                    for k in range(ND):
                        last = pe.transpose(banks(0)[:, k * P:(k + 1) * P], x[:, k, :], ident)
                    last.then_inc(s_xgt, 1)

                def expert(i, s):
                    pe.wait_ge(s_gland[s], 32 * i + 32)
                    pe.wait_ge(s_xte, 2 * i + s + 1)
                    if s or not isinstance(i, int):
                        pe.wait_ge(s_hb, 2 * i + s)
                    for u, w in enumerate((EG[s], EU[s])):
                        for k in range(ND):
                            last = pe.matmul(PS[:, 2 + u, 0:256], XT[s][:, k, :], w[:, k, :],
                                             start=(k == 0), stop=(k == ND - 1))
                    last.then_inc(s_gu, 1)

                def turn_hidden(i, s):
                    pe.wait_ge(s_hb, 2 * i + s + 1)
                    if s or not isinstance(i, int):
                        pe.wait_ge(s_hte, 2 * i + s)
                    h = HB[s][:, 0:256].rearrange("p (f k) -> p k f", k=2)
                    for k in range(2):
                        last = pe.transpose(PS[:, 4, k * P:(k + 1) * P], h[:, k, :], ident)
                    last.then_inc(s_hbt, 1)

                def down(i, s):
                    pe.wait_ge(s_dland[s], 16 * i + 16)
                    pe.wait_ge(s_hte, 2 * i + s + 1)
                    if s or not isinstance(i, int):
                        pe.wait_ge(s_yb, 2 * i + s)
                    for h in range(2):
                        for k in range(2):
                            last = pe.matmul(banks(6)[:, h * HALF:(h + 1) * HALF], HT[s][:, k, :],
                                             ED[s][:, k, h * HALF:(h + 1) * HALF], start=(k == 0), stop=(k == 1))
                    last.then_inc(s_down, 1)

                def body(i):
                    expert(i, 0)
                    turn(i, 1)
                    turn_hidden(i, 0)
                    expert(i, 1)
                    down(i, 0)
                    turn(i + 1, 0)
                    turn_hidden(i, 1)
                    down(i, 1)

                turn(0, 0)
                active_pairs(pe, body)

            @block.scalar
            def _(act):
                def turned(b, s, first):
                    act.wait_ge(s_xgt, b + 1)
                    if not first:
                        act.wait_ge(s_gu, b - 1)
                    act.activation(XT[s].rearrange("p c t -> p (c t)"), banks(0), ACT.Copy).then_inc(s_xte, 1)

                def silu(i, s):
                    b = 2 * i + s
                    act.wait_ge(s_gu, b + 1)
                    if not isinstance(i, int):
                        act.wait_ge(s_hb, b - 1)
                    act.activation(HB[s][:, 256:512], PS[:, 2, 0:256], ACT.Silu).then_inc(s_gact, 1)

                def store(i, s):
                    b = 2 * i + s
                    act.wait_ge(s_down, b + 1)
                    if not isinstance(i, int):
                        act.wait_ge(s_yst[s], 16 * i)
                    act.activation(YB[s], banks(6), ACT.Copy).then_inc(s_yb, 1)
                    act.wait_ge(s_yb, b + 1)
                    hold(act)
                    act.dma_start(y_dram[ds(b * P, P), :], YB[s]).then_inc(s_yst[s], 16)

                def body(i):
                    silu(i, 0)
                    turned(2 * i + 1, 1, isinstance(i, int))
                    silu(i, 1)
                    store(i, 0)
                    turned(2 * i + 2, 0, False)
                    store(i, 1)

                turned(0, 0, True)
                active_pairs(act, body)

            @block.vector
            def _(dve):
                def body(i):
                    for s in range(2):
                        b = 2 * i + s
                        dve.wait_ge(s_gact, b + 1)
                        if not isinstance(i, int):
                            dve.wait_ge(s_hbt, b - 1)
                        dve.tensor_tensor(HB[s][:, 0:256], HB[s][:, 256:512], PS[:, 3, 0:256],
                                          ALU.mult).then_inc(s_hb, 1)
                        dve.wait_ge(s_hbt, b + 1)
                        dve.tensor_copy(HT[s].rearrange("p k t -> p (k t)"), PS[:, 4, 0:256]).then_inc(s_hte, 1)

                active_pairs(dve, body)

        YGATH = [part(k * T, (T,)) for k in range(4)]
        s_yg = [sem(f"s_yg{k}") for k in range(4)]
        s_sum = sem("s_sum")
        s_out = sem("s_out")
        out_rows = out.rearrange("o (m p) d -> p (o m) d", p=P)

        with nc.Block() as block:
            @block.gpsimd
            def _(pool):
                used = pool.value_load(PAIRSI[0:1, 0:1], min_val=NBLK // 6, max_val=NPAIR)
                for s in range(2):
                    pool.wait_ge(s_yst[s], used * 16)
                    hold(pool)
                for m in range(NT):
                    if m >= 2:
                        pool.wait_ge(s_sum, m - 1)
                    for u in range(2):
                        k = 2 * (m % 2) + u
                        pool.indirect_dma_start(YGATH[k], None, y_dram,
                                                bass.IndirectOffsetOnAxis(ap=ROWI[:, u, m:m + 1], axis=0)
                                                ).then_inc(s_yg[k], 16)

            @block.vector
            def _(dve):
                for m in range(NT):
                    for u in range(2):
                        k = 2 * (m % 2) + u
                        dve.wait_ge(s_yg[k], 16 * (m // 2) + 16)
                        if u:
                            dve.drain()
                        last = dve.scalar_tensor_tensor(RC[:, m, :], YGATH[k], CHOSEN[u][:, m:m + 1], RC[:, m, :],
                                                        ALU.mult, ALU.add)
                    last.then_inc(s_sum, 1)

            @block.sync
            def _(sp):
                for m in range(NT):
                    sp.wait_ge(s_sum, m + 1)
                    sp.dma_start(out_rows[:, m, :], RC[:, m, :]).then_inc(s_out, 16)
                sp.wait_ge(s_out, 16 * NT)


_OUT_SHAPE = (1, T, D)


def kernel(**inputs):
    import concourse.bacc as _bacc
    from concourse.bass_utils import run_bass_kernel_spmd as _run

    nc = _bacc.Bacc("TRN2", target_bir_lowering=False, num_devices=1)
    arrays, aps = {}, {}
    for name, value in {**inputs, **shape_constants()}.items():
        v = np.ascontiguousarray(value)
        arrays[f"in_{name}"] = v
        aps[name] = nc.dram_tensor(f"in_{name}", v.shape, mybir.dt.from_np(v.dtype), kind="ExternalInput").ap()
    out = nc.dram_tensor("out_0", _OUT_SHAPE, F32, kind="ExternalOutput").ap()
    build(nc, aps, out)
    r = _run(nc, [arrays], core_ids=[0])
    return r.results[0]["out_0"]
```

```python
from contextlib import ExitStack

import numpy as np

import concourse.bass as bass
from concourse import mybir
from concourse.bass import ds

ALU = mybir.AluOpType
ACT = mybir.ActivationFunctionType
AX = mybir.AxisListType
F32 = mybir.dt.float32
F32R = mybir.dt.float32r
I32 = mybir.dt.int32
U8 = mybir.dt.uint8

P = 128
T = 1024
D = 1024
NT = T // P
ND = D // P
HALF = 512
CONV_K = 31
LEVELS = 7
EPS = 1e-6
ROUND = 1.5 * 2.0 ** 23
TWO_PI = (6.28125, 0.0019350051879882812, float(2 * np.pi - 6.28125 - 0.0019350051879882812))

ROWS = {"conv_w": 0, "ln_g": 31, "conv_b": 32, "cnorm_g": 33, "cnorm_b": 34, "b_pw2": 35,
        "lb0": 36, "lb1": 37, "onorm_g": 38, "pe_norm_g": 39, "norm_mix_g": 40, "conv_w_2": 41,
        "conv_b_2": 45, "lru_ba": 46, "lru_bx": 47, "lru_lambda": 48, "q_a_g": 49, "kv_a_g": 50}
NROWS = 51


def shape_constants():
    ident = np.eye(P, dtype=np.float32)
    mean = np.full((P, P), 1.0 / P, np.float32)
    before = np.triu(np.ones((P, P), np.float32), 1)
    restart = np.ones((P, T), np.float32)
    restart[:, ::P] = 0.0
    masks = np.zeros((P, LEVELS + 1, P), np.float32)
    s, t = np.meshgrid(np.arange(P), np.arange(P), indexing="ij")
    for level in range(LEVELS):
        size = 1 << level
        masks[:, level] = (s // (2 * size) == t // (2 * size)) & (s // size % 2 == 0) & (t // size % 2 == 1)
    masks[:, LEVELS] = s == t
    half = 16
    freq = (np.float32(10000.0) ** (-np.arange(half, dtype=np.float32) / np.float32(half))).astype(np.float32)
    return {
        "c_square": np.stack([ident, mean, before], axis=1),
        "c_restart": restart,
        "c_masks": masks,
        "c_freq": np.broadcast_to(freq, (P, half)).copy(),
        "c_expert": np.broadcast_to(np.arange(32, dtype=np.float32), (P, 32)).copy(),
        "c_block": np.broadcast_to(np.arange(48, dtype=np.float32) * 128, (P, 48)).copy(),
        "c_token": (np.arange(P)[:, None] + P * np.arange(NT)[None, :]).astype(np.int32),
    }


def build(nc, a, out):
    ctx = ExitStack()
    with ctx:
        ctx.enter_context(nc.allow_non_contiguous_dma(reason="parameter vectors and small tables"))

        def sb(name, shape, dt=F32):
            return ctx.enter_context(nc.sbuf_tensor(name, shape, dt))

        in_use = []

        def sem(name):
            in_use.append(nc.alloc_semaphore(name))
            return in_use[-1]

        def retire(*kept):
            done = [s for s in in_use if not any(s is k for k in kept)]
            in_use[:] = list(kept)
            nc.clear_and_free_semaphores(done)
            nc.all_engine_barrier()

        PS = ctx.enter_context(nc.psum_tensor("PS", [P, 8, HALF], F32))
        at_byte = {}

        def region(name, shape):
            at_byte[name] = (nc.sbuf_base + 31) // 32 * 32
            return sb(name, shape)

        def rounded(name, where, floats, shape):
            return nc.alloc_sbuf_tensor_at(name, shape, F32R, offset=at_byte[where] + 4 * floats)

        RA = region("RA", [P, ND, T])
        RB = region("RB", [P, ND, T])
        RC = region("RC", [P, ND, T])
        square = sb("square", [P, 3, P])
        ident, mean, before = square[:, 0, :], square[:, 1, :], square[:, 2, :]
        cols = sb("cols", [P, ND, NROWS])
        small = sb("small", [P, 320])
        ARENA = 25 * T
        arena = region("arena", [P, ARENA])

        def part(at, shape, dt=F32):
            n = int(np.prod(shape))
            v = arena[:, at:at + n]
            if len(shape) == 2:
                v = v.rearrange("p (x y) -> p x y", y=shape[1])
            if len(shape) == 3:
                v = v.rearrange("p (x y z) -> p x y z", y=shape[1], z=shape[2])
            return v

        def passes(a, b):
            return (a[0], b[0]), (a[0], b[1]), (a[1], b[0])

        def split_hi(act, dst, src):
            return act.activation(dst, src, ACT.Copy)

        def split_lo(eng, dst, src, hi):
            return eng.tensor_tensor(dst, src, hi.bitcast(F32), ALU.subtract)

        def banks(b, n=2):
            return PS[:, b:b + n, :].rearrange("p b n -> p (b n)")

        def col(name, j, k=0):
            r = ROWS[name] + k
            return cols[:, ds(j, 1), r:r + 1].rearrange("p a b -> p (a b)")

        s_const = sem("s_const")
        s_rows = sem("s_rows")
        s_x = [sem(f"s_xtile{m}") for m in range(NT)]
        s_zero = sem("s_zero")
        s_sumsq = sem("s_sumsq")
        s_var = sem("s_var")
        s_root = sem("s_root")
        s_scaled = sem("s_scaled")
        s_turned = sem("s_turned")
        s_ut = sem("s_ut")
        s_params = sem("s_params")
        s_turned_rows = sem("s_turned_rows")
        s_lb = sem("s_lb")
        s_lbexp = sem("s_lbexp")

        rows = part(0, (D,))
        scratch = part(1 * T, (2, D))
        xtile = RC[:, :, :]
        UHI = rounded("UHI", "RA", 0, [P, ND, T])
        ULO = rounded("ULO", "RB", 0, [P, ND, T])
        UTMP = [part((3 + k) * T, (ND, P)) for k in range(3)]
        s_uhi = sem("s_uhi")
        WRAW = [part((20 + k) * T, (ND, P)) for k in range(2)]
        FIRST_COL = [0, D, 4 * D, 3 * D, 5 * D, 6 * D]
        s_wland = [sem(f"s_wland{k}") for k in range(2)]

        def load_projection(sp, j, s):
            w = a["w_in"].rearrange("o (k p) n -> p (o k) n", p=P)[:, :, ds(j * P + FIRST_COL[s], P)]
            sp.dma_start(WRAW[s % 2], w).then_inc(s_wland[s % 2], 16)

        sumsq, meansq, root, rstd = (small[:, 8 * k:8 * k + 8] for k in range(4))
        lbound, lslack, t0, t1 = (small[:, 32 + 8 * k:40 + 8 * k] for k in range(4))

        with nc.Block() as block:
            @block.sync
            def _(sp):
                sp.dma_start(square[:], a["c_square"]).then_inc(s_const, 16)
                for m in range(NT):
                    sp.dma_start(xtile[:, m, :], a["x"][0, m * P:(m + 1) * P, :]).then_inc(s_x[m], 16)
                sp.wait_ge(s_zero, 1)
                for name, r in ROWS.items():
                    src = {"lb0": a["lb_logits"][0:1, :], "lb1": a["lb_logits"][1:2, :],
                           "conv_w": a["conv_w"].rearrange("o k d -> (o k) d"),
                           "conv_w_2": a["conv_w_2"].rearrange("o k d -> (o k) d")}.get(name)
                    if src is None:
                        full = name if name in a else name + "_2"
                        src = a[full]
                    n, w = src.shape
                    sp.dma_start(rows[r:r + n, 0:w], src).then_inc(s_rows, 16)
                for s in range(2):
                    load_projection(sp, 0, s)

            @block.scalar
            def _(act):
                for m in range(NT):
                    act.wait_ge(s_x[m], 16)
                    act.activation(scratch[:, m % 2, :], xtile[:, m, :], ACT.Square, accum_out=sumsq[:, m:m + 1])
                    act.drain()
                act.nop().then_inc(s_sumsq, 1)
                act.wait_ge(s_var, 1)
                act.activation(root, meansq, ACT.Sqrt).then_inc(s_root, 1)
                for m in range(NT):
                    act.wait_ge(s_ut, m + 1)
                    split_hi(act, UHI[:, :, m * P:(m + 1) * P], UTMP[m % 3]).then_inc(s_uhi, 1)
                act.wait_ge(s_lb, 1)
                act.activation(t0, t0, ACT.Exp)
                act.activation(t1, t1, ACT.Exp)
                act.drain()
                act.nop().then_inc(s_lbexp, 1)

            @block.vector
            def _(dve):
                dve.memset(rows, 0.0).then_inc(s_zero, 1)
                dve.wait_ge(s_sumsq, 1)
                dve.tensor_scalar(meansq, sumsq, 1.0 / D, EPS, ALU.mult, ALU.add).then_inc(s_var, 1)
                dve.wait_ge(s_root, 1)
                dve.reciprocal(rstd, root)
                dve.drain()
                for m in range(NT):
                    dve.tensor_scalar(xtile[:, m, :], xtile[:, m, :], rstd[:, m:m + 1], None,
                                      ALU.mult).then_inc(s_scaled, 1)
                for j in range(ND):
                    dve.wait_ge(s_turned_rows, j + 1)
                    dve.tensor_copy(cols[:, j, :], PS[:, 4 + j % 4, 0:NROWS]).then_inc(s_params, 1)
                dve.drain()

                def u_lo(m):
                    dve.wait_ge(s_uhi, m + 1)
                    dve.drain()
                    split_lo(dve, ULO[:, :, m * P:(m + 1) * P], UTMP[m % 3], UHI[:, :, m * P:(m + 1) * P])

                for m in range(NT):
                    dve.wait_ge(s_turned, m + 1)
                    if m >= 2:
                        dve.wait_ge(s_uhi, m - 1)
                    dve.tensor_tensor(UTMP[m % 3],
                                      banks(2 * (m % 2)).rearrange("p (c t) -> p c t", c=ND),
                                      cols[:, :, ROWS["ln_g"]:ROWS["ln_g"] + 1].to_broadcast([P, ND, P]),
                                      ALU.mult).then_inc(s_ut, 1)
                    if m:
                        u_lo(m - 1)
                u_lo(NT - 1)
                l0, l1 = cols[:, :, ROWS["lb0"]], cols[:, :, ROWS["lb1"]]
                dve.tensor_tensor(t0, l0, l1, ALU.max)
                dve.drain()
                dve.tensor_tensor(t1, l1, t0, ALU.subtract)
                dve.tensor_tensor(t0, l0, t0, ALU.subtract)
                dve.drain()
                dve.nop().then_inc(s_lb, 1)
                dve.wait_ge(s_lbexp, 1)
                dve.tensor_tensor(lslack, t0, t1, ALU.add)
                dve.drain()
                dve.reciprocal(lslack, lslack)
                dve.drain()
                dve.tensor_tensor(lbound, t0, lslack, ALU.mult)
                dve.drain()
                dve.tensor_scalar(lslack, lbound, -1.0, 1.0, ALU.mult, ALU.add)

            @block.tensor
            def _(pe):
                pe.wait_ge(s_const, 16)
                pe.wait_ge(s_rows, 16 * len(ROWS))
                for j in range(ND):
                    if j >= 4:
                        pe.wait_ge(s_params, j - 3)
                    pe.transpose(PS[:, 4 + j % 4, 0:NROWS], rows[0:NROWS, j * P:(j + 1) * P],
                                 ident[0:NROWS, 0:NROWS]).then_inc(s_turned_rows, 1)
                for m in range(NT):
                    pe.wait_ge(s_scaled, m + 1)
                    if m >= 2:
                        pe.wait_ge(s_ut, m - 1)
                    for c in range(ND):
                        last = pe.transpose(banks(2 * (m % 2))[:, c * P:(c + 1) * P],
                                            xtile[:, m, c * P:(c + 1) * P], ident)
                    last.then_inc(s_turned, 1)

        GLU, FORGET = (part(k * T, (T,)) for k in range(2))
        KEYS, QUERIES, VALUES, GATE_S = ([part((2 + 2 * n + k) * T, (T,)) for k in range(2)] for n in range(4))
        CUM, CUMEXP, QDEC, ACC, SQ = (part(k * T, (T,)) for k in range(10, 15))
        DECAY = [part(k * T, (T,)) for k in (15, 16)]
        QK = [part(k * T, (T,)) for k in (17, 18)]
        WEIGHTS = part(19 * T, (NT, P))
        KDEC = QK[1].rearrange("p (c k) -> p c k", k=P)
        STATE = QK[0].rearrange("p (c v) -> p c v", v=P)
        HSQ = QK[1]
        HOUT = [RC[:, k, :] for k in (0, 1)]
        PAD = RC[:, 2:4, :].rearrange("p a t -> p (a t)")[:, 0:CONV_K - 1 + T]
        RESTART = RC[:, 4, :]
        COUT = [RC[:, k, :] for k in (5, 7)]
        WHI = [rounded(f"WHI{k}", "arena", (22 + k) * T, [P, ND, P]) for k in range(2)]
        WLO = [rounded("WLO0", "arena", 24 * T, [P, ND, P]), rounded("WLO1", "RC", 6 * T, [P, ND, P])]
        ct_dram = nc.dram_tensor("ct_dram", [ND, P, T], F32).ap()
        yh_dram = nc.dram_tensor("yh_dram", [ND, P, T], F32).ap()
        MASKS = sb("MASKS", [P, LEVELS + 1, P], U8)
        NPROJ = 6

        s_tables = sem("s_tables")
        s_whi = sem("s_whi")
        s_wlo = sem("s_wlo")
        s_glu = sem("s_glu")
        s_ctst = [sem(f"s_ctst{k}") for k in range(2)]
        s_proj = sem("s_proj")
        s_evac = sem("s_evac")
        s_cum = sem("s_cum")
        s_logf = sem("s_logf")
        s_diff = sem("s_diff")
        s_dexp = sem("s_dexp")
        s_qk = sem("s_qk")
        s_aprod = sem("s_aprod")
        s_amask = sem("s_amask")
        s_kd = sem("s_kd")
        s_kdt = sem("s_kdt")
        s_kdec = sem("s_kdec")
        s_dstate = sem("s_dstate")
        s_state = sem("s_state")
        s_o = sem("s_o")
        s_osq = sem("s_osq")
        s_oms = sem("s_oms")
        s_oroot = sem("s_oroot")
        s_ohead = sem("s_ohead")
        s_conv = sem("s_conv")
        s_mu = sem("s_mu")
        s_cent = sem("s_cent")
        s_csq = sem("s_csq")
        s_cvar = sem("s_cvar")
        s_croot = sem("s_croot")
        s_cnorm = sem("s_cnorm")
        s_cout = sem("s_cout")
        s_epsv = sem("s_epsv")
        s_yhst = [sem(f"s_yhst{k}") for k in range(2)]
        s_held = sem("s_held")
        eps = small[:, 64:65]
        W2RAW = WRAW
        s_w2land = [sem(f"s_w2land{k}") for k in range(2)]

        def load_second(sp, b, k):
            src, c0, t = (a["w_in"], 2 * D, b) if k < 2 else (a["w_pw2"], 0, b - ND // 2)
            w = src.rearrange("o (k p) n -> p (o k) n", p=P)[:, :, ds((2 * t + k % 2) * P + c0, P)]
            sp.dma_start(W2RAW[k % 2], w).then_inc(s_w2land[k % 2], 16)

        def split(v, size):
            return v.rearrange("p (b u s) -> p b u s", u=2, s=size)

        def hold(eng):
            eng.sem_inc(s_held, 1)

        def chunks(v):
            return v.rearrange("p (c t) -> p c t", t=P)

        with nc.Block() as block:
            @block.sync
            def _(sp):
                sp.dma_start(RESTART, a["c_restart"]).then_inc(s_tables, 16)
                sp.dma_start(WEIGHTS, a["c_masks"]).then_inc(s_tables, 16)

                for s in range(2, NPROJ):
                    sp.wait_ge(s_wlo, s - 1)
                    load_projection(sp, 0, s)
                with sp.Fori(1, ND) as j:
                    for s in range(NPROJ):
                        sp.wait_ge(s_wlo, NPROJ * j + s - 1)
                        hold(sp)
                        load_projection(sp, j, s)
                sp.wait_ge(s_wlo, NPROJ * ND)
                for k in range(2):
                    load_second(sp, 0, k)

            LOW, HIGH = banks(4), banks(6)
            LEVEL_PAIR = [LOW, HIGH, LOW, HIGH, HIGH, LOW, LOW, HIGH]

            def pe_project(pe, j, s):
                pe.wait_ge(s_wlo, NPROJ * j + s + 1)
                if s >= 2 or not (isinstance(j, int) and j == 0):
                    pe.wait_ge(s_evac, NPROJ * j + s - 1)
                w = WHI[s % 2], WLO[s % 2]
                o = banks(2 * (s % 2))
                if s == 4:
                    for c in range(NT):
                        for k in range(ND):
                            for n, (x, y) in enumerate(passes((UHI, ULO), w)):
                                last = pe.matmul(o[:, c * P:(c + 1) * P], x[:, k, c * P:(c + 1) * P], y[:, k, :],
                                                 start=(k == n == 0), stop=(k == ND - 1 and n == 2))
                else:
                    for h in range(2):
                        for k in range(ND):
                            for n, (x, y) in enumerate(passes(w, (UHI, ULO))):
                                last = pe.matmul(o[:, h * HALF:(h + 1) * HALF], x[:, k, :],
                                                 y[:, k, h * HALF:(h + 1) * HALF],
                                                 start=(k == n == 0), stop=(k == ND - 1 and n == 2))
                last.then_inc(s_proj, 1)

            def pe_mean(pe, o, v, s):
                for h in range(2):
                    last = pe.matmul(o[:, h * HALF:(h + 1) * HALF], mean, v[:, h * HALF:(h + 1) * HALF],
                                     start=True, stop=True)
                last.then_inc(s, 1)

            def pe_conv_mean(pe, c):
                pe.wait_ge(s_conv, c + 1)
                pe_mean(pe, LOW, ACC, s_mu)

            def pe_conv_var(pe, c):
                pe.wait_ge(s_csq, c + 1)
                pe_mean(pe, HIGH, SQ, s_cvar)

            def pe_level(pe, i, p, level):
                if level == LEVELS:
                    keys, queries = KEYS[p], QUERIES[p]
                else:
                    pe.wait_ge(s_qk, LEVELS * i + level + 1)
                    keys = queries = QK[level % 2]
                if level == 4:
                    pe.wait_ge(s_amask, (LEVELS + 1) * i + 4)
                elif level >= 2:
                    pe.wait_ge(s_amask, (LEVELS + 1) * i + level - 1 + (level >= 6))
                o = LEVEL_PAIR[level]
                for c in range(NT):
                    last = pe.matmul(o[:, c * P:(c + 1) * P], keys[:, c * P:(c + 1) * P],
                                     queries[:, c * P:(c + 1) * P], start=True, stop=True)
                last.then_inc(s_aprod, 1)

            def pe_head(pe, i, p, conv, fill):
                later = not (isinstance(i, int) and i == 0)
                fill(2)
                if later:
                    pe.wait_ge(s_ohead, i)
                pe_level(pe, i, p, 0)
                fill(3)
                pe_level(pe, i, p, 1)
                fill(4)
                pe_level(pe, i, p, 2)
                fill(5)
                pe_level(pe, i, p, 3)
                if conv:
                    pe.wait_ge(s_amask, (LEVELS + 1) * i + 3)
                    pe_conv_mean(pe, i + 1)
                pe_level(pe, i, p, 4)
                if conv:
                    pe.wait_ge(s_cent, i + 2)
                else:
                    pe.wait_ge(s_amask, (LEVELS + 1) * i + 3)
                pe_level(pe, i, p, 5)
                if conv:
                    pe.wait_ge(s_amask, (LEVELS + 1) * i + 5)
                    pe_conv_var(pe, i + 1)
                pe_level(pe, i, p, 6)
                if conv:
                    pe.wait_ge(s_croot, i + 2)
                else:
                    pe.wait_ge(s_amask, (LEVELS + 1) * i + 5)
                pe_level(pe, i, p, 7)
                fill(6)
                pe.wait_ge(s_amask, (LEVELS + 1) * (i + 1))
                pe.wait_ge(s_kd, i + 1)
                for c in range(NT):
                    last = pe.transpose(LOW[:, c * P:(c + 1) * P], KEYS[p][:, c * P:(c + 1) * P], ident)
                last.then_inc(s_kdt, 1)
                pe.wait_ge(s_kdec, i + 1)
                for c in range(NT):
                    last = pe.matmul(HIGH[:, c * P:(c + 1) * P], KDEC[:, c, :],
                                     VALUES[p][:, c * P:(c + 1) * P], start=True, stop=True)
                last.then_inc(s_dstate, 1)
                fill(7)
                pe.wait_ge(s_state, i + 1)
                for c in range(NT):
                    o = LOW[:, c * P:(c + 1) * P]
                    last = pe.matmul(o, VALUES[p][:, c * P:(c + 1) * P], WEIGHTS[:, c, :], start=True, stop=(c == 0))
                    if c:
                        last = pe.matmul(o, STATE[:, c, :], QDEC[:, c * P:(c + 1) * P], start=False, stop=True)
                last.then_inc(s_o, 1)
                pe.wait_ge(s_osq, i + 1)
                pe_mean(pe, HIGH, HSQ, s_oms)

            def head_loop(eng, body):
                body(0, 0, 2)
                body(1, 1, 2)
                with eng.Fori(1, ND // 2 - 1) as pair:
                    body(2 * pair, 0, 2)
                    body(2 * pair + 1, 1, 2)
                body(ND - 2, 0, 1)
                body(ND - 1, 1, 0)


            @block.tensor
            def _(pe):
                pe.wait_ge(s_tables, 32)
                for s in range(NPROJ):
                    pe_project(pe, 0, s)
                pe_project(pe, 1, 0)
                pe_project(pe, 1, 1)
                pe_conv_mean(pe, 0)
                pe_conv_var(pe, 0)
                pe.wait_ge(s_croot, 1)

                def body(i, p, later):
                    def fill(n):
                        if n // NPROJ < later:
                            pe_project(pe, i + 1 + n // NPROJ, n % NPROJ)
                    pe_head(pe, i, p, later > 0, fill)

                head_loop(pe, body)

            @block.scalar
            def _(act):
                def upper(j, s):
                    act.wait_ge(s_wland[s % 2], 48 * j + 16 * (s // 2) + 16)
                    split_hi(act, WHI[s % 2][:], WRAW[s % 2]).then_inc(s_whi, 1)

                def evacuate(j, s, p):
                    pair = banks(2 * (s % 2))
                    act.wait_ge(s_proj, NPROJ * j + s + 1)
                    later = not (isinstance(j, int) and j == 0)
                    if s == 1:
                        act.activation(GLU, pair, ACT.Sigmoid).then_inc(s_glu, 1)
                    if s == 2:
                        if later:
                            act.wait_ge(s_cum, j)
                        act.activation(FORGET, pair, ACT.Sigmoid)
                        act.activation(KEYS[p], pair, ACT.Sigmoid, scale=-1.0).then_inc(s_evac, 1)
                        act.drain()
                        act.activation(FORGET, FORGET, ACT.Ln, scale=lslack[:, ds(j, 1)],
                                       bias=lbound[:, ds(j, 1)]).then_inc(s_logf, 1)
                    if s == 3:
                        act.activation(QUERIES[p], pair, ACT.Silu).then_inc(s_evac, 1)
                    if s == 4:
                        act.activation(VALUES[p], pair, ACT.Copy).then_inc(s_evac, 1)
                    if s == 5:
                        act.activation(GATE_S[p], pair, ACT.Silu).then_inc(s_evac, 1)
                    if not (isinstance(j, int) and NPROJ * j + s + 2 >= NPROJ * ND):
                        upper(j + (s + 2) // NPROJ, (s + 2) % NPROJ)

                def inverse_root(v, src, done):
                    act.activation(v, src, ACT.Ln, bias=eps)
                    act.drain()
                    act.activation(v, v, ACT.Exp, scale=-0.5).then_inc(done, 1)

                def conv_out(c, p):
                    act.wait_ge(s_cnorm, c + 1)
                    if not (isinstance(c, int) and c < 2):
                        act.wait_ge(s_ctst[p], 8 * (c - p))
                        hold(act)
                    act.activation(COUT[p], ACC, ACT.Silu,
                                   scale=col("cnorm_g", c), bias=col("cnorm_b", c)).then_inc(s_cout, 1)

                def decay(i, n):
                    act.wait_ge(s_diff, (LEVELS + 1) * i + n + 1)
                    act.activation(DECAY[n % 2], DECAY[n % 2], ACT.Exp).then_inc(s_dexp, 1)

                def begin(i):
                    act.wait_ge(s_cum, i + 1)
                    act.activation(CUMEXP, CUM, ACT.Exp).then_inc(s_dexp, 1)
                    decay(i, 0)
                    decay(i, 1)

                def body(i, p, later):
                    def fill(n):
                        if n // NPROJ < later:
                            q = (p + 1 + n // NPROJ) % 2
                            evacuate(i + 1 + n // NPROJ, n % NPROJ, q)

                    def decays(*ns):
                        for n in ns:
                            decay(i, n)

                    fill(2)
                    decays(2)
                    fill(3)
                    decays(3)
                    fill(4)
                    decays(4)
                    fill(5)
                    if later:
                        act.wait_ge(s_cent, i + 2)
                        act.activation(SQ, ACC, ACT.Square).then_inc(s_csq, 1)
                    decays(5, 6)
                    if later:
                        act.wait_ge(s_cvar, i + 2)
                        inverse_root(SQ, HIGH, s_croot)
                    decays(7)
                    if later:
                        conv_out(i + 1, 1 - p)
                    fill(6)
                    act.wait_ge(s_kdt, i + 1)
                    act.activation(KDEC.rearrange("p c k -> p (c k)"), LOW, ACT.Copy).then_inc(s_kdec, 1)
                    if later:
                        begin(i + 1)
                    fill(7)
                    act.wait_ge(s_o, i + 1)
                    act.activation(HSQ, LOW, ACT.Square).then_inc(s_osq, 1)
                    act.wait_ge(s_oms, i + 1)
                    inverse_root(HSQ, HIGH, s_oroot)

                act.wait_ge(s_epsv, 1)
                upper(0, 0)
                upper(0, 1)
                for s in range(NPROJ):
                    evacuate(0, s, 0)
                evacuate(1, 0, 1)
                evacuate(1, 1, 1)
                act.wait_ge(s_cent, 1)
                act.activation(SQ, ACC, ACT.Square).then_inc(s_csq, 1)
                act.wait_ge(s_cvar, 1)
                inverse_root(SQ, HIGH, s_croot)
                conv_out(0, 0)
                begin(0)
                head_loop(act, body)

            @block.gpsimd
            def _(pool):
                def lower(j, s):
                    pool.wait_ge(s_whi, NPROJ * j + s + 1)
                    split_lo(pool, WLO[s % 2][:], WRAW[s % 2], WHI[s % 2][:]).then_inc(s_wlo, 1)

                def store_conv(c, p):
                    pool.wait_ge(s_cout, c + 1)
                    hold(pool)
                    pool.dma_start(ct_dram[ds(c, 1)].rearrange("a p t -> p (a t)"), COUT[p]).then_inc(s_ctst[p], 16)

                def store_head(i, p):
                    pool.wait_ge(s_ohead, i + 1)
                    hold(pool)
                    pool.dma_start(yh_dram[ds(i, 1)].rearrange("a p t -> p (a t)"), HOUT[p]).then_inc(s_yhst[p], 16)

                def differences(level):
                    size = 1 << level
                    b, d = split(CUM, size), split(DECAY[level % 2], size)
                    pivot = b[:, :, 0, size - 1:size].to_broadcast([P, T // (2 * size), size])
                    pool.tensor_tensor(d[:, :, 1, :], b[:, :, 1, :], pivot, ALU.subtract)
                    pool.tensor_tensor(d[:, :, 0, :], pivot, b[:, :, 0, :], ALU.subtract).then_inc(s_diff, 1)

                def begin(i):
                    pool.wait_ge(s_cum, i + 1)
                    hold(pool)
                    differences(0)
                    differences(1)

                def body(i, p, later):
                    def ahead(n):
                        if (n + 2) // NPROJ < later:
                            lower(i + 1 + (n + 2) // NPROJ, (n + 2) % NPROJ)

                    for level in range(2, LEVELS):
                        pool.wait_ge(s_qk, LEVELS * i + level - 1)
                        differences(level)
                        if level == 2 and not (isinstance(i, int) and i == 0):
                            store_head(i - 1, 1 - p)
                        if level < LEVELS - 1:
                            ahead(level)
                    pool.wait_ge(s_qk, LEVELS * i + LEVELS - 1)
                    b = chunks(CUM)
                    pool.tensor_tensor(chunks(DECAY[LEVELS % 2]), b[:, :, P - 1:P].to_broadcast([P, NT, P]), b,
                                       ALU.subtract).then_inc(s_diff, 1)
                    pool.wait_ge(s_dexp, (LEVELS + 2) * (i + 1))
                    pool.wait_ge(s_aprod, (LEVELS + 1) * (i + 1))
                    pool.tensor_tensor(KEYS[p], KEYS[p], DECAY[LEVELS % 2], ALU.mult).then_inc(s_kd, 1)
                    if later:
                        store_conv(i + 1, 1 - p)
                    ahead(6)
                    if later:
                        begin(i + 1)
                    ahead(7)

                pool.memset(eps, EPS).then_inc(s_epsv, 1)
                for s in range(NPROJ):
                    lower(0, s)
                lower(1, 0)
                lower(1, 1)
                lower(1, 2)
                lower(1, 3)
                store_conv(0, 0)
                begin(0)
                head_loop(pool, body)
                store_head(ND - 1, 1)

            TAPS = [4, 11, 18, 25, CONV_K]

            @block.vector
            def _(dve):
                def pad(c):
                    dve.drain()
                    dve.wait_ge(s_glu, c + 1)
                    hold(dve)
                    dve.tensor_tensor(PAD[:, CONV_K - 1:], banks(0), GLU, ALU.mult).then_inc(s_evac, 2)

                def begin(i, p):
                    dve.wait_ge(s_logf, i + 1)
                    hold(dve)
                    dve.tensor_tensor_scan(CUM, RESTART, FORGET, 0.0, ALU.mult, ALU.add).then_inc(s_cum, 1)
                    dve.wait_ge(s_evac, NPROJ * i + 4)
                    hold(dve)
                    dve.tensor_scalar(KEYS[p], KEYS[p], lslack[:, ds(i, 1)], None, ALU.mult)

                def first_taps(c):
                    dve.wait_ge(s_cout, c)
                    hold(dve)
                    taps(c, 0, TAPS[0])

                def taps(c, first, end):
                    for k in range(first, end):
                        dve.drain()
                        if k == 0:
                            last = dve.tensor_scalar(ACC, PAD[:, 0:T], col("conv_w", c, 0), col("conv_b", c),
                                                     ALU.mult, ALU.add)
                        else:
                            last = dve.scalar_tensor_tensor(ACC, PAD[:, k:k + T], col("conv_w", c, k), ACC,
                                                            ALU.mult, ALU.add)
                    if end == CONV_K:
                        last.then_inc(s_conv, 1)

                def centre(c):
                    dve.wait_ge(s_mu, c + 1)
                    dve.tensor_tensor(ACC, ACC, LOW, ALU.subtract).then_inc(s_cent, 1)

                def norm(c):
                    dve.wait_ge(s_croot, c + 1)
                    dve.tensor_tensor(ACC, ACC, SQ, ALU.mult).then_inc(s_cnorm, 1)

                def body(i, p, later):
                    dve.wait_ge(s_dexp, (LEVELS + 2) * i + 1)
                    dve.tensor_tensor(QDEC, QUERIES[p], CUMEXP, ALU.mult)
                    dve.drain()

                    def masked(level):
                        dve.drain()
                        dve.wait_ge(s_aprod, (LEVELS + 1) * i + level + 1)
                        hold(dve)
                        dve.copy_predicated(WEIGHTS, MASKS[:, level:level + 1, :].to_broadcast([P, NT, P]),
                                            chunks(LEVEL_PAIR[level])).then_inc(s_amask, 1)

                    for level in range(LEVELS):
                        size = 1 << level
                        dve.wait_ge(s_dexp, (LEVELS + 2) * i + level + 2)
                        if level >= 2:
                            dve.wait_ge(s_aprod, (LEVELS + 1) * i + level - 1)
                        qk, e = split(QK[level % 2], size), split(DECAY[level % 2], size)
                        dve.tensor_tensor(qk[:, :, 1, :], split(QUERIES[p], size)[:, :, 1, :], e[:, :, 1, :], ALU.mult)
                        dve.tensor_tensor(qk[:, :, 0, :], split(KEYS[p], size)[:, :, 0, :], e[:, :, 0, :],
                                          ALU.mult).then_inc(s_qk, 1)
                        if later and level < 4:
                            taps(i + 1, TAPS[level], TAPS[level + 1])
                        if level:
                            masked(level - 1)
                        if later and level == 4:
                            centre(i + 1)
                    masked(LEVELS - 1)
                    if later:
                        norm(i + 1)
                    masked(LEVELS)
                    dve.wait_ge(s_dstate, i + 1)
                    dstate = chunks(HIGH)
                    dve.tensor_copy(STATE[:, 1, :], dstate[:, 0, :])
                    for c in range(1, NT - 1):
                        dve.drain()
                        last = dve.scalar_tensor_tensor(STATE[:, c + 1, :], STATE[:, c, :],
                                                        CUMEXP[:, c * P + P - 1:c * P + P], dstate[:, c, :],
                                                        ALU.mult, ALU.add)
                    last.then_inc(s_state, 1)
                    if later:
                        begin(i + 1, 1 - p)
                    if later == 2:
                        pad(i + 2)
                        first_taps(i + 2)
                    dve.wait_ge(s_oroot, i + 1)
                    if not (isinstance(i, int) and i < 2):
                        dve.wait_ge(s_yhst[p], 8 * (i - p))
                        hold(dve)
                    dve.tensor_tensor(HOUT[p], LOW, HSQ, ALU.mult)
                    dve.drain()
                    dve.scalar_tensor_tensor(HOUT[p], HOUT[p], col("onorm_g", i), GATE_S[p], ALU.mult,
                                             ALU.mult).then_inc(s_ohead, 1)

                dve.memset(PAD[:, 0:CONV_K - 1], 0.0)
                dve.wait_ge(s_tables, 32)
                dve.tensor_copy(MASKS[:], WEIGHTS)
                dve.drain()
                dve.memset(WEIGHTS, 0.0)
                pad(0)
                begin(0, 0)
                taps(0, 0, CONV_K)
                pad(1)
                centre(0)
                norm(0)
                first_taps(1)
                head_loop(dve, body)

        CONVOUT = part(0, (ND, T))
        HTOK = part(8 * T, (NT, T))
        PTOK = part(22 * T, (NT, 256))
        FINAL_G = part(24 * T, (T,))
        W2HI = [rounded(f"W2HI{k}", "arena", (18 + k) * T, [P, ND, P]) for k in range(2)]
        W2LO = [rounded(f"W2LO{k}", "arena", (16 + k) * T, [P, ND, P]) for k in range(2)]
        NPAIR = ND // 2
        CHI, CLO = UHI, ULO

        s_w2hi = sem("s_w2hi")
        s_w2lo = sem("s_w2lo")
        s_proj2 = sem("s_proj2")
        s_silu = sem("s_silu")
        s_cgated = sem("s_cgated")
        s_cland = sem("s_cland")
        s_chi = sem("s_chi")
        s_clo = sem("s_clo")
        s_x3 = sem("s_x3")
        s_yland = sem("s_yland")
        s_ptok = sem("s_ptok")
        s_wpp = sem("s_wpp")

        with nc.Block() as block:
            @block.sync
            def _(sp):
                def pair(b, second):
                    for k in range(2):
                        sp.wait_ge(s_w2lo, 2 * b + k - 1)
                        hold(sp)
                        load_second(sp, b, k + 2 * second)

                for p in range(2):
                    sp.wait_ge(s_ctst[p], 16 * ND // 2)
                    sp.wait_ge(s_yhst[p], 16 * ND // 2)
                sp.dma_start(RC[:], ct_dram.rearrange("j p t -> p j t")).then_inc(s_cland, 16)
                with sp.Fori(1, NPAIR) as b:
                    pair(b, 0)
                sp.dma_start(HTOK, a["x"].rearrange("o (m p) d -> p (o m) d", p=P)).then_inc(s_x3, 16)
                sp.dma_start(PTOK, a["p"].rearrange("l o (m p) d -> p (l o m) d", p=P)).then_inc(s_ptok, 16)
                sp.dma_start(FINAL_G, a["final_g"].rearrange("(o d) -> o d", o=1).to_broadcast([P, D])
                             ).then_inc(s_wpp, 16)
                with sp.Fori(NPAIR, 2 * NPAIR) as b:
                    pair(b, 1)
                sp.wait_ge(s_clo, ND)
                sp.dma_start(RC[:], yh_dram.rearrange("j p t -> p j t")).then_inc(s_yland, 16)

            @block.tensor
            def _(pe):
                def project(b, k):
                    pe.wait_ge(s_w2lo, 2 * b + k + 1)
                    for h in range(2):
                        for j in range(ND):
                            for n, (x, y) in enumerate(passes((W2HI[k], W2LO[k]), (UHI, ULO))):
                                last = pe.matmul(banks(2 * k)[:, h * HALF:(h + 1) * HALF], x[:, j, :],
                                                 y[:, j, h * HALF:(h + 1) * HALF],
                                                 start=(j == n == 0), stop=(j == ND - 1 and n == 2))
                    last.then_inc(s_proj2, 1)

                project(0, 0)
                project(0, 1)
                with pe.Fori(1, NPAIR) as b:
                    for k in range(2):
                        pe.wait_ge(s_silu, 2 * b + k - 1)
                        project(b, k)
                pe.wait_ge(s_silu, ND - 1)
                pe.wait_ge(s_w2lo, ND + 1)
                for j in range(ND):
                    pe.wait_ge(s_clo, j + 1)
                    for h in range(2):
                        for n, (x, y) in enumerate(passes((W2HI[0], W2LO[0]), (CHI, CLO))):
                            last = pe.matmul(banks(0)[:, h * HALF:(h + 1) * HALF], x[:, j, :],
                                             y[:, j, h * HALF:(h + 1) * HALF],
                                             start=(j == n == 0), stop=(j == ND - 1 and n == 2))
                last.then_inc(s_proj2, 1)
                pe.wait_ge(s_silu, ND)
                project(NPAIR, 1)
                with pe.Fori(NPAIR + 1, 2 * NPAIR) as b:
                    for k in range(2):
                        pe.wait_ge(s_cgated, 2 * b + k - 1 - ND)
                        project(b, k)

            @block.scalar
            def _(act):
                def upper(b, k):
                    act.wait_ge(s_w2land[k], 16 * b + 16)
                    split_hi(act, W2HI[k][:], W2RAW[k]).then_inc(s_w2hi, 1)

                def gate(b, k):
                    act.wait_ge(s_proj2, 2 * b + k + 1)
                    act.activation(CONVOUT[:, ds(2 * b + k, 1), :].rearrange("p a t -> p (a t)"),
                                   banks(2 * k), ACT.Silu).then_inc(s_silu, 1)

                upper(0, 0)
                upper(0, 1)
                with act.Fori(0, NPAIR - 1) as b:
                    for k in range(2):
                        gate(b, k)
                        upper(b + 1, k)
                gate(NPAIR - 1, 0)
                upper(NPAIR, 0)
                act.wait_ge(s_proj2, ND)
                act.wait_ge(s_cland, 16)
                for j in range(ND):
                    split_hi(act, CHI[:, j, :], RC[:, j, :]).then_inc(s_chi, 1)
                gate(NPAIR - 1, 1)
                upper(NPAIR, 1)
                with act.Fori(NPAIR + 1, 2 * NPAIR) as b:
                    for k in range(2):
                        act.wait_ge(s_proj2, 2 * b + k - 1)
                        hold(act)
                        upper(b, k)

            @block.vector
            def _(dve):
                def lower(b, k):
                    dve.wait_ge(s_w2hi, 2 * b + k + 1)
                    split_lo(dve, W2LO[k][:], W2RAW[k], W2HI[k][:]).then_inc(s_w2lo, 1)

                def product(b, k):
                    dve.wait_ge(s_proj2, 2 * b + k + 1)
                    hold(dve)
                    gate = CONVOUT[:, ds(2 * b + k - ND, 1), :].rearrange("p a t -> p (a t)")
                    dve.scalar_tensor_tensor(gate, banks(2 * k), col("b_pw2", 2 * b + k - ND), gate,
                                             ALU.add, ALU.mult).then_inc(s_cgated, 1)

                with dve.Fori(0, NPAIR) as b:
                    lower(b, 0)
                    lower(b, 1)
                lower(NPAIR, 0)
                for j in range(ND):
                    dve.wait_ge(s_chi, j + 1)
                    split_lo(dve, CLO[:, j, :], RC[:, j, :], CHI[:, j, :]).then_inc(s_clo, 1)
                lower(NPAIR, 1)
                dve.wait_ge(s_silu, ND)
                with dve.Fori(NPAIR, 2 * NPAIR - 1) as b:
                    for k in range(2):
                        product(b, k)
                        lower(b + 1, k)
                product(2 * NPAIR - 1, 0)
                product(2 * NPAIR - 1, 1)

        SQUARES = sb("SQUARES", [P, T])
        PFEAT = part(20 * T, (2, T))
        WPP = part(22 * T, (2, T))
        BRANCH = CONVOUT, RC
        BHI = rounded("CONVHI", "RA", 0, [P, ND, T]), rounded("YHI", "RB", 0, [P, ND, T])
        BLO = rounded("CONVLO", "arena", 0, [P, ND, T]), rounded("YLO", "RC", 0, [P, ND, T])
        NRAW = 4

        def stream_buffers(name, where, floats):
            raw = [(part(floats + k * HALF, (HALF,)) if where == "arena" else
                    RA[:, (floats + k * HALF) // T, k % 2 * HALF:(k % 2 + 1) * HALF]) for k in range(NRAW)]
            hi, lo = ([rounded(f"{name}{w}{k}", where, floats + (NRAW + 2 * n + k) * HALF, [P, HALF])
                       for k in range(2)] for n, w in enumerate(("HI", "LO")))
            return raw, hi, lo

        W3RAW, W3HI, W3LO = stream_buffers("W3", "arena", 16 * T)
        s_w3land = [sem(f"s_w3land{k}") for k in range(NRAW)]
        s_w3hi = sem("s_w3hi")
        s_w3lo = sem("s_w3lo")
        s_w3used = sem("s_w3used")
        s_bhi = sem("s_bhi")
        s_blo = sem("s_blo")
        s_hprod = sem("s_hprod")
        s_h = sem("s_h")
        s_pturn = sem("s_pturn")
        s_pfeat = sem("s_pfeat")
        s_hss = sem("s_hss")
        s_hvar = sem("s_hvar")
        s_hroot = sem("s_hroot")

        def stream_load(sp, n, src, k, h, raw, land, lo):
            if n >= NRAW:
                sp.wait_ge(lo, n - NRAW + 1)
            sp.dma_start(raw[n % NRAW], src[0, k * P:(k + 1) * P, h * HALF:(h + 1) * HALF]
                         ).then_inc(land[n % NRAW], 16)

        def stream_hi(act, n, raw, hi, land, used, done):
            act.wait_ge(land[n % NRAW], 16 * (n // NRAW) + 16)
            if n >= 2:
                act.wait_ge(used, n - 1)
            split_hi(act, hi[n % 2][:], raw[n % NRAW]).then_inc(done, 1)

        def stream_lo(dve, n, raw, hi, lo, his, done):
            dve.wait_ge(his, n + 1)
            split_lo(dve, lo[n % 2][:], raw[n % NRAW], hi[n % 2][:]).then_inc(done, 1)

        with nc.Block() as block:
            @block.sync
            def _(sp):
                for n in range(4 * ND):
                    stream_load(sp, n, a["w_out"], n % (2 * ND), n // (2 * ND), W3RAW, s_w3land, s_w3lo)
                    if n == NRAW:
                        sp.wait_ge(s_pturn, 1)
                        sp.dma_start(WPP, a["w_pp"].rearrange("o (k p) n -> p (o k) n", p=P)).then_inc(s_wpp, 16)

            @block.tensor
            def _(pe):
                pe.wait_ge(s_ptok, 16)
                for k in range(2):
                    for m in range(NT):
                        last = pe.transpose(banks(4 + 2 * k)[:, m * P:(m + 1) * P],
                                            PTOK[:, m, k * P:(k + 1) * P], ident)
                last.then_inc(s_pturn, 1)
                pe.wait_ge(s_pfeat, 2)
                for n in range(4 * ND):
                    h, k = n // (2 * ND), n % (2 * ND)
                    pe.wait_ge(s_w3lo, n + 1)
                    if h == 0:
                        pe.wait_ge(s_blo, k + 1)
                    lhs = BHI[k // ND], BLO[k // ND]
                    for m in range(NT):
                        if h and k == 0:
                            pe.wait_ge(s_h, m + 1)
                        for i, (x, y) in enumerate(passes(lhs, (W3HI[n % 2], W3LO[n % 2]))):
                            last = pe.matmul(PS[:, m, :], x[:, k % ND, m * P:(m + 1) * P], y[:],
                                             start=(k == i == 0), stop=(k == 2 * ND - 1 and i == 2))
                        if k == 2 * ND - 1:
                            last.then_inc(s_hprod, 1)
                    if k < 2 * ND - 1:
                        last.then_inc(s_w3used, 1)
                    else:
                        pe.drain()
                        pe.nop().then_inc(s_w3used, 1)

            @block.vector
            def _(dve):
                dve.wait_ge(s_pturn, 1)
                dve.tensor_copy(PFEAT[:, 0, :], banks(4)).then_inc(s_pfeat, 1)
                dve.wait_ge(s_x3, 16)

                def sums(h):
                    for m in range(NT):
                        dve.wait_ge(s_hprod, NT * h + m + 1)
                        r = HTOK[:, m, h * HALF:(h + 1) * HALF]
                        dve.tensor_tensor(r, PS[:, m, :], r, ALU.add).then_inc(s_h, 1)

                for n in range(4 * ND):
                    if n < 2 * ND:
                        dve.wait_ge(s_bhi, n + 1)
                        c, k = n // ND, n % ND
                        split_lo(dve, BLO[c][:, k, :], BRANCH[c][:, k, :], BHI[c][:, k, :]).then_inc(s_blo, 1)
                    stream_lo(dve, n, W3RAW, W3HI, W3LO, s_w3hi, s_w3lo)
                    if n == 2 * ND:
                        sums(0)
                sums(1)
                dve.wait_ge(s_hss, 1)
                dve.tensor_scalar(meansq, sumsq, 1.0 / D, EPS, ALU.mult, ALU.add).then_inc(s_hvar, 1)
                dve.wait_ge(s_hroot, 1)
                dve.reciprocal(rstd, root)

            @block.scalar
            def _(act):
                act.wait_ge(s_pturn, 1)
                act.activation(PFEAT[:, 1, :], banks(6), ACT.Copy).then_inc(s_pfeat, 1)

                def upper(n):
                    if n == ND:
                        act.wait_ge(s_yland, 16)
                    split_hi(act, BHI[n // ND][:, n % ND, :], BRANCH[n // ND][:, n % ND, :]).then_inc(s_bhi, 1)

                upper(0)
                for n in range(4 * ND):
                    stream_hi(act, n, W3RAW, W3HI, s_w3land, s_w3used, s_w3hi)
                    if n + 1 < 2 * ND:
                        upper(n + 1)
                for m in range(NT):
                    act.wait_ge(s_h, NT + m + 1)
                    act.activation(SQUARES[:], HTOK[:, m, :], ACT.Square,
                                   accum_out=sumsq[:, m:m + 1])
                    act.drain()
                act.nop().then_inc(s_hss, 1)
                act.wait_ge(s_hvar, 1)
                act.activation(root, meansq, ACT.Sqrt).then_inc(s_hroot, 1)

        retire(s_wpp, s_held)
        x1_dram = nc.dram_tensor("x1_dram", [NT, P, D], F32).ap()
        NORMED = [part((16 + k) * T, (T,)) for k in range(2)]
        GATES = [part(18 * T + k * HALF, (HALF,)) for k in range(2)]
        PETOK = part(0, (NT, T))
        TURNED = [RA[:, 4 + k, :].rearrange("p (c t) -> p c t", c=ND) for k in range(3)]
        NHI, NLO = rounded("NHI", "RB", 0, [P, ND, T]), rounded("NLO", "RC", 0, [P, ND, T])
        W4RAW, W4HI, W4LO = stream_buffers("W4", "RA", 0)
        s_w4land = [sem(f"s_w4land{k}") for k in range(NRAW)]
        s_w4hi = sem("s_w4hi")
        U2HI, U2LO = rounded("U2HI", "RC", 0, [P, ND, T]), rounded("U2LO", "RB", 0, [P, ND, T])
        s_u2hi = sem("s_u2hi")
        s_w4lo = sem("s_w4lo")
        s_w4used = sem("s_w4used")
        s_nhi = sem("s_nhi")
        s_nlo = sem("s_nlo")
        s_peprod = sem("s_peprod")
        s_petok = sem("s_petok")
        s_normed = sem("s_normed")
        s_nturn = sem("s_nturn")
        s_hnt = sem("s_hnt")
        s_gprod = sem("s_gprod")
        s_gsig = sem("s_gsig")
        s_h1 = sem("s_h1")
        s_x1 = sem("s_x1")
        s_st = [sem(f"s_st{k}") for k in range(3)]
        s_u2n = sem("s_u2n")
        s_u2turn = sem("s_u2turn")
        s_u2t = sem("s_u2t")
        s_x1st = sem("s_x1st")

        def root_mean_square(act, ready, before_them, n, src):
            for m in range(NT):
                act.wait_ge(ready, before_them + m + 1)
                act.activation(SQUARES[:], src[:, m, :], ACT.Square, accum_out=sumsq[:, m:m + 1])
                act.drain()
            act.nop().then_inc(s_st[0], 1)
            act.wait_ge(s_st[1], n)
            act.activation(root, meansq, ACT.Sqrt).then_inc(s_st[2], 1)

        def reciprocal_roots(dve, n):
            dve.wait_ge(s_st[0], n)
            dve.tensor_scalar(meansq, sumsq, 1.0 / D, EPS, ALU.mult, ALU.add).then_inc(s_st[1], 1)
            dve.wait_ge(s_st[2], n)
            dve.reciprocal(rstd, root)
            dve.drain()

        def pe_turn(pe, dst, src, done):
            for c in range(ND):
                last = pe.transpose(dst[:, c * P:(c + 1) * P], src[:, c * P:(c + 1) * P], ident)
            last.then_inc(done, 1)

        def gain_of(name):
            r = ROWS[name]
            return cols[:, :, r:r + 1].to_broadcast([P, ND, P])

        with nc.Block() as block:
            @block.sync
            def _(sp):
                for n in range(2 * ND):
                    stream_load(sp, n, a["w_pg"], n % ND, n // ND, W4RAW, s_w4land, s_w4lo)
                for m in range(NT):
                    sp.wait_ge(s_x1, m + 1)
                    sp.dma_start(x1_dram[m], HTOK[:, m, :]).then_inc(s_x1st, 16)
                sp.wait_ge(s_x1st, 16 * NT)

            @block.tensor
            def _(pe):
                pe.wait_ge(s_wpp, 32)
                for m in range(NT):
                    if m >= 2:
                        pe.wait_ge(s_petok, m - 1)
                    for h in range(2):
                        for k in range(2):
                            last = pe.matmul(banks(4 + 2 * (m % 2))[:, h * HALF:(h + 1) * HALF],
                                             PFEAT[:, k, m * P:(m + 1) * P], WPP[:, k, h * HALF:(h + 1) * HALF],
                                             start=(k == 0), stop=(k == 1))
                    last.then_inc(s_peprod, 1)
                for m in range(NT):
                    pe.wait_ge(s_normed, m + 1)
                    if m >= 2:
                        pe.wait_ge(s_hnt, m - 1)
                    pe_turn(pe, banks(2 * (m % 2)), NORMED[m % 2], s_nturn)
                pe.wait_ge(s_hnt, NT)
                pe.wait_ge(s_petok, NT)
                pe.wait_ge(s_nlo, NT)
                for n in range(2 * ND):
                    h, k = n // ND, n % ND
                    pe.wait_ge(s_w4lo, n + 1)
                    for m in range(NT):
                        if h and k == 0:
                            pe.wait_ge(s_gsig, m + 1)
                        for i, (x, y) in enumerate(passes((NHI, NLO), (W4HI[n % 2], W4LO[n % 2]))):
                            last = pe.matmul(PS[:, m, :], x[:, k, m * P:(m + 1) * P], y[:],
                                             start=(k == i == 0), stop=(k == ND - 1 and i == 2))
                        if k == ND - 1:
                            last.then_inc(s_gprod, 1)
                    if k < ND - 1:
                        last.then_inc(s_w4used, 1)
                    else:
                        pe.drain()
                        pe.nop().then_inc(s_w4used, 1)
                pe.wait_ge(s_gsig, 2 * NT)
                for m in range(NT):
                    pe.wait_ge(s_u2n, m + 1)
                    if m >= 2:
                        pe.wait_ge(s_u2t, m - 1)
                    pe_turn(pe, banks(2 * (m % 2)), NORMED[m % 2], s_u2turn)

            @block.scalar
            def _(act):
                def upper(m):
                    act.wait_ge(s_hnt, m + 1)
                    split_hi(act, NHI[:, :, m * P:(m + 1) * P], TURNED[m % 3]).then_inc(s_nhi, 1)

                stream_hi(act, 0, W4RAW, W4HI, s_w4land, s_w4used, s_w4hi)
                stream_hi(act, 1, W4RAW, W4HI, s_w4land, s_w4used, s_w4hi)
                for m in range(NT):
                    act.wait_ge(s_peprod, m + 1)
                    act.activation(PETOK[:, m, :], banks(4 + 2 * (m % 2)), ACT.Copy).then_inc(s_petok, 1)
                for m in range(NT):
                    upper(m)

                def square(m):
                    act.wait_ge(s_h1, NT + m + 1)
                    act.drain()
                    act.activation(SQUARES[:], HTOK[:, m, :], ACT.Square, accum_out=sumsq[:, m:m + 1])
                    act.drain()

                def gates(h):
                    for m in range(NT):
                        n = NT * h + m
                        act.wait_ge(s_gprod, n + 1)
                        if n >= 2:
                            act.wait_ge(s_h1, n - 1)
                        act.activation(GATES[m % 2], PS[:, m, :], ACT.Sigmoid).then_inc(s_gsig, 1)
                        if h and m:
                            square(m - 1)
                    if h:
                        square(NT - 1)

                for n in range(2, 2 * ND):
                    stream_hi(act, n, W4RAW, W4HI, s_w4land, s_w4used, s_w4hi)
                    if n == ND + 1:
                        gates(0)
                gates(1)
                act.nop().then_inc(s_st[0], 1)
                act.wait_ge(s_st[1], 1)
                act.activation(root, meansq, ACT.Sqrt).then_inc(s_st[2], 1)
                root_mean_square(act, s_x1, 0, 2, HTOK)
                for m in range(NT):
                    act.wait_ge(s_u2t, m + 1)
                    split_hi(act, U2HI[:, :, m * P:(m + 1) * P], TURNED[m % 3]).then_inc(s_u2hi, 1)

            @block.vector
            def _(dve):
                def evacuate(m, turned, dst, name, done):
                    dve.wait_ge(turned, m + 1)
                    dve.tensor_tensor(dst, banks(2 * (m % 2)).rearrange("p (c t) -> p c t", c=ND),
                                      gain_of(name), ALU.mult).then_inc(done, 1)

                def lower(m):
                    dve.wait_ge(s_nhi, m + 1)
                    dve.drain()
                    split_lo(dve, NLO[:, :, m * P:(m + 1) * P], TURNED[m % 3],
                             NHI[:, :, m * P:(m + 1) * P]).then_inc(s_nlo, 1)

                for m in range(NT + 1):
                    if m < NT:
                        if m >= 2:
                            dve.wait_ge(s_nturn, m - 1)
                        dve.tensor_scalar(NORMED[m % 2], HTOK[:, m, :], rstd[:, m:m + 1], None,
                                          ALU.mult).then_inc(s_normed, 1)
                    if m:
                        evacuate(m - 1, s_nturn, TURNED[(m - 1) % 3], "pe_norm_g", s_hnt)
                    if m >= 2:
                        lower(m - 2)
                lower(NT - 1)

                def add(h):
                    for m in range(NT):
                        dve.wait_ge(s_gsig, NT * h + m + 1)
                        g, c = GATES[m % 2], slice(h * HALF, (h + 1) * HALF)
                        dve.tensor_tensor(g, g, PETOK[:, m, c], ALU.mult)
                        dve.drain()
                        dve.tensor_tensor(HTOK[:, m, c], HTOK[:, m, c], g, ALU.add).then_inc(s_h1, 1)

                for n in range(2 * ND):
                    stream_lo(dve, n, W4RAW, W4HI, W4LO, s_w4hi, s_w4lo)
                    if n == ND + 1:
                        add(0)
                add(1)
                reciprocal_roots(dve, 1)
                dve.wait_ge(s_wpp, 32)
                for m in range(NT):
                    dve.scalar_tensor_tensor(HTOK[:, m, :], HTOK[:, m, :], rstd[:, m:m + 1], FINAL_G,
                                             ALU.mult, ALU.mult).then_inc(s_x1, 1)
                reciprocal_roots(dve, 2)
                for m in range(NT + 2):
                    if m < NT:
                        if m >= 2:
                            dve.wait_ge(s_u2turn, m - 1)
                        dve.tensor_scalar(NORMED[m % 2], HTOK[:, m, :], rstd[:, m:m + 1], None,
                                          ALU.mult).then_inc(s_u2n, 1)
                    if 1 <= m <= NT:
                        evacuate(m - 1, s_u2turn, TURNED[(m - 1) % 3], "norm_mix_g", s_u2t)
                    if m >= 2:
                        c = slice((m - 2) * P, (m - 1) * P)
                        dve.wait_ge(s_u2hi, m - 1)
                        dve.drain()
                        split_lo(dve, U2LO[:, :, c], TURNED[(m - 2) % 3], U2HI[:, :, c])

        NB = ND // 2
        NBLK = 48
        SURE = 2 * T // P
        y_dram = nc.dram_tensor("y_dram", [NBLK * P, D], F32).ap()
        s_filled = sem("s_filled")
        GATE0_COL = 2 * D + 768 + 256 + 32
        RPAD = [part(k * (T + 4), (T + 4,))[:, 0:T + 3] for k in range(2)]
        REC, INP, AEXP, THMUL, GELU, SIG, XA = ([part((2 + 2 * n + k) * T + 8, (T,)) for k in range(2)]
                                                for n in range(7))
        WRAW5 = [part((16 + k) * T + 8, (ND, P)) for k in range(2)]
        WHI5 = [rounded(f"WHI5{k}", "arena", (18 + k) * T + 8, [P, ND, P]) for k in range(2)]
        WLO5 = [rounded(f"WLO5{k}", "arena", (20 + k) * T + 8, [P, ND, P]) for k in range(2)]
        WAX = part(22 * T + 8, (2, 2, 256))
        CREC = [small[:, 72 + 8 * k:80 + 8 * k] for k in range(5)]
        crec = CREC[0]
        one = small[:, 65:66]
        XCOLS = [0, P, D, D + P, GATE0_COL, GATE0_COL + P]

        s_rland = [sem(f"s_rland{k}") for k in range(2)]
        s_rwhi = sem("s_rwhi")
        s_rwlo = sem("s_rwlo")
        s_ax = sem("s_ax")
        s_rproj = sem("s_rproj")
        s_revac = sem("s_revac")
        s_xa = sem("s_xa")
        s_ri = sem("s_ri")
        s_riev = sem("s_riev")
        s_la = sem("s_la")
        s_mroot = sem("s_mroot")
        s_mt = sem("s_mt")
        s_soft = sem("s_soft")
        s_softexp = sem("s_softexp")

        with nc.Block() as block:
            @block.sync
            def _(sp):
                def load(b, n):
                    w = a["w_in_2"].rearrange("o (k p) n -> p (o k) n", p=P)[:, :, ds(b * 256 + XCOLS[n], P)]
                    sp.dma_start(WRAW5[n % 2], w).then_inc(s_rland[n % 2], 16)

                def load_gates(b):
                    for i, name in enumerate(("lru_wa_2", "lru_wx_2")):
                        w = a[name].rearrange("o b (k p) n -> p (o b) k n", p=P)[:, ds(b, 1)]
                        sp.dma_start(WAX[:, i], w.rearrange("p a k n -> p (a k) n")).then_inc(s_ax, 16)

                for n in range(6):
                    if n >= 2:
                        sp.wait_ge(s_rwlo, n - 1)
                    load(0, n)
                    if n == 5:
                        for r in range(SURE * P, NBLK * P, T):
                            sp.dma_start(y_dram[r:r + T, :], x1_dram.rearrange("m p d -> (m p) d")
                                         ).then_inc(s_filled, 16)
                    if n == 2:
                        load_gates(0)
                with sp.Fori(1, NB) as b:
                    for n in range(6):
                        sp.wait_ge(s_rwlo, 6 * b + n - 1)
                        hold(sp)
                        load(b, n)
                    sp.wait_ge(s_ri, 2 * b)
                    hold(sp)
                    load_gates(b)

            @block.gpsimd
            def _(pool):
                def lower(b, n):
                    pool.wait_ge(s_rwhi, 6 * b + n + 1)
                    hold(pool)
                    split_lo(pool, WLO5[n % 2][:], WRAW5[n % 2], WHI5[n % 2][:]).then_inc(s_rwlo, 1)

                with pool.Fori(0, NB) as b:
                    for n in range(6):
                        lower(b, n)

            @block.tensor
            def _(pe):
                def project(b, n):
                    pe.wait_ge(s_rwlo, 6 * b + n + 1)
                    if n >= 2 or not isinstance(b, int):
                        pe.wait_ge(s_revac, 6 * b + n - 1)
                    o = banks(2 * (n % 2))
                    for h in range(2):
                        for k in range(ND):
                            for i, (x, y) in enumerate(passes((WHI5[n % 2], WLO5[n % 2]), (U2HI, U2LO))):
                                last = pe.matmul(o[:, h * HALF:(h + 1) * HALF], x[:, k, :],
                                                 y[:, k, h * HALF:(h + 1) * HALF],
                                                 start=(k == i == 0), stop=(k == ND - 1 and i == 2))
                    last.then_inc(s_rproj, 1)

                def gates(b, t):
                    pe.wait_ge(s_ax, 32 * b + 32)
                    pe.wait_ge(s_xa, 2 * b + 2)
                    if t or not isinstance(b, int):
                        pe.wait_ge(s_riev, 2 * b + t)
                    for i in range(2):
                        for h in range(2):
                            for k in range(2):
                                last = pe.matmul(banks(4 + 2 * i)[:, h * HALF:(h + 1) * HALF],
                                                 WAX[:, i, k, t * P:(t + 1) * P],
                                                 XA[k][:, h * HALF:(h + 1) * HALF], start=(k == 0), stop=(k == 1))
                    last.then_inc(s_ri, 1)

                def block_of(b):
                    for n in range(3):
                        project(b, n)
                    gates(b, 0)
                    project(b, 3)
                    gates(b, 1)
                    project(b, 4)
                    project(b, 5)

                block_of(0)
                with pe.Fori(1, NB) as b:
                    block_of(b)

            @block.scalar
            def _(act):
                def upper(b, n):
                    act.wait_ge(s_rland[n % 2], 48 * b + 16 * (n // 2) + 16)
                    split_hi(act, WHI5[n % 2][:], WRAW5[n % 2]).then_inc(s_rwhi, 1)

                def evacuate(b, n, more=True):
                    evacuate_one(b, n)
                    if more or n < 4:
                        upper(b + (n + 2) // 6, (n + 2) % 6)

                def evacuate_one(b, n):
                    act.wait_ge(s_rproj, 6 * b + n + 1)
                    t, pair, later = n % 2, banks(2 * (n % 2)), not (isinstance(b, int) and b == 0)
                    if n < 2:
                        if later:
                            act.wait_ge(s_xa, 2 * b)
                        act.activation(RPAD[t][:, 3:], pair, ACT.Copy).then_inc(s_revac, 1)
                    else:
                        if later:
                            act.wait_ge(s_mt, 2 * b + t - 1)
                        act.activation((GELU if n < 4 else SIG)[t], pair,
                                       ACT.Gelu_apprx_tanh if n < 4 else ACT.Sigmoid).then_inc(s_revac, 1)

                def gates(b, t):
                    act.wait_ge(s_ri, 2 * b + t + 1)
                    if not (isinstance(b, int) and b == 0):
                        act.wait_ge(s_mt, 2 * b + t - 1)
                    act.activation(REC[t], banks(4), ACT.Sigmoid, bias=col("lru_ba", 2 * b + t))
                    act.activation(INP[t], banks(6), ACT.Sigmoid, bias=col("lru_bx", 2 * b + t)).then_inc(s_riev, 1)

                def block_of(b, more=True):
                    for n in range(3):
                        evacuate(b, n)
                    gates(b, 0)
                    evacuate(b, 3)
                    gates(b, 1)
                    act.wait_ge(s_la, 2 * b + 2)
                    for t in range(2):
                        act.activation(AEXP[t], REC[t], ACT.Exp)
                    for t in range(2):
                        act.activation(THMUL[t], REC[t], ACT.Tanh, scale=-1.0)
                    act.drain()
                    for t in range(2):
                        act.activation(REC[t], THMUL[t], ACT.Ln, bias=one)
                    act.drain()
                    for t in range(2):
                        act.activation(REC[t], REC[t], ACT.Exp, scale=-0.5)
                    for t in range(2):
                        act.activation(THMUL[t], THMUL[t], ACT.Sqrt, scale=2.0).then_inc(s_mroot, 1)
                    evacuate(b, 4, more)
                    evacuate(b, 5, more)

                act.wait_ge(s_soft, 1)
                act.activation(CREC[1], CREC[1], ACT.Exp, scale=-1.0).then_inc(s_softexp, 1)
                act.wait_ge(s_soft, 2)
                act.activation(CREC[3], CREC[2], ACT.Ln).then_inc(s_softexp, 1)
                upper(0, 0)
                upper(0, 1)
                block_of(0)
                with act.Fori(1, NB - 1) as b:
                    block_of(b)
                block_of(NB - 1, False)

            @block.vector
            def _(dve):
                lam = cols[:, :, ROWS["lru_lambda"]]
                dve.tensor_scalar(CREC[0], lam, -1.0, 0.0, ALU.mult, ALU.max)
                dve.drain()
                dve.scalar_tensor_tensor(CREC[1], CREC[0], 2.0, lam, ALU.mult, ALU.add).then_inc(s_soft, 1)
                for t in range(2):
                    dve.memset(RPAD[t][:, 0:3], 0.0)
                dve.memset(one, 1.0)
                dve.wait_ge(s_softexp, 1)
                dve.tensor_scalar(CREC[2], CREC[1], 1.0, None, ALU.add).then_inc(s_soft, 1)
                dve.drain()
                dve.wait_ge(s_softexp, 2)
                dve.tensor_scalar(CREC[2], CREC[2], -1.0, None, ALU.add)
                dve.drain()
                dve.tensor_scalar(CREC[4], CREC[2], 0.0, None, ALU.is_equal)
                dve.tensor_tensor(CREC[3], CREC[3], CREC[1], ALU.mult)
                dve.drain()
                dve.tensor_tensor(CREC[2], CREC[2], CREC[4], ALU.add)
                dve.tensor_tensor(CREC[4], CREC[4], CREC[1], ALU.mult)
                dve.drain()
                dve.reciprocal(CREC[2], CREC[2])
                dve.drain()
                dve.tensor_tensor(CREC[3], CREC[3], CREC[2], ALU.mult)
                dve.drain()
                dve.tensor_tensor(CREC[3], CREC[3], CREC[4], ALU.add)
                dve.drain()
                dve.tensor_tensor(CREC[0], CREC[0], CREC[3], ALU.add)
                dve.drain()
                dve.tensor_scalar(crec, CREC[0], -8.0, None, ALU.mult)
                dve.drain()
                with dve.Fori(0, NB) as b:
                    for t in range(2):
                        j = 2 * b + t
                        dve.wait_ge(s_revac, 6 * b + t + 1)
                        hold(dve)
                        dve.tensor_scalar(XA[t], RPAD[t][:, 0:T], col("conv_w_2", j, 0), col("conv_b_2", j),
                                          ALU.mult, ALU.add)
                        for k in range(1, 4):
                            dve.drain()
                            last = dve.scalar_tensor_tensor(XA[t], RPAD[t][:, k:k + T], col("conv_w_2", j, k),
                                                            XA[t], ALU.mult, ALU.add)
                        last.then_inc(s_xa, 1)
                    for t in range(2):
                        dve.wait_ge(s_riev, 2 * b + t + 1)
                        hold(dve)
                        dve.tensor_scalar(REC[t], REC[t], crec[:, ds(2 * b + t, 1)], None,
                                          ALU.mult).then_inc(s_la, 1)
                        dve.tensor_tensor(INP[t], INP[t], XA[t], ALU.mult)
                    for t in range(2):
                        dve.drain()
                        dve.wait_ge(s_mroot, 2 * b + t + 1)
                        dve.tensor_tensor(INP[t], INP[t], THMUL[t], ALU.mult)
                        dve.drain()
                        dve.tensor_tensor(INP[t], INP[t], REC[t], ALU.mult)
                        dve.drain()
                        dve.tensor_tensor_scan(REC[t], AEXP[t], INP[t], 0.0, ALU.mult, ALU.add)
                        dve.drain()
                        dve.wait_ge(s_revac, 6 * b + 5 + t)
                        dve.tensor_tensor(REC[t], REC[t], GELU[t], ALU.mult)
                        dve.drain()
                        dve.tensor_tensor(RA[:, ds(2 * b + t, 1), :].rearrange("p a t -> p (a t)"), REC[t],
                                          SIG[t], ALU.mult).then_inc(s_mt, 1)

        NQ, NKV, NROPE = 768, 256, 32
        NTHIRD = (NQ + NKV + NROPE) // 3
        LAT = part(0, (NT, 3 * NTHIRD))
        QC, KVC = LAT[:, :, 0:NQ], LAT[:, :, NQ:]
        W6RAW = [part(12 * T + k * NTHIRD, (NTHIRD,)) for k in range(NRAW)]
        W6HI, W6LO = ([rounded(f"W6{w}{k}", "arena", 12 * T + (NRAW + 2 * n + k) * NTHIRD, [P, NTHIRD])
                       for k in range(2)] for n, w in enumerate(("HI", "LO")))
        ROPE = part(23 * T + 512, (4, NT, 16))
        COS, SIN, ANG, TURNS = (ROPE[:, k] for k in range(4))
        KPE = part(24 * T, (NT, NROPE))
        GAINS = part(24 * T + 256, (2, 96))
        FREQ = part(24 * T + 448, (16,))
        POSF = part(24 * T + 464, (NT,))
        POSI = sb("POSI", [P, NT], I32)
        WUQ = part(8 * T + 256, (6, 384))
        WUKV = part(10 * T + 512, (2, HALF))
        latss = small[:, 112:128].rearrange("p (u m) -> p u m", u=2)
        latfirst = small[:, 216:224]
        latms = small[:, 128:144].rearrange("p (u m) -> p u m", u=2)
        s_pos = sem("s_pos")
        s_wup = sem("s_wup")
        s_w6land = [sem(f"s_w6land{k}") for k in range(NRAW)]
        s_w6hi = sem("s_w6hi")
        s_w6lo = sem("s_w6lo")
        s_w6used = sem("s_w6used")
        s_whole = sem("s_whole")
        s_lproj = sem("s_lproj")
        s_levac = sem("s_levac")
        s_lss = sem("s_lss")
        s_lms = sem("s_lms")
        s_lroot = sem("s_lroot")
        s_lnorm = sem("s_lnorm")
        s_lturn = sem("s_lturn")
        s_lt = sem("s_lt")
        s_ang = sem("s_ang")
        s_trig = sem("s_trig")

        def whole(eng, k):
            return eng.tensor_tensor(RC[:, k, :], U2HI[:, k, :].bitcast(F32), U2LO[:, k, :].bitcast(F32), ALU.add)

        with nc.Block() as block:
            @block.sync
            def _(sp):
                def load(n):
                    if n >= NRAW:
                        sp.wait_ge(s_w6lo, n - NRAW + 1)
                    c0 = 2 * D + n // ND * NTHIRD
                    sp.dma_start(W6RAW[n % NRAW], a["w_in_2"][0, n % ND * P:(n % ND + 1) * P, c0:c0 + NTHIRD]
                                 ).then_inc(s_w6land[n % NRAW], 16)

                for n in range(NRAW):
                    load(n)
                sp.dma_start(POSI[:], a["positions_2"].rearrange("o (m p) -> p (o m)", p=P)).then_inc(s_pos, 16)
                sp.dma_start(FREQ, a["c_freq"]).then_inc(s_pos, 16)
                for i, name in enumerate(("q_norm_g_2", "k_norm_g_2")):
                    sp.dma_start(GAINS[:, i, :], a[name].to_broadcast([P, 96])).then_inc(s_pos, 16)
                sp.dma_start(WUQ, a["w_uq_2"].rearrange("o (k p) n -> p (o k) n", p=P)[:, :, 0:384]
                             ).then_inc(s_wup, 16)
                sp.dma_start(WUKV, a["w_ukv_2"].rearrange("o (k p) n -> p (o k) n", p=P)[:, :, 0:HALF]
                             ).then_inc(s_wup, 16)

                for n in range(NRAW, 3 * ND):
                    load(n)

            @block.gpsimd
            def _(pool):
                pool.wait_ge(s_lproj, 3 * NT)
                for k in range(5, ND):
                    last = whole(pool, k)
                last.then_inc(s_whole, 1)

            @block.tensor
            def _(pe):
                for n in range(3 * ND):
                    c, k = n // ND, n % ND
                    pe.wait_ge(s_w6lo, n + 1)
                    for m in range(NT):
                        if c and k == 0:
                            pe.wait_ge(s_levac, NT * (c - 1) + m + 1)
                        for i, (x, y) in enumerate(passes((U2HI, U2LO), (W6HI[n % 2], W6LO[n % 2]))):
                            last = pe.matmul(PS[:, m, 0:NTHIRD], x[:, k, m * P:(m + 1) * P], y[:],
                                             start=(k == i == 0), stop=(k == ND - 1 and i == 2))
                        if k == ND - 1:
                            last.then_inc(s_lproj, 1)
                    if k < ND - 1:
                        last.then_inc(s_w6used, 1)
                    else:
                        pe.drain()
                        pe.nop().then_inc(s_w6used, 1)
                pe.wait_ge(s_levac, 3 * NT)
                for m in range(NT):
                    pe.wait_ge(s_lnorm, m + 1)
                    if m >= 2:
                        pe.wait_ge(s_lt, m - 1)
                    o = banks(2 * (m % 2))
                    for c in range(ND):
                        src = QC[:, m, c * P:(c + 1) * P] if c < 6 else KVC[:, m, (c - 6) * P:(c - 5) * P]
                        last = pe.transpose(o[:, c * P:(c + 1) * P], src, ident)
                    last.then_inc(s_lturn, 1)

            @block.scalar
            def _(act):
                def square(src, total):
                    act.activation(SQUARES[:, 0:src.shape[-1]], src, ACT.Square, accum_out=total)
                    act.drain()

                for n in range(3 * ND):
                    stream_hi(act, n, W6RAW, W6HI, s_w6land, s_w6used, s_w6hi)
                    if n >= 2 * ND:
                        m = n - 2 * ND
                        act.wait_ge(s_levac, NT + m + 1)
                        square(LAT[:, m, 0:2 * NTHIRD], latfirst[:, m:m + 1])
                for m in range(NT):
                    act.wait_ge(s_levac, 2 * NT + m + 1)
                    square(QC[:, m, 2 * NTHIRD:], latss[:, 0, m:m + 1])
                    square(KVC[:, m, 0:NKV], latss[:, 1, m:m + 1])
                act.nop().then_inc(s_lss, 1)
                act.wait_ge(s_lms, 1)
                act.activation(latms, latms, ACT.Sqrt).then_inc(s_lroot, 1)
                act.wait_ge(s_ang, 1)
                act.activation(SIN, SIN, ACT.Sin)
                act.activation(COS, COS, ACT.Sin)
                act.drain()
                act.nop().then_inc(s_trig, 1)

            @block.vector
            def _(dve):
                def latents(c):
                    for m in range(NT):
                        dve.wait_ge(s_lproj, NT * c + m + 1)
                        dve.tensor_copy(LAT[:, m, c * NTHIRD:(c + 1) * NTHIRD], PS[:, m, 0:NTHIRD]
                                        ).then_inc(s_levac, 1)

                def rotary_tables():
                    dve.wait_ge(s_pos, 64)
                    dve.tensor_copy(POSF, POSI[:])
                    dve.drain()
                    pos = POSF.rearrange("p (m o) -> p m o", o=1).to_broadcast([P, NT, 16])
                    freq = FREQ.rearrange("p (o i) -> p o i", o=1).to_broadcast([P, NT, 16])
                    dve.tensor_tensor(ANG, pos, freq, ALU.mult)
                    dve.drain()
                    dve.tensor_scalar(TURNS, ANG, float(1 / (2 * np.pi)), ROUND, ALU.mult, ALU.add)
                    dve.drain()
                    dve.tensor_scalar(TURNS, TURNS, -ROUND, None, ALU.add)
                    dve.drain()
                    for c in TWO_PI:
                        dve.scalar_tensor_tensor(ANG, TURNS, -c, ANG, ALU.mult, ALU.add)
                        dve.drain()
                    dve.tensor_scalar(COS, ANG, float(np.pi / 2), None, ALU.add)
                    dve.drain()
                    dve.tensor_scalar(TURNS, COS, float(np.pi), -float(2 * np.pi), ALU.is_gt, ALU.mult)
                    dve.drain()
                    dve.tensor_tensor(COS, COS, TURNS, ALU.add)
                    dve.drain()
                    dve.tensor_scalar(SIN, ANG, 3.1415925, -3.1415925, ALU.min, ALU.max)
                    dve.tensor_scalar(COS, COS, 3.1415925, -3.1415925, ALU.min, ALU.max)
                    dve.drain()
                    dve.nop().then_inc(s_ang, 1)

                for n in range(3 * ND):
                    stream_lo(dve, n, W6RAW, W6HI, W6LO, s_w6hi, s_w6lo)
                    if n % ND == 0 and n:
                        latents(n // ND - 1)
                    if n == 1:
                        rotary_tables()
                latents(2)
                for k in range(5):
                    last = whole(dve, k)
                last.then_inc(s_whole, 1)
                dve.wait_ge(s_lss, 1)
                dve.tensor_tensor(latss[:, 0], latss[:, 0], latfirst, ALU.add)
                dve.drain()
                dve.tensor_scalar(latms[:, 0], latss[:, 0], 1.0 / NQ, EPS, ALU.mult, ALU.add)
                dve.tensor_scalar(latms[:, 1], latss[:, 1], 1.0 / NKV, EPS, ALU.mult, ALU.add)
                dve.tensor_copy(KPE, KVC[:, :, NKV:NKV + NROPE])
                dve.drain()
                dve.nop().then_inc(s_lms, 1)
                dve.wait_ge(s_lroot, 1)
                dve.reciprocal(latms, latms)
                dve.drain()

                def evacuate(m):
                    if m == 0:
                        dve.wait_ge(s_whole, 2)
                    dve.wait_ge(s_lturn, m + 1)
                    o = banks(2 * (m % 2)).rearrange("p (c t) -> p c t", c=ND)
                    for c0, c1, name in ((0, 6, "q_a_g"), (6, 8, "kv_a_g")):
                        g = cols[:, 0:c1 - c0, ROWS[name]:ROWS[name] + 1].to_broadcast([P, c1 - c0, P])
                        last = dve.tensor_tensor(RB[:, c0:c1, m * P:(m + 1) * P], o[:, c0:c1, :], g, ALU.mult)
                    dve.drain()
                    dve.nop().then_inc(s_lt, 1)

                for m in range(NT):
                    dve.tensor_scalar(QC[:, m, :], QC[:, m, :], latms[:, 0, m:m + 1], None, ALU.mult)
                    dve.tensor_scalar(KVC[:, m, 0:NKV], KVC[:, m, 0:NKV], latms[:, 1, m:m + 1], None, ALU.mult)
                    dve.drain()
                    dve.nop().then_inc(s_lnorm, 1)
                    if m:
                        evacuate(m - 1)
                evacuate(NT - 1)

        NG, GH, NTASK = 4, 4, 4 * NT
        GATE1_COL = GATE0_COL + D
        SCALE = 96 ** -0.5
        QKTOK = part(0, (NT * 2 * GH, 96))
        PROB = [part(k * T, (T,)) for k in range(2)]
        PROBT = [part((2 + k) * T, (NT, P)) for k in range(2)]
        YTOK = part(4 * T, (NT, GH * 64))
        QKSQ = part(6 * T, (2 * GH, 96))
        ROT = [part(11 * T + 512 + k * T, (T,)) for k in range(4)]
        QFEAT = part(11 * T + 512, (GH, T))
        KFEAT = part(15 * T + 512, (GH, T))
        VTOK = part(19 * T + 512, (NT, GH, 64))
        WGATE = [part(21 * T + 512 + k * T, (ND, P)) for k in range(2)]
        SIG1 = [part(21 * T + 512 + k * T, (T,)) for k in range(2)]
        headss = small[:, 144:208]
        rowmax = small[:, 208:210]
        rowsum = small[:, 210:212]
        rowrec = small[:, 212:214]

        s_w1 = sem("s_w1")
        s_w8 = sem("s_w8")
        s_wup7 = sem("s_wup7")
        s_qkv = sem("s_qkv")
        s_qev = sem("s_qev")
        s_kev = sem("s_kev")
        s_g1 = sem("s_g1")
        s_g1sig = sem("s_g1sig")
        s_qms = sem("s_qms")
        s_qroot = sem("s_qroot")
        s_rot = sem("s_rot")
        s_qkturn = sem("s_qkturn")
        s_qfeat = sem("s_qfeat")
        s_kfeat = sem("s_kfeat")
        s_score = sem("s_score")
        s_max = sem("s_max")
        s_prob = sem("s_prob")
        s_pturn7 = sem("s_pturn7")
        s_probt = sem("s_probt")
        s_pv = sem("s_pv")
        s_y = sem("s_y")
        s_yturn = sem("s_yturn")
        s_merged = sem("s_merged")

        with nc.Block() as block:
            @block.sync
            def _(sp):
                def load_gate(g):
                    for t in range(2):
                        w = a["w_in_2"].rearrange("o (k p) n -> p (o k) n", p=P)
                        sp.dma_start(WGATE[t], w[:, :, ds(g * 256 + GATE1_COL + t * P, P)]).then_inc(s_w1, 16)

                load_gate(0)
                with sp.Fori(1, NG) as g:
                    sp.wait_ge(s_qkv, NT * g)
                    hold(sp)
                    sp.dma_start(WUQ, a["w_uq_2"].rearrange("o (k p) n -> p (o k) n", p=P)[:, :, ds(g * 384, 384)]
                                 ).then_inc(s_wup7, 16)
                    sp.dma_start(WUKV, a["w_ukv_2"].rearrange("o (k p) n -> p (o k) n", p=P)[:, :, ds(g * HALF, HALF)]
                                 ).then_inc(s_wup7, 16)
                    sp.wait_ge(s_merged, g)
                    hold(sp)
                    load_gate(g)
                sp.wait_ge(s_qkv, NT * NG)
                sp.dma_start(RB[:], a["w_out_2"].rearrange("o (k p) n -> p (o k) n", p=P)).then_inc(s_w8, 16)
                sp.wait_ge(s_filled, 16 * (NBLK - SURE) * P // T)

            @block.tensor
            def _(pe):
                def scores(g, n):
                    h, i = n // NT, n % NT
                    if n >= 2:
                        pe.wait_ge(s_prob, NTASK * g + n - 1)
                    o = banks(2 * (n % 2))
                    for c0 in range(0, (i + 1) * P, HALF):
                        c1 = min(c0 + HALF, (i + 1) * P)
                        last = pe.matmul(o[:, c0:c1], QFEAT[0:96, h, i * P:(i + 1) * P], KFEAT[0:96, h, c0:c1],
                                         start=True, stop=True)
                    last.then_inc(s_score, 1)

                def turn(g, n):
                    i = n % NT
                    pe.wait_ge(s_prob, NTASK * g + n + 1)
                    if n:
                        pe.wait_ge(s_probt, NTASK * g + n)
                    for c in range(i + 1):
                        last = pe.transpose(banks(4)[:, c * P:(c + 1) * P], PROB[n % 2][:, c * P:(c + 1) * P], ident)
                    last.then_inc(s_pturn7, 1)

                def values(g, n):
                    h, i = n // NT, n % NT
                    pe.wait_ge(s_probt, NTASK * g + n + 1)
                    if n >= 2:
                        pe.wait_ge(s_y, NTASK * g + n - 1)
                    for c in range(i + 1):
                        last = pe.matmul(PS[:, 6 + n % 2, 0:64], PROBT[n % 2][:, c, :], VTOK[:, c, h, :],
                                         start=(c == 0), stop=(c == i))
                    last.then_inc(s_pv, 1)

                def group(g, first):
                    if first:
                        pe.wait_ge(s_wup, 32)
                    else:
                        pe.wait_ge(s_wup7, 32 * g)
                        pe.wait_ge(s_merged, g)
                    for m in range(NT):
                        if m >= 2:
                            pe.wait_ge(s_qev, NT * g + m - 1)
                            pe.wait_ge(s_kev, NT * g + m - 1)
                        for k in range(6):
                            pe.matmul(PS[:, m % 2, 0:384], RB[:, k, m * P:(m + 1) * P], WUQ[:, k, :],
                                      start=(k == 0), stop=(k == 5))
                        for k in range(2):
                            last = pe.matmul(PS[:, 2 + m % 2, :], RB[:, 6 + k, m * P:(m + 1) * P], WUKV[:, k, :],
                                             start=(k == 0), stop=(k == 1))
                        last.then_inc(s_qkv, 1)
                    pe.wait_ge(s_w1, 32 * g + 32)
                    for t in range(2):
                        for h in range(2):
                            for k in range(ND):
                                last = pe.matmul(banks(4 + 2 * t)[:, h * HALF:(h + 1) * HALF], WGATE[t][:, k, :],
                                                 RC[:, k, h * HALF:(h + 1) * HALF],
                                                 start=(k == 0), stop=(k == ND - 1))
                        last.then_inc(s_g1, 1)
                    pe.wait_ge(s_rot, g + 1)
                    for m in range(NT):
                        if m >= 2:
                            pe.wait_ge(s_qfeat, NT * g + m - 1)
                            pe.wait_ge(s_kfeat, NT * g + m - 1)
                        for u in range(2):
                            for h in range(GH):
                                last = pe.transpose(PS[0:96, 2 * (m % 2) + u, h * P:(h + 1) * P],
                                                    QKTOK[:, (2 * m + u) * GH + h, :], ident)
                        last.then_inc(s_qkturn, 1)
                    pe.wait_ge(s_qfeat, NT * g + NT)
                    pe.wait_ge(s_kfeat, NT * g + NT)
                    pe.wait_ge(s_g1sig, 2 * g + 2)
                    scores(g, 0)
                    for n in range(NTASK):
                        if n + 1 < NTASK:
                            scores(g, n + 1)
                        turn(g, n)
                        if n:
                            values(g, n - 1)
                    values(g, NTASK - 1)
                    pe.wait_ge(s_y, NTASK * g + NTASK)
                    for t in range(2):
                        for m in range(NT):
                            last = pe.transpose(banks(2 * t)[:, m * P:(m + 1) * P],
                                                YTOK[:, m, t * P:(t + 1) * P], ident)
                    last.then_inc(s_yturn, 1)

                group(0, True)
                with pe.Fori(1, NG) as g:
                    group(g, False)

            @block.scalar
            def _(act):
                with act.Fori(0, NG) as g:
                    for m in range(NT):
                        act.wait_ge(s_qkv, NT * g + m + 1)
                        act.activation(QKTOK[:, 2 * m * GH:(2 * m + 1) * GH, :].rearrange("p h d -> p (h d)"),
                                       PS[:, m % 2, 0:384], ACT.Copy).then_inc(s_qev, 1)
                    act.wait_ge(s_qms, g + 1)
                    act.activation(headss, headss, ACT.Sqrt).then_inc(s_qroot, 1)
                    for t in range(2):
                        act.wait_ge(s_g1, 2 * g + t + 1)
                        act.activation(SIG1[t], banks(4 + 2 * t), ACT.Sigmoid).then_inc(s_g1sig, 1)
                    for m in range(NT):
                        act.wait_ge(s_qkturn, NT * g + m + 1)
                        act.activation(QFEAT[0:96, :, m * P:(m + 1) * P],
                                       PS[0:96, 2 * (m % 2), :].rearrange("p (h t) -> p h t", h=GH),
                                       ACT.Copy).then_inc(s_qfeat, 1)
                    for n in range(NTASK):
                        w = (n % NT + 1) * P
                        act.wait_ge(s_max, NTASK * g + n + 1)
                        if n >= 2:
                            act.wait_ge(s_pturn7, NTASK * g + n - 1)
                        act.activation(PROB[n % 2][:, 0:w], banks(2 * (n % 2))[:, 0:w], ACT.Exp, scale=SCALE,
                                       bias=rowmax[:, n % 2:n % 2 + 1], accum_out=rowsum[:, n % 2:n % 2 + 1])
                        act.drain()
                        act.nop().then_inc(s_prob, 1)

            @block.vector
            def _(dve):
                with dve.Fori(0, NG) as g:
                    def sums(m):
                        dve.wait_ge(s_qev, NT * g + m + 1)
                        hold(dve)
                        qk = QKTOK[:, 2 * m * GH:2 * (m + 1) * GH, :]
                        dve.tensor_tensor(QKSQ, qk, qk, ALU.mult)
                        dve.drain()
                        dve.tensor_reduce(headss[:, 2 * m * GH:2 * (m + 1) * GH], QKSQ, AX.X, ALU.add)
                        dve.drain()

                    for m in range(NT):
                        dve.wait_ge(s_qkv, NT * g + m + 1)
                        k = QKTOK[:, (2 * m + 1) * GH:(2 * m + 2) * GH, :]
                        dve.tensor_copy(k[:, :, 0:64],
                                        PS[:, 2 + m % 2, :].rearrange("p (h d) -> p h d", h=GH)[:, :, 0:64])
                        dve.tensor_copy(VTOK[:, m], PS[:, 2 + m % 2, :].rearrange("p (h d) -> p h d", h=GH)[:, :, 64:])
                        dve.tensor_copy(k[:, :, 64:96], KPE[:, m:m + 1, :].to_broadcast([P, GH, NROPE]))
                        dve.drain()
                        dve.nop().then_inc(s_kev, 1)
                        if m:
                            sums(m - 1)
                    sums(NT - 1)
                    dve.tensor_scalar(headss, headss, 1.0 / 96, EPS, ALU.mult, ALU.add).then_inc(s_qms, 1)
                    dve.wait_ge(s_qroot, g + 1)
                    dve.reciprocal(headss, headss)
                    dve.drain()
                    dve.tensor_tensor(QKTOK, QKTOK, headss.rearrange("p (h o) -> p h o", o=1)
                                      .to_broadcast([P, NT * 2 * GH, 96]), ALU.mult)
                    dve.drain()
                    for m in range(NT):
                        for u in range(2):
                            qk = QKTOK[:, (2 * m + u) * GH:(2 * m + u + 1) * GH, :]
                            dve.tensor_tensor(qk, qk, GAINS[:, u:u + 1, :].to_broadcast([P, GH, 96]), ALU.mult)
                    dve.drain()
                    qk = QKTOK.rearrange("p (m h) d -> p m h d", m=NT)
                    x1, x2 = qk[:, :, :, 64:80], qk[:, :, :, 80:96]

                    def table(v):
                        return v.rearrange("p m (o i) -> p m o i", o=1).to_broadcast([P, NT, 2 * GH, 16])

                    r = [v.rearrange("p (m h i) -> p m h i", m=NT, h=2 * GH) for v in ROT]
                    for v, x, c in ((r[0], x1, COS), (r[1], x2, SIN), (r[2], x1, SIN), (r[3], x2, COS)):
                        dve.tensor_tensor(v, x, table(c), ALU.mult)
                    dve.drain()
                    dve.tensor_tensor(x1, r[0], r[1], ALU.subtract)
                    dve.tensor_tensor(x2, r[2], r[3], ALU.add)
                    dve.drain()
                    dve.nop().then_inc(s_rot, 1)
                    for m in range(NT):
                        dve.wait_ge(s_qkturn, NT * g + m + 1)
                        dve.tensor_copy(KFEAT[0:96, :, m * P:(m + 1) * P],
                                        PS[0:96, 2 * (m % 2) + 1, :].rearrange("p (h t) -> p h t", h=GH)
                                        ).then_inc(s_kfeat, 1)

                    def largest(n):
                        w = (n % NT + 1) * P
                        s = banks(2 * (n % 2))
                        dve.wait_ge(s_score, NTASK * g + n + 1)
                        dve.memset(s[0:64, w - 64:w], -1e30)
                        dve.drain()
                        dve.tensor_reduce(rowmax[:, n % 2:n % 2 + 1], s[:, 0:w], AX.X, ALU.max)
                        dve.drain()
                        dve.tensor_scalar(rowmax[:, n % 2:n % 2 + 1], rowmax[:, n % 2:n % 2 + 1], -SCALE, None,
                                          ALU.mult).then_inc(s_max, 1)

                    def normalise(n):
                        h, i = n // NT, n % NT
                        dve.wait_ge(s_pv, NTASK * g + n + 1)
                        dve.tensor_scalar(YTOK[:, i, h * 64:(h + 1) * 64], PS[:, 6 + n % 2, 0:64],
                                          rowrec[:, n % 2:n % 2 + 1], None, ALU.mult).then_inc(s_y, 1)

                    largest(0)
                    for n in range(NTASK):
                        w = (n % NT + 1) * P
                        if n + 1 < NTASK:
                            if n >= 1:
                                dve.wait_ge(s_prob, NTASK * g + n)
                            largest(n + 1)
                        dve.wait_ge(s_pturn7, NTASK * g + n + 1)
                        if n >= 2:
                            dve.wait_ge(s_pv, NTASK * g + n - 1)
                        dve.tensor_copy(PROBT[n % 2].rearrange("p c t -> p (c t)")[:, 0:w],
                                        banks(4)[:, 0:w]).then_inc(s_probt, 1)
                        if n:
                            normalise(n - 1)
                        dve.reciprocal(rowrec[:, n % 2:n % 2 + 1], rowsum[:, n % 2:n % 2 + 1])
                        dve.drain()
                    normalise(NTASK - 1)
                    dve.wait_ge(s_yturn, g + 1)
                    for t in range(2):
                        dve.tensor_tensor(SIG1[t], SIG1[t], banks(2 * t), ALU.mult)
                    dve.drain()
                    for t in range(2):
                        r = RA[:, ds(2 * g + t, 1), :].rearrange("p a t -> p (a t)")
                        last = dve.tensor_tensor(r, r, SIG1[t], ALU.add)
                    last.then_inc(s_merged, 1)

        retire(*s_st, s_held, s_w8)
        NE, NGRP, EPG = 32, 4, 8
        BIG = 1e30
        xn_dram = nc.dram_tensor("xn_dram", [T, D], F32).ap()
        list_dram = nc.dram_tensor("list_dram", [(NBLK + 1) * P, 1], I32).ap()
        MHI = rounded("MHI", "arena", 14 * T, [P, ND, T])
        MLO = rounded("MLO", "RA", 0, [P, ND, T])
        W8HI, W8LO = ([rounded(f"W8{w}{k}", "arena", 22 * T + (2 * n + k) * HALF, [P, HALF]) for k in range(2)]
                      for n, w in enumerate(("HI", "LO")))
        NORM8 = [part((2 + k) * T, (T,)) for k in range(2)]
        XNT = [part((4 + k) * T, (ND, P)) for k in range(2)]
        FFN_G = part(6 * T, (T,))
        WROUTE = part(7 * T, (ND, NGRP + NE))
        BROUTE = part(7 * T + 288, (NGRP + NE,))
        LOGITS = part(7 * T + 328, (NT, NGRP + NE))
        R = [part(8 * T + 256 * k, (NT, NE)) for k in range(6)]
        PICK = [part(8 * T + 256 * (6 + k), (NT, NE)) for k in range(2)]
        EXPERT = part(10 * T, (NE,))
        BLOCKAT = part(10 * T + 32, (NBLK,))
        SHORT = [part(10 * T + 96 + 8 * k, (NT,)) for k in range(12)]
        CHOSEN = [small[:, 216 + 8 * k:224 + 8 * k] for k in range(2)]
        LISTROW = [part(10 * T + 208 + 8 * k, (NT,)) for k in range(2)]
        EARLIER = part(10 * T + 384, (NE,))
        ENDS = part(10 * T + 224, (NE,))
        STARTS = part(10 * T + 256, (NE,))
        PADDED = part(10 * T + 288, (NE,))
        OFBLOCK = part(11 * T, (NBLK, NE))
        BLKF = part(13 * T, (NBLK,))
        PAIRSF = part(13 * T + 128, (1,))
        PAIRSI = sb("PAIRSI", [P, 1], I32)
        GGRP = part(13 * T + 64, (NT, NGRP))
        GGRP2 = part(13 * T + 96, (NT, NGRP))
        ONES = sb("ONES", [P, P])
        ROWI = sb("ROWI", [P, 2, NT], I32)
        TOKI = sb("TOKI", [P, NT], I32)
        COUNTI = sb("COUNTI", [P, NE], I32)
        BLKI = sb("BLKI", [P, NBLK], I32)
        LISTI = sb("LISTI", [P, NBLK + 1], I32)

        s_wr = sem("s_wr")
        s_x1land = sem("s_x1land")
        s_mhi = sem("s_mhi")
        s_mlo = sem("s_mlo")
        s_w8hi = sem("s_w8hi")
        s_w8lo = sem("s_w8lo")
        s_w8used = sem("s_w8used")
        s_h2p = sem("s_h2p")
        s_h2 = sem("s_h2")
        s_xn = sem("s_xn")
        s_xnst = [sem(f"s_xnst{k}") for k in range(2)]
        s_xnturn = sem("s_xnturn")
        s_xnt = sem("s_xnt")
        s_log = sem("s_log")
        s_logev = sem("s_logev")
        s_gsub = sem("s_gsub")
        s_gexp = sem("s_gexp")
        s_pick = sem("s_pick")
        s_rank = sem("s_rank")
        s_rows8 = sem("s_rows8")
        s_zlist = sem("s_zlist")
        s_list = sem("s_list")

        with nc.Block() as block:
            @block.sync
            def _(sp):
                sp.dma_start(RC[:], x1_dram.rearrange("m p d -> p m d")).then_inc(s_x1land, 16)
                sp.dma_start(FFN_G, a["norm_ffn_g_2"].to_broadcast([P, D])).then_inc(s_wr, 16)
                sp.dma_start(WROUTE[:, :, 0:NGRP], a["router_group_w_2"].rearrange("o (k p) n -> p (o k) n", p=P)
                             ).then_inc(s_wr, 16)
                sp.dma_start(WROUTE[:, :, NGRP:], a["router_expert_w_2"].rearrange("o (k p) n -> p (o k) n", p=P)
                             ).then_inc(s_wr, 16)
                sp.dma_start(BROUTE[:, 0:NGRP], a["router_group_b_2"].to_broadcast([P, NGRP])).then_inc(s_wr, 16)
                sp.dma_start(BROUTE[:, NGRP:], a["router_expert_b_2"].to_broadcast([P, NE])).then_inc(s_wr, 16)
                sp.dma_start(EXPERT, a["c_expert"]).then_inc(s_wr, 16)
                sp.dma_start(BLOCKAT, a["c_block"]).then_inc(s_wr, 16)
                sp.dma_start(TOKI[:], a["c_token"]).then_inc(s_wr, 16)
                for m in range(NT):
                    sp.wait_ge(s_xn, m + 1)
                    sp.dma_start(xn_dram[m * P:(m + 1) * P, :], NORM8[m % 2]).then_inc(s_xnst[m % 2], 16)
                for k in range(2):
                    sp.wait_ge(s_xnst[k], 8 * NT)

            @block.tensor
            def _(pe):
                for n in range(2 * ND):
                    h, k = n // ND, n % ND
                    pe.wait_ge(s_w8lo, n + 1)
                    if h == 0:
                        pe.wait_ge(s_mlo, k + 1)
                    for m in range(NT):
                        if h and k == 0:
                            pe.wait_ge(s_h2, m + 1)
                        for i, (x, y) in enumerate(passes((MHI, MLO), (W8HI[n % 2], W8LO[n % 2]))):
                            last = pe.matmul(PS[:, m, :], x[:, k, m * P:(m + 1) * P], y[:],
                                             start=(k == i == 0), stop=(k == ND - 1 and i == 2))
                        if k == ND - 1:
                            last.then_inc(s_h2p, 1)
                    if k < ND - 1:
                        last.then_inc(s_w8used, 1)
                    else:
                        pe.drain()
                        pe.nop().then_inc(s_w8used, 1)
                pe.wait_ge(s_h2, 2 * NT)
                pe.wait_ge(s_wr, 16 * 8)
                def turn(m):
                    pe.wait_ge(s_xn, m + 1)
                    if m >= 2:
                        pe.wait_ge(s_xnt, m - 1)
                    pe_turn(pe, banks(2 * (m % 2)), NORM8[m % 2], s_xnturn)

                turn(0)
                for m in range(NT):
                    if m + 1 < NT:
                        turn(m + 1)
                    pe.wait_ge(s_xnt, m + 1)
                    if m >= 2:
                        pe.wait_ge(s_logev, m - 1)
                    for k in range(ND):
                        last = pe.matmul(PS[:, 4 + m % 2, 0:NGRP + NE], XNT[m % 2][:, k, :], WROUTE[:, k, :],
                                         start=(k == 0), stop=(k == ND - 1))
                    last.then_inc(s_log, 1)
                pe.wait_ge(s_pick, 1)
                pe.wait_ge(s_zlist, 1)
                wide = [v.rearrange("p m e -> p (m e)") for v in R]
                pe.matmul(PS[:, 6, 0:NT * NE], before, wide[0], start=True, stop=False)
                pe.matmul(PS[:, 6, 0:NT * NE], ONES[:], wide[3], start=False, stop=True)
                last = pe.matmul(PS[:, 7, 0:NE], ONES[:], EARLIER, start=True, stop=True)
                last.then_inc(s_rank, 1)

            @block.scalar
            def _(act):
                def upper(k):
                    split_hi(act, MHI[:, k, :], RA[:, k, :]).then_inc(s_mhi, 1)

                act.wait_ge(s_w8, 16)
                upper(0)
                for n in range(2 * ND):
                    if n >= 2:
                        act.wait_ge(s_w8used, n - 1)
                    split_hi(act, W8HI[n % 2][:], RB[:, n % ND, n // ND * HALF:(n // ND + 1) * HALF]
                             ).then_inc(s_w8hi, 1)
                    if n + 1 < ND:
                        upper(n + 1)
                root_mean_square(act, s_h2, NT, 3, RC)
                for m in range(NT):
                    act.wait_ge(s_xnturn, m + 1)
                    if m >= 2:
                        act.wait_ge(s_log, m - 1)
                    act.activation(XNT[m % 2].rearrange("p c t -> p (c t)"), banks(2 * (m % 2)),
                                   ACT.Copy).then_inc(s_xnt, 1)
                for n in range(2):
                    act.wait_ge(s_gsub, n + 1)
                    v = (GGRP, SHORT[4])[n]
                    act.activation(v, v, ACT.Exp).then_inc(s_gexp, 1)

            @block.gpsimd
            def _(pool):
                pool.memset(LISTI[:], 0)
                pool.memset(ONES[:], 1.0).then_inc(s_zlist, 1)
                pool.drain()
                pool.dma_start(list_dram.rearrange("(b p) o -> p (b o)", p=P), LISTI[:]).then_inc(s_list, 16)
                pool.wait_ge(s_rows8, 1)
                pool.wait_ge(s_list, 16)
                pool.wait_ge(s_wr, 16 * 8)
                for u in range(2):
                    for m in range(NT):
                        pool.indirect_dma_start(list_dram, bass.IndirectOffsetOnAxis(ap=ROWI[:, u, m:m + 1], axis=0),
                                                TOKI[:, m:m + 1], None).then_inc(s_list, 16)
                pool.wait_ge(s_list, 16 * (1 + 2 * NT))
                pool.dma_start(LISTI[:], list_dram.rearrange("(b p) o -> p (b o)", p=P)).then_inc(s_list, 16)

            @block.vector
            def _(dve):
                def sums(h):
                    dve.wait_ge(s_x1land, 16)
                    for m in range(NT):
                        dve.wait_ge(s_h2p, NT * h + m + 1)
                        r = RC[:, m, h * HALF:(h + 1) * HALF]
                        dve.tensor_tensor(r, PS[:, m, :], r, ALU.add).then_inc(s_h2, 1)

                for n in range(2 * ND):
                    if n < ND:
                        dve.wait_ge(s_mhi, n + 1)
                        split_lo(dve, MLO[:, n, :], RA[:, n, :], MHI[:, n, :]).then_inc(s_mlo, 1)
                    dve.wait_ge(s_w8hi, n + 1)
                    split_lo(dve, W8LO[n % 2][:], RB[:, n % ND, n // ND * HALF:(n // ND + 1) * HALF],
                             W8HI[n % 2][:]).then_inc(s_w8lo, 1)
                    if n == ND:
                        sums(0)
                sums(1)
                reciprocal_roots(dve, 3)
                dve.wait_ge(s_wr, 16 * 8)

                def logits(m):
                    dve.wait_ge(s_log, m + 1)
                    dve.tensor_tensor(LOGITS[:, m, :], PS[:, 4 + m % 2, 0:NGRP + NE], BROUTE,
                                      ALU.add).then_inc(s_logev, 1)

                for m in range(NT):
                    if m >= 2:
                        dve.wait_ge(s_xnturn, m - 1)
                        dve.wait_ge(s_xnst[m % 2], 16 * (m // 2))
                    dve.scalar_tensor_tensor(NORM8[m % 2], RC[:, m, :], rstd[:, m:m + 1], FFN_G, ALU.mult,
                                             ALU.mult).then_inc(s_xn, 1)
                    if m:
                        logits(m - 1)
                logits(NT - 1)
                dve.drain()

                def wide(v, n):
                    return v.rearrange("p (m o) -> p m o", o=1).to_broadcast([P, NT, n])

                def narrow(v, n):
                    return v[:, 0:n].rearrange("p (o e) -> p o e", o=1).to_broadcast([P, NT, n])

                def then(*_):
                    dve.drain()

                def first_largest(v, n, top, index, pick, scratch):
                    then(dve.tensor_reduce(top, v, AX.X, ALU.max))
                    then(dve.tensor_tensor(scratch, v, wide(top, n), ALU.not_equal))
                    then(dve.tensor_scalar(scratch, scratch, BIG, None, ALU.mult))
                    then(dve.tensor_tensor(scratch, scratch, narrow(EXPERT, n), ALU.add))
                    then(dve.tensor_reduce(index, scratch, AX.X, ALU.min))
                    then(dve.tensor_tensor(pick, narrow(EXPERT, n), wide(index, n), ALU.is_equal))

                grp, exp = LOGITS[:, :, 0:NGRP], LOGITS[:, :, NGRP:]
                gmax, gidx, ptop, v1, v2, w1, w2, idx = SHORT[0], SHORT[1], SHORT[2], SHORT[3], SHORT[4], *SHORT[5:8]
                first_largest(grp, NGRP, gmax, gidx, GGRP2, GGRP)
                dve.tensor_tensor(GGRP, grp, wide(gmax, NGRP), ALU.subtract).then_inc(s_gsub, 1)
                dve.wait_ge(s_gexp, 1)
                then(dve.tensor_reduce(ptop, GGRP, AX.X, ALU.add))
                then(dve.reciprocal(ptop, ptop))
                oh = GGRP2.rearrange("p m (g o) -> p m g o", o=1).to_broadcast([P, NT, NGRP, EPG])
                e4 = exp.rearrange("p m (g e) -> p m g e", g=NGRP)
                r1 = R[1].rearrange("p m (g e) -> p m g e", g=NGRP)
                r2 = R[2].rearrange("p m (g e) -> p m g e", g=NGRP)
                dve.tensor_tensor(r1, e4, oh, ALU.mult)
                then(dve.tensor_scalar(r2, oh, -1.0, BIG, ALU.add, ALU.mult))
                then(dve.tensor_tensor(R[1], R[1], R[2], ALU.add))
                first_largest(R[1], NE, v1, idx, PICK[0], R[2])
                then(dve.tensor_scalar(R[2], PICK[0], -2 * BIG, None, ALU.mult))
                then(dve.tensor_tensor(R[1], R[1], R[2], ALU.add))
                first_largest(R[1], NE, v2, idx, PICK[1], R[2])
                then(dve.tensor_tensor(R[0], PICK[0], PICK[1], ALU.add))
                then(dve.memset(R[3][:, 0, :], 0.0))
                for m in range(NT):
                    then(dve.tensor_tensor(R[3][:, m + 1, :] if m + 1 < NT else EARLIER, R[3][:, m, :],
                                           R[0][:, m, :], ALU.add))
                dve.nop().then_inc(s_pick, 1)
                dve.tensor_tensor(v2, v2, v1, ALU.subtract).then_inc(s_gsub, 1)
                dve.wait_ge(s_gexp, 2)
                then(dve.tensor_scalar(w1, v2, 1.0, None, ALU.add))
                then(dve.reciprocal(w1, w1))
                then(dve.tensor_tensor(CHOSEN[0], ptop, w1, ALU.mult))
                then(dve.tensor_tensor(CHOSEN[1], CHOSEN[0], v2, ALU.mult))
                dve.wait_ge(s_zlist, 1)
                dve.wait_ge(s_rank, 1)
                then(dve.tensor_scalar(PADDED, PS[:, 7, 0:NE], float(P - 1), None, ALU.add))
                then(dve.tensor_copy(COUNTI[:], PADDED))
                then(dve.tensor_scalar(COUNTI[:], COUNTI[:], 7, 7, ALU.arith_shift_right, ALU.arith_shift_left))
                then(dve.tensor_copy(PADDED, COUNTI[:]))
                then(dve.tensor_tensor_scan(ENDS, ONES[:, 0:NE], PADDED, 0.0, ALU.mult, ALU.add))
                then(dve.tensor_tensor(STARTS, ENDS, PADDED, ALU.subtract))
                then(dve.tensor_tensor(R[3], PS[:, 6, 0:NT * NE].rearrange("p (m e) -> p m e", e=NE),
                                       narrow(STARTS, NE), ALU.add))
                for u in range(2):
                    then(dve.tensor_tensor(R[4], R[3], PICK[u], ALU.mult))
                    then(dve.tensor_reduce(LISTROW[u], R[4], AX.X, ALU.add))
                    then(dve.tensor_copy(ROWI[:, u, :], LISTROW[u]))
                dve.nop().then_inc(s_rows8, 1)
                ends = ENDS.rearrange("p (o e) -> p o e", o=1).to_broadcast([P, NBLK, NE])
                at = BLOCKAT.rearrange("p (b o) -> p b o", o=1).to_broadcast([P, NBLK, NE])
                then(dve.tensor_tensor(OFBLOCK, ends, at, ALU.is_le))
                then(dve.tensor_reduce(BLKF, OFBLOCK, AX.X, ALU.add))
                then(dve.tensor_scalar(BLKF, BLKF, float(NE - 1), None, ALU.min))
                then(dve.tensor_copy(BLKI[:], BLKF))
                then(dve.tensor_scalar(PAIRSF, ENDS[:, NE - 1:NE], float(P), None, ALU.add))
                then(dve.tensor_copy(PAIRSI[:], PAIRSF))
                dve.tensor_scalar(PAIRSI[:], PAIRSI[:], 8, None, ALU.arith_shift_right)

        TOKS = [sb(f"TOKS{k}", [P, 1], I32) for k in range(2)]
        EG = [part(k * 6 * T, (ND, 256)) for k in range(2)]
        EU = [part(2 * T + k * 6 * T, (ND, 256)) for k in range(2)]
        ED = [part(4 * T + k * 6 * T, (2, T)) for k in range(2)]
        XG = [part((14 + k) * T, (T,)) for k in range(2)]
        XT = [part((16 + k) * T, (ND, P)) for k in range(2)]
        HB = [part(18 * T + 512 * k, (512,)) for k in range(2)]
        HT = [part(19 * T + 256 * k, (2, P)) for k in range(2)]
        YB = [part((20 + k) * T, (T,)) for k in range(2)]

        s_gland = [sem(f"s_gland{k}") for k in range(2)]
        s_dland = [sem(f"s_dland{k}") for k in range(2)]
        s_xgath = [sem(f"s_xgath{k}") for k in range(2)]
        s_xgt = sem("s_xgt")
        s_xte = sem("s_xte")
        s_gu = sem("s_gu")
        s_gact = sem("s_gact")
        s_hb = sem("s_hb")
        s_hbt = sem("s_hbt")
        s_hte = sem("s_hte")
        s_down = sem("s_down")
        s_yb = sem("s_yb")
        s_yst = [sem(f"s_yst{k}") for k in range(2)]
        NPAIR = NBLK // 2
        wg_t = a["w_gate_2"].rearrange("o e (p k) n -> p (o e) (k n)", k=ND)
        wu_t = a["w_up_2"].rearrange("o e (p k) n -> p (o e) (k n)", k=ND)
        wd_t = a["w_down_2"].rearrange("o e (p k) n -> p (o e) (k n)", k=2)

        def active_pairs(eng, body):
            used = eng.value_load(PAIRSI[0:1, 0:1], min_val=NBLK // 6, max_val=NPAIR)
            body(0)
            with eng.Fori(1, NPAIR) as i:
                with eng.If(i < used):
                    body(i)

        with nc.Block() as block:
            @block.sync
            def _(sp):
                def body(i):
                    for s in range(2):
                        b = 2 * i + s
                        e = sp.value_load(BLKI[0:1, ds(b, 1)], min_val=0, max_val=NE - 1)
                        if not isinstance(i, int):
                            sp.wait_ge(s_gu, b - 1)
                            hold(sp)
                        for dst, src in ((EG, wg_t), (EU, wu_t)):
                            sp.dma_start(dst[s].rearrange("p k n -> p (k n)"),
                                         src[:, ds(e, 1), :].rearrange("p a n -> p (a n)")).then_inc(s_gland[s], 16)
                        if not isinstance(i, int):
                            sp.wait_ge(s_down, b - 1)
                            hold(sp)
                        sp.dma_start(ED[s].rearrange("p k n -> p (k n)"),
                                     wd_t[:, ds(e, 1), :].rearrange("p a n -> p (a n)")).then_inc(s_dland[s], 16)

                active_pairs(sp, body)

            @block.gpsimd
            def _(pool):
                pool.wait_ge(s_list, 16 * (2 + 2 * NT))

                def gather(b, s):
                    pool.tensor_copy(TOKS[s][:], LISTI[:, ds(b, 1)])
                    pool.drain()
                    pool.indirect_dma_start(XG[s], None, xn_dram,
                                            bass.IndirectOffsetOnAxis(ap=TOKS[s][:], axis=0)
                                            ).then_inc(s_xgath[s], 16)

                def body(i):
                    if not isinstance(i, int):
                        pool.wait_ge(s_xgt, 2 * i)
                        hold(pool)
                    gather(2 * i + 1, 1)
                    pool.wait_ge(s_xgt, 2 * i + 1)
                    hold(pool)
                    gather(2 * i + 2, 0)

                gather(0, 0)
                active_pairs(pool, body)

            @block.tensor
            def _(pe):
                def turn(i, s):
                    pe.wait_ge(s_xgath[s], 16 * i + 16)
                    if s or not (isinstance(i, int) and i == 0):
                        pe.wait_ge(s_xte, 2 * i + s)
                    x = XG[s].rearrange("p (d k) -> p k d", k=ND)
                    for k in range(ND):
                        last = pe.transpose(banks(0)[:, k * P:(k + 1) * P], x[:, k, :], ident)
                    last.then_inc(s_xgt, 1)

                def expert(i, s):
                    pe.wait_ge(s_gland[s], 32 * i + 32)
                    pe.wait_ge(s_xte, 2 * i + s + 1)
                    if s or not isinstance(i, int):
                        pe.wait_ge(s_hb, 2 * i + s)
                    for u, w in enumerate((EG[s], EU[s])):
                        for k in range(ND):
                            last = pe.matmul(PS[:, 2 + u, 0:256], XT[s][:, k, :], w[:, k, :],
                                             start=(k == 0), stop=(k == ND - 1))
                    last.then_inc(s_gu, 1)

                def turn_hidden(i, s):
                    pe.wait_ge(s_hb, 2 * i + s + 1)
                    if s or not isinstance(i, int):
                        pe.wait_ge(s_hte, 2 * i + s)
                    h = HB[s][:, 0:256].rearrange("p (f k) -> p k f", k=2)
                    for k in range(2):
                        last = pe.transpose(PS[:, 4, k * P:(k + 1) * P], h[:, k, :], ident)
                    last.then_inc(s_hbt, 1)

                def down(i, s):
                    pe.wait_ge(s_dland[s], 16 * i + 16)
                    pe.wait_ge(s_hte, 2 * i + s + 1)
                    if s or not isinstance(i, int):
                        pe.wait_ge(s_yb, 2 * i + s)
                    for h in range(2):
                        for k in range(2):
                            last = pe.matmul(banks(6)[:, h * HALF:(h + 1) * HALF], HT[s][:, k, :],
                                             ED[s][:, k, h * HALF:(h + 1) * HALF], start=(k == 0), stop=(k == 1))
                    last.then_inc(s_down, 1)

                def body(i):
                    expert(i, 0)
                    turn(i, 1)
                    turn_hidden(i, 0)
                    expert(i, 1)
                    down(i, 0)
                    turn(i + 1, 0)
                    turn_hidden(i, 1)
                    down(i, 1)

                turn(0, 0)
                active_pairs(pe, body)

            @block.scalar
            def _(act):
                def turned(b, s, first):
                    act.wait_ge(s_xgt, b + 1)
                    if not first:
                        act.wait_ge(s_gu, b - 1)
                    act.activation(XT[s].rearrange("p c t -> p (c t)"), banks(0), ACT.Copy).then_inc(s_xte, 1)

                def silu(i, s):
                    b = 2 * i + s
                    act.wait_ge(s_gu, b + 1)
                    if not isinstance(i, int):
                        act.wait_ge(s_hb, b - 1)
                    act.activation(HB[s][:, 256:512], PS[:, 2, 0:256], ACT.Silu).then_inc(s_gact, 1)

                def store(i, s):
                    b = 2 * i + s
                    act.wait_ge(s_down, b + 1)
                    if not isinstance(i, int):
                        act.wait_ge(s_yst[s], 16 * i)
                    act.activation(YB[s], banks(6), ACT.Copy).then_inc(s_yb, 1)
                    act.wait_ge(s_yb, b + 1)
                    hold(act)
                    act.dma_start(y_dram[ds(b * P, P), :], YB[s]).then_inc(s_yst[s], 16)

                def body(i):
                    silu(i, 0)
                    turned(2 * i + 1, 1, isinstance(i, int))
                    silu(i, 1)
                    store(i, 0)
                    turned(2 * i + 2, 0, False)
                    store(i, 1)

                turned(0, 0, True)
                active_pairs(act, body)

            @block.vector
            def _(dve):
                def body(i):
                    for s in range(2):
                        b = 2 * i + s
                        dve.wait_ge(s_gact, b + 1)
                        if not isinstance(i, int):
                            dve.wait_ge(s_hbt, b - 1)
                        dve.tensor_tensor(HB[s][:, 0:256], HB[s][:, 256:512], PS[:, 3, 0:256],
                                          ALU.mult).then_inc(s_hb, 1)
                        dve.wait_ge(s_hbt, b + 1)
                        dve.tensor_copy(HT[s].rearrange("p k t -> p (k t)"), PS[:, 4, 0:256]).then_inc(s_hte, 1)

                active_pairs(dve, body)

        YGATH = [part(k * T, (T,)) for k in range(2 * NT)]
        s_yg = [sem(f"s_yg{k}") for k in range(2 * NT)]
        s_sum = sem("s_sum")
        s_out = sem("s_out")
        out_rows = out.rearrange("o (m p) d -> p (o m) d", p=P)

        with nc.Block() as block:
            @block.gpsimd
            def _(pool):
                used = pool.value_load(PAIRSI[0:1, 0:1], min_val=NBLK // 6, max_val=NPAIR)
                for s in range(2):
                    pool.wait_ge(s_yst[s], used * 16)
                    hold(pool)
                for m in range(NT):
                    for u in range(2):
                        k = 2 * m + u
                        pool.indirect_dma_start(YGATH[k], None, y_dram,
                                                bass.IndirectOffsetOnAxis(ap=ROWI[:, u, m:m + 1], axis=0)
                                                ).then_inc(s_yg[k], 16)

            @block.vector
            def _(dve):
                for m in range(NT):
                    for u in range(2):
                        k = 2 * m + u
                        dve.wait_ge(s_yg[k], 16)
                        if u:
                            dve.drain()
                        last = dve.scalar_tensor_tensor(RC[:, m, :], YGATH[k], CHOSEN[u][:, m:m + 1], RC[:, m, :],
                                                        ALU.mult, ALU.add)
                    last.then_inc(s_sum, 1)

            @block.sync
            def _(sp):
                for m in range(NT):
                    sp.wait_ge(s_sum, m + 1)
                    sp.dma_start(out_rows[:, m, :], RC[:, m, :]).then_inc(s_out, 16)
                sp.wait_ge(s_out, 16 * NT)


_OUT_SHAPE = (1, T, D)


def kernel(**inputs):
    import concourse.bacc as _bacc
    from concourse.bass_utils import run_bass_kernel_spmd as _run

    nc = _bacc.Bacc("TRN2", target_bir_lowering=False, num_devices=1)
    arrays, aps = {}, {}
    for name, value in {**inputs, **shape_constants()}.items():
        v = np.ascontiguousarray(value)
        arrays[f"in_{name}"] = v
        aps[name] = nc.dram_tensor(f"in_{name}", v.shape, mybir.dt.from_np(v.dtype), kind="ExternalInput").ap()
    out = nc.dram_tensor("out_0", _OUT_SHAPE, F32, kind="ExternalOutput").ap()
    build(nc, aps, out)
    r = _run(nc, [arrays], core_ids=[0])
    return r.results[0]["out_0"]
```
